# Optimizing a Trainium2 kernel written in Bass

```python
import jax, jax.numpy as jnp
from jax import lax
import numpy as np

D_MODEL = 1024
BATCH = 1
SEQ = 256
DEPTH = 2

N_MIXERS = 2
ALPHA = (2 * DEPTH) ** 0.25
BETA = (8 * DEPTH) ** -0.25
CHUNK = 64
LN_EPS = 1e-5
NEG_BIG = -1e30

GLA_HEADS = 4
GLA_DK = D_MODEL // 2
GLA_DV = D_MODEL
GLA_RANK = 16
GLA_TEMP = 16.0
GLA_IN = 2 * GLA_DK + 2 * GLA_DV + GLA_RANK

MLSTM_HEADS = 4
MLSTM_DH = D_MODEL // MLSTM_HEADS
CONV_W = 4
MLSTM_IN = 4 * D_MODEL + 2 * MLSTM_HEADS

N_EXPERTS = 16
N_GROUPS = 4
TOP_K = 2
D_FF = D_MODEL // 2

N_GLA_LAYERS = (DEPTH + 1) // 2
N_MLSTM_LAYERS = DEPTH // 2


def layer_norm(x, g, b):
    x32 = x.astype(jnp.float32)
    mu = x32.mean(-1, keepdims=True)
    var = jnp.square(x32 - mu).mean(-1, keepdims=True)
    return (x32 - mu) * lax.rsqrt(var + LN_EPS) * g + b

def head_norm(o, g, n_heads):
    B, S, W = o.shape
    oh = o.astype(jnp.float32).reshape(B, S, n_heads, W // n_heads)
    mu = oh.mean(-1, keepdims=True)
    var = jnp.square(oh - mu).mean(-1, keepdims=True)
    return ((oh - mu) * lax.rsqrt(var + LN_EPS)).reshape(B, S, W) * g

def to_chunks(t, n_heads):
    B, S, _ = t.shape
    t = t.reshape(B, S // CHUNK, CHUNK, n_heads, -1)
    return t.transpose(0, 3, 1, 2, 4)

def from_chunks(t):
    B, H, N, C, d = t.shape
    return t.transpose(0, 2, 3, 1, 4).reshape(B, N * C, H * d)

def gate_chunks(g):
    B, S, H = g.shape
    return g.reshape(B, S // CHUNK, CHUNK, H).transpose(0, 3, 1, 2)

def causal_mask():
    return jnp.tril(jnp.ones((CHUNK, CHUNK), dtype=bool))

def gla_mixer(x, w_in, w_gate_up, b_gate, norm_g, w_out):
    B, S, _ = x.shape
    H = GLA_HEADS
    dk, dv = GLA_DK // H, GLA_DV // H
    proj = x @ w_in
    q, k, v, r, g_lr = jnp.split(
        proj, [GLA_DK, 2 * GLA_DK, 2 * GLA_DK + GLA_DV, 2 * GLA_DK + 2 * GLA_DV], axis=-1)
    log_a = jax.nn.log_sigmoid((g_lr @ w_gate_up + b_gate).astype(jnp.float32)) / GLA_TEMP
    q = to_chunks(q.astype(jnp.float32) * dk ** -0.5, H)
    k = to_chunks(k.astype(jnp.float32), H)
    v = to_chunks(v.astype(jnp.float32), H)
    bcum = jnp.cumsum(to_chunks(log_a, H), axis=3)
    b_last = bcum[:, :, :, -1:, :]
    q_e = q * jnp.exp(bcum)
    scores = jnp.einsum('bhnik,bhnjk->bhnij', q_e, k * jnp.exp(-bcum))
    scores = jnp.where(causal_mask(), scores, 0.0)
    o_intra = jnp.einsum('bhnij,bhnjv->bhniv', scores, v)
    k_dec = k * jnp.exp(b_last - bcum)
    decay = jnp.exp(b_last[:, :, :, 0, :])

    def step(state, inp):
        qe_n, kd_n, v_n, dec_n = inp
        o_n = jnp.einsum('bhik,bhkv->bhiv', qe_n, state)
        state = dec_n[..., None] * state + jnp.einsum('bhjk,bhjv->bhkv', kd_n, v_n)
        return state, o_n

    s0 = jnp.zeros((B, H, dk, dv), jnp.float32)
    mv = lambda t: jnp.moveaxis(t, 2, 0)
    _, o_inter = lax.scan(step, s0, (mv(q_e), mv(k_dec), mv(v), mv(decay)))
    o = from_chunks(o_intra + jnp.moveaxis(o_inter, 0, 2))
    o = head_norm(o, norm_g, H) * jax.nn.silu(r.astype(jnp.float32))
    return o @ w_out

def causal_conv(u, w, bias):
    S = u.shape[1]
    up = jnp.pad(u, ((0, 0), (CONV_W - 1, 0), (0, 0)))
    return sum(up[:, j:j + S] * w[j] for j in range(CONV_W)) + bias

def mlstm_mixer(x, w_in, b_gates, conv_w, conv_b, norm_g, w_out):
    B, S, D = x.shape
    H, dh = MLSTM_HEADS, MLSTM_DH
    proj = x @ w_in
    qk, v, o_pre, gates = jnp.split(proj, [2 * D, 3 * D, 4 * D], axis=-1)
    qk = jax.nn.silu(causal_conv(qk, conv_w, conv_b))
    q, k = jnp.split(qk, 2, axis=-1)
    gates = (gates + b_gates).astype(jnp.float32)
    i_pre = gate_chunks(gates[..., :H])
    log_f = gate_chunks(jax.nn.log_sigmoid(gates[..., H:]))
    q = to_chunks(q.astype(jnp.float32), H)
    k = to_chunks(k.astype(jnp.float32) * dh ** -0.5, H)
    v = to_chunks(v.astype(jnp.float32), H)
    mask = causal_mask()

    def step(carry, inp):
        c_st, n_st, m_st = carry
        q_n, k_n, v_n, i_n, f_n = inp
        bcum = jnp.cumsum(f_n, axis=-1)
        d_mat = bcum[..., :, None] - bcum[..., None, :] + i_n[..., None, :]
        d_mat = jnp.where(mask, d_mat, -jnp.inf)
        inter = bcum + m_st[..., None]
        m_row = jnp.maximum(inter, d_mat.max(-1))
        p = jnp.exp(d_mat - m_row[..., None])
        w_inter = jnp.exp(inter - m_row)
        s = jnp.einsum('bhid,bhjd->bhij', q_n, k_n) * p
        num = w_inter[..., None] * jnp.einsum('bhid,bhde->bhie', q_n, c_st) \
            + jnp.einsum('bhij,bhje->bhie', s, v_n)
        den = w_inter * jnp.einsum('bhid,bhd->bhi', q_n, n_st) + s.sum(-1)
        h = num / jnp.maximum(jnp.abs(den), jnp.exp(-m_row))[..., None]
        b_last = bcum[..., -1]
        logit_k = b_last[..., None] - bcum + i_n
        m_new = jnp.maximum(b_last + m_st, logit_k.max(-1))
        w_k = jnp.exp(logit_k - m_new[..., None])
        w_old = jnp.exp(b_last + m_st - m_new)
        c_st = w_old[..., None, None] * c_st + jnp.einsum('bhj,bhjd,bhje->bhde', w_k, k_n, v_n)
        n_st = w_old[..., None] * n_st + jnp.einsum('bhj,bhjd->bhd', w_k, k_n)
        return (c_st, n_st, m_new), h

    carry0 = (jnp.zeros((B, H, dh, dh), jnp.float32),
              jnp.zeros((B, H, dh), jnp.float32),
              jnp.full((B, H), NEG_BIG, jnp.float32))
    mv = lambda t: jnp.moveaxis(t, 2, 0)
    _, hs = lax.scan(step, carry0, (mv(q), mv(k), mv(v), mv(i_pre), mv(log_f)))
    h = from_chunks(jnp.moveaxis(hs, 0, 2))
    h = head_norm(h, norm_g, H) * jax.nn.sigmoid(o_pre.astype(jnp.float32))
    return h @ w_out

def grouped_moe(x, w_router, w1, w3, w2):
    B, S, D = x.shape
    t = x.reshape(-1, D)
    T = t.shape[0]
    per_group = N_EXPERTS // N_GROUPS
    aff = jax.nn.sigmoid((t @ w_router).astype(jnp.float32))
    group_score = lax.top_k(aff.reshape(T, N_GROUPS, per_group), TOP_K)[0].sum(-1)
    g_sel = jnp.argmax(group_score, axis=-1)
    in_group = (jnp.arange(N_EXPERTS) // per_group)[None, :] == g_sel[:, None]
    top_val, top_idx = lax.top_k(jnp.where(in_group, aff, -1.0), TOP_K)
    gates_k = top_val / top_val.sum(-1, keepdims=True)
    gates = jnp.einsum('tk,tke->te', gates_k, jax.nn.one_hot(top_idx, N_EXPERTS, dtype=jnp.float32))
    y = jnp.zeros((T, D), jnp.float32)
    for e in range(N_EXPERTS):
        h = jax.nn.silu(t @ w1[e]) * (t @ w3[e])
        y = y + gates[:, e:e + 1] * (h @ w2[e])
    return y.reshape(B, S, D)

def first_inputs(seed: int = 0) -> dict:
    key = jax.random.key(seed)
    ks = jax.random.split(key, 24)
    f32 = jnp.float32
    nrm = lambda k, shape, scale: jax.random.normal(k, shape, f32) * scale
    D, NG, NM = D_MODEL, N_GLA_LAYERS, N_MLSTM_LAYERS
    b_gates = jnp.concatenate(
        [nrm(ks[8], (NM, MLSTM_HEADS), 0.1),
         jnp.linspace(3.0, 6.0, MLSTM_HEADS, dtype=f32)[None, :] + nrm(ks[9], (NM, MLSTM_HEADS), 0.1)],
        axis=-1)
    return {
        "x": nrm(ks[0], (BATCH, SEQ, D), 1.0),
        "gla_w_in": nrm(ks[1], (NG, D, GLA_IN), D ** -0.5),
        "gla_w_gate_up": nrm(ks[2], (NG, GLA_RANK, GLA_DK), GLA_RANK ** -0.5),
        "gla_b_gate": nrm(ks[3], (NG, GLA_DK), 0.1),
        "gla_norm_g": 1.0 + nrm(ks[4], (NG, GLA_DV), 0.02),
        "gla_w_out": nrm(ks[5], (NG, GLA_DV, D), GLA_DV ** -0.5 * BETA),
        "mlstm_w_in": nrm(ks[6], (NM, D, MLSTM_IN), D ** -0.5),
        "mlstm_b_gates": b_gates,
        "mlstm_conv_w": nrm(ks[10], (NM, CONV_W, 2 * D), CONV_W ** -0.5),
        "mlstm_conv_b": nrm(ks[11], (NM, 2 * D), 0.02),
        "mlstm_norm_g": 1.0 + nrm(ks[12], (NM, D), 0.02),
        "mlstm_w_out": nrm(ks[13], (NM, D, D), D ** -0.5 * BETA),
        "router_w": nrm(ks[14], (D, N_EXPERTS), D ** -0.5),
        "moe_w1": nrm(ks[15], (DEPTH, N_EXPERTS, D, D_FF), D ** -0.5),
        "moe_w3": nrm(ks[16], (DEPTH, N_EXPERTS, D, D_FF), D ** -0.5),
        "moe_w2": nrm(ks[17], (DEPTH, N_EXPERTS, D_FF, D), D_FF ** -0.5 * BETA),
        "ln_g": 1.0 + nrm(ks[18], (DEPTH, 2, D), 0.02),
        "ln_b": nrm(ks[19], (DEPTH, 2, D), 0.02),
    }

def first_block(x, gla_w_in, gla_w_gate_up, gla_b_gate, gla_norm_g, gla_w_out,
              mlstm_w_in, mlstm_b_gates, mlstm_conv_w, mlstm_conv_b, mlstm_norm_g, mlstm_w_out,
              router_w, moe_w1, moe_w3, moe_w2, ln_g, ln_b):
    h = x
    for i in range(DEPTH):
        j = i // N_MIXERS
        if i % N_MIXERS == 0:
            mix = gla_mixer(h, gla_w_in[j], gla_w_gate_up[j], gla_b_gate[j], gla_norm_g[j], gla_w_out[j])
        else:
            mix = mlstm_mixer(h, mlstm_w_in[j], mlstm_b_gates[j], mlstm_conv_w[j], mlstm_conv_b[j],
                              mlstm_norm_g[j], mlstm_w_out[j])
        h = layer_norm(ALPHA * h + mix, ln_g[i, 0], ln_b[i, 0])
        ffn = grouped_moe(h, router_w, moe_w1[i], moe_w3[i], moe_w2[i])
        h = layer_norm(ALPHA * h + ffn, ln_g[i, 1], ln_b[i, 1])
    return h


HEAD_DIM = 64
A_Q_HEADS = 8
A_KV_HEADS = 2
B_GROUPS = ((128, 1), (512, 4), (2048, 16))
B_HEADS = 4
N_B = len(B_GROUPS)
D_FF_2 = 4 * D_MODEL
GRID_W = 64
ROPE_THETA = 10000.0
Q_BLOCK = 128
EPS = 1e-6

A_Q_W = A_Q_HEADS * HEAD_DIM
A_KV_W = A_KV_HEADS * HEAD_DIM
B_W = B_HEADS * HEAD_DIM
IN_SIZES = [A_Q_W, A_KV_W, A_KV_W] + [B_W] * (3 * N_B) + [D_MODEL, D_MODEL]
IN_W = sum(IN_SIZES)
IN_SPLITS = [int(v) for v in np.cumsum(IN_SIZES)[:-1]]


def rms(x, g):
    x32 = x.astype(jnp.float32)
    y = x32 * lax.rsqrt(jnp.mean(x32 * x32, axis=-1, keepdims=True) + EPS)
    return (y * g.astype(jnp.float32)).astype(x.dtype)

def rope_cos_sin(pos, dim):
    inv = ROPE_THETA ** (-jnp.arange(0, dim, 2, dtype=jnp.float32) / dim)
    ang = pos.astype(jnp.float32)[:, None] * inv[None, :]
    return jnp.cos(ang), jnp.sin(ang)

def apply_rope(x, cos, sin):
    x32 = x.astype(jnp.float32)
    x1, x2 = jnp.split(x32, 2, axis=-1)
    c = cos[None, :, None, :]
    s = sin[None, :, None, :]
    return jnp.concatenate([x1 * c - x2 * s, x2 * c + x1 * s], axis=-1).astype(x.dtype)

def axial_rope(x, row_cs, col_cs):
    half = x.shape[-1] // 2
    return jnp.concatenate([apply_rope(x[..., :half], *row_cs),
                            apply_rope(x[..., half:], *col_cs)], axis=-1)

def gqa_attention(q, k, v):
    B, S, Hq, hd = q.shape
    Hkv = k.shape[2]
    rep = Hq // Hkv
    q = q.reshape(B, S, Hkv, rep, hd)
    scale = hd ** -0.5

    def block(i):
        qi = lax.dynamic_slice_in_dim(q, i * Q_BLOCK, Q_BLOCK, axis=1)
        s = jnp.einsum('bqgrd,bkgd->bgrqk', qi, k, preferred_element_type=jnp.float32) * scale
        p = jax.nn.softmax(s, axis=-1).astype(v.dtype)
        return jnp.einsum('bgrqk,bkgd->bqgrd', p, v)

    o = lax.map(block, jnp.arange(S // Q_BLOCK))
    return jnp.moveaxis(o, 0, 1).reshape(B, S, Hq * hd)

def dilated_attention(qs, ks, vs):
    B, S, H, hd = qs[0].shape
    scale = hd ** -0.5
    offs = []
    for (w, d) in B_GROUPS:
        kk = (w // 2) // d
        offs.append(jnp.asarray(np.arange(-kk, kk + 1) * d, dtype=jnp.int32))

    def block(i):
        t = i * Q_BLOCK + jnp.arange(Q_BLOCK, dtype=jnp.int32)
        outs, lses = [], []
        for q, k, v, off in zip(qs, ks, vs, offs):
            idx = t[:, None] + off[None, :]
            valid = (idx >= 0) & (idx < S)
            idx = jnp.clip(idx, 0, S - 1)
            qi = lax.dynamic_slice_in_dim(q, i * Q_BLOCK, Q_BLOCK, axis=1)
            kg = k[:, idx]
            vg = v[:, idx]
            s = jnp.einsum('bqhd,bqkhd->bhqk', qi, kg, preferred_element_type=jnp.float32) * scale
            s = jnp.where(valid[None, None], s, -jnp.inf)
            lse = jax.nn.logsumexp(s, axis=-1)
            p = jnp.exp(s - lse[..., None]).astype(vg.dtype)
            outs.append(jnp.einsum('bhqk,bqkhd->bqhd', p, vg))
            lses.append(lse)
        wts = jax.nn.softmax(jnp.stack(lses), axis=0)
        wts = jnp.transpose(wts, (0, 1, 3, 2))[..., None]
        return jnp.sum(wts.astype(outs[0].dtype) * jnp.stack(outs), axis=0)

    o = lax.map(block, jnp.arange(S // Q_BLOCK))
    return jnp.moveaxis(o, 0, 1).reshape(B, S, H * hd)

def second_inputs(seed: int = 0) -> dict:
    key = jax.random.key(seed)
    ks = jax.random.split(key, 16)
    f = jnp.float32
    nrm = lambda k, shape, fan: jax.random.normal(k, shape, f) * (fan ** -0.5)
    return {
        "x": jax.random.normal(ks[0], (BATCH, SEQ, D_MODEL), f),
        "c": jax.random.normal(ks[1], (BATCH, D_MODEL), f),
        "w_ada": nrm(ks[2], (DEPTH, D_MODEL, 6 * D_MODEL), D_MODEL),
        "b_ada": 0.02 * jax.random.normal(ks[3], (DEPTH, 6 * D_MODEL), f),
        "g_mix": 1.0 + 0.05 * jax.random.normal(ks[4], (DEPTH, D_MODEL), f),
        "g_mlp": 1.0 + 0.05 * jax.random.normal(ks[5], (DEPTH, D_MODEL), f),
        "w_in": nrm(ks[6], (DEPTH, D_MODEL, IN_W), D_MODEL),
        "q_norm_a": 1.0 + 0.05 * jax.random.normal(ks[7], (DEPTH, HEAD_DIM), f),
        "k_norm_a": 1.0 + 0.05 * jax.random.normal(ks[8], (DEPTH, HEAD_DIM), f),
        "q_norm_b": 1.0 + 0.05 * jax.random.normal(ks[9], (DEPTH, N_B, HEAD_DIM), f),
        "k_norm_b": 1.0 + 0.05 * jax.random.normal(ks[10], (DEPTH, N_B, HEAD_DIM), f),
        "w_branch_a": nrm(ks[11], (DEPTH, A_Q_W, D_MODEL), A_Q_W),
        "w_branch_b": nrm(ks[12], (DEPTH, B_W, D_MODEL), B_W),
        "w_out": nrm(ks[13], (DEPTH, D_MODEL, D_MODEL), D_MODEL),
        "w_ff1": nrm(ks[14], (DEPTH, D_MODEL, D_FF_2), D_MODEL),
        "w_ff2": nrm(ks[15], (DEPTH, D_FF_2, D_MODEL), D_FF_2),
    }

def second_block(x, c, w_ada, b_ada, g_mix, g_mlp, w_in, q_norm_a, k_norm_a, q_norm_b, k_norm_b,
              w_branch_a, w_branch_b, w_out, w_ff1, w_ff2):
    B, S, D = x.shape
    rows = S // GRID_W
    row_idx = jnp.broadcast_to(jnp.arange(rows)[:, None], (rows, GRID_W)).reshape(-1)
    col_idx = jnp.broadcast_to(jnp.arange(GRID_W)[None, :], (rows, GRID_W)).reshape(-1)
    row_cs = rope_cos_sin(row_idx, HEAD_DIM // 2)
    col_cs = rope_cos_sin(col_idx, HEAD_DIM // 2)
    seq_cs = rope_cos_sin(jnp.arange(S), HEAD_DIM)
    c_act = jax.nn.silu(c)

    for l in range(DEPTH):
        ada = c_act @ w_ada[l] + b_ada[l]
        sh1, sc1, gt1, sh2, sc2, gt2 = [a[:, None, :] for a in jnp.split(ada, 6, axis=-1)]

        h = rms(x, g_mix[l]) * (1.0 + sc1) + sh1
        parts = jnp.split(h @ w_in[l], IN_SPLITS, axis=-1)
        qa = parts[0].reshape(B, S, A_Q_HEADS, HEAD_DIM)
        ka = parts[1].reshape(B, S, A_KV_HEADS, HEAD_DIM)
        va = parts[2].reshape(B, S, A_KV_HEADS, HEAD_DIM)
        qa = axial_rope(rms(qa, q_norm_a[l]), row_cs, col_cs)
        ka = axial_rope(rms(ka, k_norm_a[l]), row_cs, col_cs)
        y_a = gqa_attention(qa, ka, va) @ w_branch_a[l]

        qs, kss, vs = [], [], []
        for g in range(N_B):
            qb = parts[3 + 3 * g].reshape(B, S, B_HEADS, HEAD_DIM)
            kb = parts[4 + 3 * g].reshape(B, S, B_HEADS, HEAD_DIM)
            vb = parts[5 + 3 * g].reshape(B, S, B_HEADS, HEAD_DIM)
            qs.append(apply_rope(rms(qb, q_norm_b[l, g]), *seq_cs))
            kss.append(apply_rope(rms(kb, k_norm_b[l, g]), *seq_cs))
            vs.append(vb)
        y_b = dilated_attention(qs, kss, vs) @ w_branch_b[l]

        gate_a = jax.nn.sigmoid(parts[3 + 3 * N_B])
        gate_b = jax.nn.sigmoid(parts[4 + 3 * N_B])
        mixed = gate_a * y_a + gate_b * y_b
        x = x + gt1 * (mixed @ w_out[l])

        h2 = rms(x, g_mlp[l]) * (1.0 + sc2) + sh2
        x = x + gt2 * (jnp.square(jax.nn.relu(h2 @ w_ff1[l])) @ w_ff2[l])

    return x


def setup_inputs(seed=0):
    out = dict(first_inputs(seed))
    for name, value in second_inputs(seed + 1).items():
        if name != "x":
            out[name + "_2"] = value
    return out


def reference(
    x, gla_w_in, gla_w_gate_up, gla_b_gate, gla_norm_g, gla_w_out, mlstm_w_in, mlstm_b_gates,
    mlstm_conv_w, mlstm_conv_b, mlstm_norm_g, mlstm_w_out, router_w, moe_w1, moe_w3, moe_w2,
    ln_g, ln_b, c_2, w_ada_2, b_ada_2, g_mix_2, g_mlp_2, w_in_2, q_norm_a_2, k_norm_a_2,
    q_norm_b_2, k_norm_b_2, w_branch_a_2, w_branch_b_2, w_out_2, w_ff1_2, w_ff2_2,
):
    x = first_block(
        x, gla_w_in, gla_w_gate_up, gla_b_gate, gla_norm_g, gla_w_out, mlstm_w_in,
        mlstm_b_gates, mlstm_conv_w, mlstm_conv_b, mlstm_norm_g, mlstm_w_out, router_w, moe_w1,
        moe_w3, moe_w2, ln_g, ln_b,
    )
    return second_block(
        x, c_2, w_ada_2, b_ada_2, g_mix_2, g_mlp_2, w_in_2, q_norm_a_2, k_norm_a_2, q_norm_b_2,
        k_norm_b_2, w_branch_a_2, w_branch_b_2, w_out_2, w_ff1_2, w_ff2_2,
    )


_drawn_inputs = setup_inputs


def setup_inputs(seed=0):
    import zlib

    import numpy as np

    out = dict(_drawn_inputs(seed))
    spreads = {}
    factors = {'gla_b_gate': 2.864,
     'gla_norm_g': 4.01,
     'mlstm_conv_b': 8.0,
     'mlstm_norm_g': 5.806,
     'g_mix_2': 4.83,
     'q_norm_a_2': 8.0,
     'k_norm_a_2': 8.0,
     'q_norm_b_2': 8.0,
     'k_norm_b_2': 8.0}
    for name, (base, spread) in spreads.items():
        noise = np.random.default_rng([zlib.crc32(name.encode()), seed]).standard_normal(out[name].shape)
        drawn = base * np.exp(spread * noise) if base else spread * noise
        out[name] = __import__('jax').numpy.asarray(drawn.astype(out[name].dtype))
    for name, factor in factors.items():
        out[name] = (out[name] * factor).astype(out[name].dtype)
    return out
```

```python
import concourse.bass as bass
from concourse import mybir
from contextlib import ExitStack
import numpy as np


class Queue:

    def __init__(self, sem):
        self.sem = sem
        self.n = 0
        self.items = []
        self.outer = None

    def __call__(self, fn, *after):
        self.n += 1
        self.items.append((fn, after, True))
        return (self.sem, self.n)

    def bare(self, fn, *after):
        self.items.append((fn, after, False))

    def enter(self, sem):
        self.outer = (self.sem, self.n, self.items)
        self.sem, self.n, self.items = sem, 0, []

    def leave(self):
        part = (self.sem, self.items)
        self.sem, self.n, self.items = self.outer
        return part

    def emit(self, eng):
        self.run(eng, self.sem, self.items, {})

    def run(self, eng, sem, items, met):
        def wait(tokens):
            for tok in tokens:
                if len(tok) == 2 and isinstance(tok[1], int):
                    if met.get(id(tok[0]), 0) < tok[1]:
                        eng.wait_ge(tok[0], tok[1])
                        met[id(tok[0])] = tok[1]
                else:
                    wait(tok)

        for item in items:
            if isinstance(item, Part):
                wait(item.after)
                with eng.register(item.name) as reg:
                    eng.reg_load(reg, item.flag)
                    with eng.If_ne(reg, 0):
                        self.run(eng, item.sem, item.items, dict(met))
                continue
            fn, after, counted = item
            wait(after)
            ins = fn(eng)
            if counted:
                ins.then_inc(sem, 1)


class Part:

    def __init__(self, name, flag, after):
        self.name, self.flag, self.after = name, flag, after
        self.sem, self.items = None, []


CST = ["ident", "causal", "before", "ones", "decay", "fold", "slots", "heads"]
VEC = ["gla_g", "mlstm_g", "conv_w", "conv_b", "ln_g", "ln_b", "g_mix", "g_mlp", "b_ada", "c",
       "router", "glr", "mgate"]


def two_block_kernel(nc, D, out, small, stop=None):
    F32 = mybir.dt.float32
    F32R = mybir.dt.float32r
    I32 = mybir.dt.int32
    ALU = mybir.AluOpType
    ACT = mybir.ActivationFunctionType
    AX = mybir.AxisListType
    MUL, ADD, SUB, MAX, MIN = ALU.mult, ALU.add, ALU.subtract, ALU.max, ALU.min

    ALPHA = float(4 ** 0.25)
    NR = 6
    NC = 4
    ctx = ExitStack()
    with ctx:
        def sb(name, shape, dt=F32):
            return ctx.enter_context(nc.sbuf_tensor(name, shape, dt))

        def sem(name):
            return ctx.enter_context(nc.semaphore(name))

        P, S, V, G = (Queue(sem(n)) for n in ("s_pe", "s_act", "s_dve", "s_pool"))
        Y = Queue(None)

        def act(o, i, f, *after, **kw):
            return S(lambda e: e.activation(o, i, f, **kw), *after)

        def tt(o, a, b, op, *after):
            return V(lambda e: e.tensor_tensor(o, a, b, op), *after)

        def ts(o, a, s1, s2, op0, op1, *after):
            return V(lambda e: e.tensor_scalar(o, a, s1, s2, op0=op0, op1=op1), *after)

        def stt(o, a, s, b, op0, op1, *after):
            return V(lambda e: e.scalar_tensor_tensor(out=o, in0=a, scalar=s, in1=b, op0=op0, op1=op1), *after)

        def cp(o, a, *after):
            return V(lambda e: e.tensor_copy(o, a), *after)

        def mms(seq, *after):
            def go(e):
                for o, l, r, a, z in seq:
                    ins = e.matmul(o, l, r, start=a, stop=z, skip_group_check=True)
                return ins
            return P(go, *after)

        def turns(seq, *after):
            def go(e):
                for o, i in seq:
                    ins = e.transpose(o, i, ident)
                return ins
            return P(go, *after)

        def load(dst, src, *after):
            s = sem(f"s_ld{len(loads)}")
            loads.append(s)
            Y.bare(lambda e: e.dma_start(dst, src).then_inc(s, 16), *after)
            return (s, 16)

        loads = []

        PS = [ctx.enter_context(nc.psum_tensor(f"ps{i}", [128, 512], F32)) for i in range(8)]
        PF = [()] * 8
        turn = list(range(8))

        def take():
            b = turn.pop(0)
            turn.append(b)
            return b

        def three(o, xh, xl, wh, wl, first, last):
            return [(o, xh, wh, first, False), (o, xh, wl, False, False), (o, xl, wh, False, last)]

        def three_w(o, wh, wl, xh, xl, first, last):
            return [(o, wh, xh, first, False), (o, wh, xl, False, False), (o, wl, xh, False, last)]

        cst = sb("cst", [128, small["cst"][1]])
        vec = sb("vec", [128, small["vec"][1]])

        def part(t, table, name, shape=None):
            o, n = table[name]
            ap = t[:, o:o + n]
            return ap

        C = {n: part(cst, small["cst"][0], n) for n in small["cst"][0]}
        VE = {n: part(vec, small["vec"][0], n) for n in small["vec"][0]}
        ident = C["ident"]

        raw = [sb(f"raw{i}", [128, 2048]) for i in range(NR)]
        hi = [sb(f"hi{i}", [128, 1024], F32R) for i in range(NC)]
        lo = [sb(f"lo{i}", [128, 1024], F32R) for i in range(NC)]
        X = sb("X", [128, 2, 1024])
        F = sb("F", [128, 8, 256])
        FR = nc.alloc_sbuf_tensor_at("FR", [128, 2048], F32R, offset=nc.sbuf_base - 4 * 2048)
        T2 = sb("T2", [128, 4096], F32R)
        TH = T2[:, 0:2048].rearrange("p (k i) -> p k i", k=8)
        TL = T2[:, 2048:4096].rearrange("p (k i) -> p k i", k=8)
        ACC = sb("ACC", [128, 2048])
        FLAG = sb("FLAG", [1, 2], I32)
        ADA = sb("ADA", [128, 2, 48])
        STG = ACC[0:1, :]
        TINY = sb("TINY", [128, 512])
        AR = sb("AR", [128, 18040])
        AF = nc.alloc_sbuf_tensor_at("AF", [128, 18040], F32R, offset=nc.sbuf_base - 4 * 18040)

        def ar(o, *shape, dt=None):
            n = int(np.prod(shape))
            ap = (AR if dt is None else AF)[:, o:o + n]
            if len(shape) == 1:
                return ap
            names = "abcdef"[:len(shape)]
            return ap.rearrange(f"p ({' '.join(names)}) -> p {' '.join(names)}",
                                **{k: v for k, v in zip(names[:-1], shape[:-1])})

        tcst = load(cst[:, :], D["cst"])
        tF = load(F[:, :, :], D["xT"])
        tvec = load(vec[:, :], D["vec"])

        chunks = small["chunks"]
        stops = small["stops"]

        def stream(chunks, sems, stops):
            events = []
            for c, ch in enumerate(chunks):
                if ch[0] == "w":
                    events += [("w", c, 0), ("w", c, 1)]
                else:
                    events.append(("ada", c, 1))
            return {"chunks": chunks, "sems": sems, "events": events, "stops": stops, "ev": 0, "u": 0, "dma": 0,
                    "conv": [], "used": {}}

        st = stream(chunks, [sem(f"s_raw{i}") for i in range(NR)], stops)
        parts = {}
        ada_tok = {}

        def issue(*after):
            c, chunks = st["dma"], st["chunks"]
            if c >= len(chunks):
                return
            st["dma"] += 1
            if c in st["stops"]:
                Y.items.append(parts[st["stops"][c]]["sync"])
            src, s = chunks[c][1], st["sems"][c % NR]
            Y.bare(lambda e: e.dma_start(raw[c % NR][:, :], src).then_inc(s, 16), *after)

        def landed(c):
            return (st["sems"][c % NR], 16 * (c // NR + 1))

        def step():
            kind, c, half = st["events"][st["ev"]]
            st["ev"] += 1
            if kind == "w":
                u = len(st["conv"])
                r = raw[c % NR][:, 1024 * half:1024 * half + 1024]
                h, l = hi[u % NC][:, :], lo[u % NC][:, :]
                th = act(h, r, ACT.Copy, landed(c), st["used"].get(u - NC, ()))
                tl = tt(l, r, h, SUB, th)
                st["conv"].append((h, l, tl))
                if half:
                    issue(tl)
            else:
                issue(ada_step(c))

        def unit():
            u = st["u"]
            st["u"] += 1
            ahead = u + NC - 1
            while len(st["conv"]) <= ahead and st["ev"] < len(st["events"]):
                c = st["events"][st["ev"]][1]
                if c in st["stops"] and len(st["conv"]) > u:
                    break
                step()
            return (u,) + st["conv"][u]

        def used(u, tok):
            st["used"][u] = tok

        def ada_step(c):
            _, _, layer, blk, k = st["chunks"][c]
            w = raw[c % NR][:, :]
            cc = small_ap["c_act"][:, k:k + 1]
            if k == 0:
                t = ts(ACC[:, :], w, cc, None, MUL, ALU.bypass, landed(c), small_ap["t_c"],
                       ada_tok.get("acc", ()))
            else:
                t = stt(ACC[:, :], w, cc, ACC[:, :], MUL, ADD, landed(c), ada_tok["acc"])
            ada_tok["acc"] = t
            if k == 7:
                b = take()
                m = mms([(PS[b][:, j:j + 1], ACC[:, 128 * j:128 * j + 128], C["ones"][:, 0:1], True, True)
                         for j in range(16)], PF[b], t)
                o = layer * 48 + blk * 16
                e = tt(ADA[:, layer, 16 * blk:16 * blk + 16], PS[b][:, 0:16],
                       VE["b_ada"][:, o:o + 16], ADD, m)
                PF[b] = (e,)
                ada_tok["acc"] = (m,)
                ada_tok[layer, blk] = e
                return t
            return t

        for _ in range(NR):
            issue()
        tX = load(X[:, :, :], D["x"].rearrange("(t p) d -> p t d", p=128))
        tWG = load(ar(16400, 512)[0:17, :], D["wgu"])

        small_ap = {}
        tc0 = act(TINY[:, 0:8], VE["c"], ACT.Tanh, tvec, scale=0.5)
        tc1 = stt(TINY[:, 8:16], TINY[:, 0:8], 1.0, VE["c"], ADD, MUL, tc0)
        tc2 = ts(TINY[:, 16:24], TINY[:, 8:16], 0.5, None, MUL, ALU.bypass, tc1)
        small_ap["c_act"] = TINY[:, 16:24]
        small_ap["t_c"] = tc2
        tg = ts(TINY[:, 24:40], vec[:, small["vec"][0]["gla_g"][0]:small["vec"][0]["gla_g"][0] + 16],
                0.5, None, MUL, ALU.bypass, tvec)
        halfg = TINY[:, 24:40]

        IDR = sb("IDR", [128, 128], F32R)
        t_idr = act(IDR[:, :], ident, ACT.Copy, tcst)

        def gload(dst, src, *after):
            q = sem(f"s_gl{len(gloads)}")
            gloads.append(q)
            G.bare(lambda e: e.dma_start(dst, src).then_inc(q, 16), *after)
            return (q, 16)

        gloads = []

        def split(src, h, l, *after):
            th = act(h, src, ACT.Copy, *after)
            return tt(l, src, h, SUB, th)

        def rsqrt(o, v, n, base, *after):
            two = TINY[:, base:base + 2 * n] if isinstance(base, int) else base
            y, t1 = two[:, 0:n], two[:, n:2 * n]
            t = ts(y.bitcast(I32), v.bitcast(I32), -0.5, 1597463007.0, MUL, ADD, *after)
            for i in range(3):
                t = tt(t1, y, y, MUL, t)
                t = stt(t1, t1, -0.5, v, MUL, MUL, t)
                d = o if i == 2 else y
                t = stt(d, t1, 1.5, y, ADD, MUL, t)
            return t

        def norm_rows(groups, n, base, *after):
            pass

        def ln(i, j, z, tz, with_T, keep_F):
            base = 64
            o = (2 * i + j) * 8
            tstg = load(STG[:, :], D["lnrow"][2 * i + j:2 * i + j + 1, :], *small_ap.get("stg", ()))
            gb = ar(LNB, 2048)
            tgb = G(lambda e: e.partition_broadcast(gb, STG[0:1, :]), tstg, *small_ap["lnb"])
            small_ap["stg"] = (tgb,)
            stats = TINY[:, base:base + 24]
            mv = TINY[:, base + 24:base + 28].rearrange("p (a b) -> p a b", a=2)
            ta = []
            for t in range(2):
                for q in range(2):
                    ta.append(V(lambda e, t=t, q=q: e.bn_stats(
                        stats[:, 12 * t + 6 * q:12 * t + 6 * q + 6], z[:, t, 512 * q:512 * q + 512]), tz))
            tb = []
            for t in range(2):
                tb.append(V(lambda e, t=t: e.bn_aggr(mv[:, t, :], stats[:, 12 * t:12 * t + 12]), ta[2 * t + 1], ta[2 * t]))
            ve = TINY[:, base + 28:base + 30]
            rs = TINY[:, base + 30:base + 32]
            tv = ts(ve, mv[:, :, 1], 1e-5, None, ADD, ALU.bypass, tb[1], tb[0])
            tr = rsqrt(rs, ve, 2, base + 32, tv)
            xn = [ts(X[:, t, :], z[:, t, :], mv[:, t, 0:1], rs[:, t:t + 1], SUB, MUL, tr) for t in range(2)]
            out = transposed(X, xn, VE["ln_g"][:, o:o + 8], VE["ln_b"][:, o:o + 8], with_T, keep_F)
            tx = []
            for t in range(2):
                a = tt(X[:, t, :], X[:, t, :], gb[:, 0:1024], MUL, tgb, xn[t], out[1])
                tx.append(tt(X[:, t, :], X[:, t, :], gb[:, 1024:2048], ADD, a))
            small_ap["lnb"] = (tx[1],)
            return tx, out[0]

        def transposed(src, tsrc, scale, bias, with_T, keep_F, wait_F=(), wait_T=()):
            te = []
            tt_ = []
            tf = []
            for g in range(4):
                b = take()
                m = turns([(PS[b][:, 256 * k + 128 * t:256 * k + 128 * t + 128],
                            src[:, t, 128 * (2 * g + k):128 * (2 * g + k) + 128])
                           for k in range(2) for t in range(2)], PF[b], tsrc)
                for k in range(2):
                    kt = 2 * g + k
                    f = act(F[:, kt, :], PS[b][:, 256 * k:256 * k + 256], ACT.Identity, m, wait_F,
                            scale=scale[:, kt:kt + 1], bias=bias[:, kt:kt + 1])
                    tf.append(f)
                PF[b] = (f,)
                if with_T:
                    tt_.append(split(F[:, 2 * g:2 * g + 2, :], TH[:, 2 * g:2 * g + 2, :],
                                     TL[:, 2 * g:2 * g + 2, :], f, tf[-2], wait_T))
            return (tt_ if with_T else tf), m

        LNB = 14900

        def linear_b(nb, kt, waits, sink, th=None, tl=None):
            th = TH if th is None else th
            tl = TL if tl is None else tl
            for n in range(nb):
                bk = [take(), take()]
                for u2 in range(kt // 2):
                    u, h, l, tok = unit()
                    seq = []
                    for j in range(2):
                        k = 2 * u2 + j
                        for t in range(2):
                            seq += three(PS[bk[t]][:, :], th[:, k, 128 * t:128 * t + 128],
                                         tl[:, k, 128 * t:128 * t + 128],
                                         h[:, 512 * j:512 * j + 512], l[:, 512 * j:512 * j + 512],
                                         k == 0, k == kt - 1)
                    m = mms(seq, tok, waits, PF[bk[0]] if u2 == 0 else (), PF[bk[1]] if u2 == 0 else ())
                    used(u, m)
                for t in range(2):
                    PF[bk[t]] = sink(n, t, PS[bk[t]][:, :], m)

        def linear_a(mt, kt, waits, sink, th=None, tl=None):
            th = TH if th is None else th
            tl = TL if tl is None else tl
            per = 8 // kt
            for n in range(mt // 2):
                b = take()
                for i in range(2):
                    m = 2 * n + i
                    if m % per == 0:
                        u, h, l, tok = unit()
                    seq = []
                    for k in range(kt):
                        c = 128 * (kt * (m % per) + k)
                        seq += three_w(PS[b][:, 256 * i:256 * i + 256], h[:, c:c + 128], l[:, c:c + 128],
                                       th[:, k, :], tl[:, k, :], k == 0, k == kt - 1)
                    done = mms(seq, tok, waits, PF[b] if i == 0 else ())
                    if m % per == per - 1:
                        used(u, done)
                PF[b] = sink(n, PS[b][:, :], done)

        def gla():
            QT, KT, BT = ar(0, 4, 256), ar(1024, 4, 256), ar(2048, 4, 256)
            KM = ar(3072, 4, 4, 256)
            VV, SR = ar(7168, 2, 1024), ar(9216, 2, 1024)
            LA, PM = ar(11264, 2, 512), ar(11264, 4, 384)
            E1, E3 = ar(12800, 4, 256), ar(13824, 4, 256)
            GL = ar(15000, 256)
            LB = ar(15300, 2, 512)
            ET = TINY[:, 128:144].rearrange("p (h c) -> p h c", h=4)
            tz = [G(lambda e: e.memset(KM[:, :, 0, 64:128], 0.0)),
                  G(lambda e: e.memset(KM[:, :, 2, 192:256], 0.0))]
            tone = G(lambda e: e.memset(GL[0:17, :], 1.0))
            tT = [split(F[:, 4 * g:4 * g + 4, :], TH[:, 4 * g:4 * g + 4, :], TL[:, 4 * g:4 * g + 4, :], tF)
                  for g in range(2)]
            b = take()
            glr = VE["glr"].rearrange("p (k r) -> p k r", k=8)
            m = mms([(PS[b][0:16, 0:256], glr[:, k, :], F[:, k, :], k == 0, k == 7) for k in range(8)],
                    PF[b], tF, tvec)
            t = act(GL[0:16, :], PS[b][0:16, 0:256], ACT.Copy, m, tone)
            PF[b] = (t,)
            tla = []
            for q in range(2):
                b = take()
                m = mms([(PS[b][:, :], GL[0:17, 128 * q:128 * q + 128], ar(16400, 512)[0:17, :], True, True)],
                        PF[b], t, tWG)
                e = act(LA[:, q, :], PS[b][:, :], ACT.Abs, m)
                e = act(LA[:, q, :], LA[:, q, :], ACT.Exp, e, scale=-1.0)
                e = act(LA[:, q, :], LA[:, q, :], ACT.Ln, e, bias=1.0)
                d = stt(LB[:, q, :], PS[b][:, :], 0.0, LA[:, q, :], MIN, SUB, e)
                PF[b] = (d,)
                tla.append(d)
            qk = []

            def sink_qk(n, p, m):
                dst = (QT if n < 2 else KT)[:, 2 * (n % 2):2 * (n % 2) + 2, :]
                e = act(dst, p.rearrange("p (h i) -> p h i", h=2), ACT.Copy, m, scale=128 ** -0.5 if n < 2 else 1.0)
                qk.append(e)
                return (e,)

            linear_a(8, 8, tT, sink_qk)
            tb = []
            for hp in range(2):
                b = take()
                m = mms([(PS[b][:, 256 * hh + 128 * q:256 * hh + 128 * q + 128],
                          LB[:, q, 128 * (2 * hp + hh):128 * (2 * hp + hh) + 128], C["decay"], True, True)
                         for hh in range(2) for q in range(2)], PF[b], tla, tcst)
                e = cp(BT[:, 2 * hp:2 * hp + 2, :], PS[b][:, :].rearrange("p (h i) -> p h i", h=2), m)
                PF[b] = (e,)
                tb.append(e)
            BC = BT.rearrange("p h (c i) -> p h c i", c=4)
            e1 = act(E1, BT, ACT.Exp, tb)
            tq = tt(QT, QT, E1, MUL, e1, qk)
            e2 = act(E1, BT, ACT.Exp, tq, scale=-1.0)
            dk = ar(3072, 4, 4, 256)
            KM4 = KM.rearrange("p h c (d i) -> p h (c d) i", d=4)
            KC = KT.rearrange("p h (c i) -> p h c i", c=4)
            ki = tt(KM4[:, :, 0:16:5, :], KC, E1.rearrange("p h (c i) -> p h c i", c=4), MUL, e2, tz)
            d3 = tt(E3.rearrange("p h (c i) -> p h c i", c=4)[:, :, 0:3, :],
                    BC[:, :, 0:3, 63:64].broadcast_to([128, 4, 3, 64]), BC[:, :, 0:3, :], SUB, tb)
            e3 = act(E3.rearrange("p h (c i) -> p h c i", c=4)[:, :, 0:3, :],
                     E3.rearrange("p h (c i) -> p h c i", c=4)[:, :, 0:3, :], ACT.Exp, d3)
            k1 = tt(KM4[:, :, 4:16:5, :], KC[:, :, 0:3, :],
                    E3.rearrange("p h (c i) -> p h c i", c=4)[:, :, 0:3, :], MUL, e3, qk)
            et = act(ET, BC[:, :, :, 63], ACT.Exp, tb)
            k2 = tt(KM[:, :, 2, 0:64], KM[:, :, 1, 0:64], ET[:, :, 1:2].broadcast_to([128, 4, 64]), MUL, k1, et)
            k3 = tt(KM[:, :, 3, 0:128], KM[:, :, 2, 0:128], ET[:, :, 2:3].broadcast_to([128, 4, 128]), MUL, k2)
            tp = []

            def scores(h):
                b = take()
                seq = []
                for n, (q, kk) in enumerate(((0, 0), (1, 0), (1, 1))):
                    for c in range(2 * q, 2 * q + 2):
                        o = 128 * n + 64 * (c % 2)
                        seq.append((PS[b][:, o:o + 64], KM[:, h, c, 128 * kk:128 * kk + 128],
                                    QT[:, h, 64 * c:64 * c + 64], True, True))
                m = mms(seq, PF[b], k3, tq, ki)
                d = tt(PM[:, h, :], PS[b][:, 0:384], C["tri3"], MUL, m)
                PF[b] = (d,)
                tp.append(d)

            tv = {}

            def sink(n, t, p, m):
                if n < 2:
                    e = act(VV[:, t, 512 * n:512 * n + 512], p, ACT.Copy, m)
                else:
                    o = SR[:, t, 512 * (n - 2):512 * (n - 2) + 512]
                    e = act(o, p, ACT.Tanh, m, scale=0.5)
                    e = stt(o, o, 1.0, p, ADD, MUL, e)
                tv[n, t] = e
                return (e,)

            linear_b(4, 8, tT, sink)
            for h in range(4):
                scores(h)
            ob = {}
            to = {}
            for hp in range(2):
                for t in range(2):
                    ob[t, hp] = take()
                for h in (2 * hp, 2 * hp + 1):
                    for t in range(2):
                        o = PS[ob[t, hp]][:, 256 * (h % 2):256 * (h % 2) + 256]
                        v = slice(256 * h, 256 * h + 256)
                        if t == 0:
                            seq = [(o, PM[:, h, 0:128], VV[:, 0, v], True, True)]
                        else:
                            seq = [(o, PM[:, h, 128:256], VV[:, 0, v], True, False),
                                   (o, PM[:, h, 256:384], VV[:, 1, v], False, True)]
                        to[t, h] = mms(seq, PF[ob[t, hp]] if h % 2 == 0 else (), tp[h], tv[0, t], tv[0, 0],
                                       tv[1, t], tv[1, 0])
                for t in range(2):
                    to[t, 2 * hp] = to[t, 2 * hp + 1]
            YN = ar(3072, 2, 1024)
            return head_out(ob, to, None, SR, 0.0, tv, YN, halfg[:, 0:8], tX)

        def head_out(ob, to, rden, SR, shift, tsr, YN, gcol, tx):
            base = 160
            stats = TINY[:, base:base + 48]
            mv = TINY[:, base + 48:base + 64].rearrange("p (a b) -> p a b", a=8)
            ve = TINY[:, base + 64:base + 72]
            rs = TINY[:, base + 72:base + 80]
            nb = TINY[:, base + 80:base + 88]

            def head(t, h):
                return PS[ob[t, h // 2]][:, 256 * (h % 2):256 * (h % 2) + 256]

            ta = []
            for i, (t, h) in enumerate((t, h) for t in range(2) for h in range(4)):
                ta.append(V(lambda e, i=i, t=t, h=h: e.bn_stats(stats[:, 6 * i:6 * i + 6], head(t, h)), to[t, h]))
            tb = [V(lambda e, i=i: e.bn_aggr(mv[:, i, :], stats[:, 6 * i:6 * i + 6]), ta[i]) for i in range(8)]
            if rden is None:
                tv = ts(ve, mv[:, :, 1], 1e-5, None, ADD, ALU.bypass, tb)
                tr = rsqrt(rs, ve, 8, base + 88, tv)
            else:
                rd, trd = rden
                tv = tt(ve, rd, rd, MUL, trd)
                tv = tt(ve, ve, mv[:, :, 1], MUL, tv, tb)
                tv = ts(ve, ve, 1e-5, None, ADD, ALU.bypass, tv)
                tr = rsqrt(rs, ve, 8, base + 88, tv)
                tr = tt(rs, rs, rd, MUL, tr)
            tn = stt(nb, mv[:, :, 0], -1.0, rs, MUL, MUL, tr, tb)
            ty = []
            for t in range(2):
                ty_ = []
                for h in range(4):
                    i = 4 * t + h
                    ty_.append(act(YN[:, t, 256 * h:256 * h + 256], head(t, h), ACT.Identity, tn,
                                   scale=rs[:, i:i + 1], bias=nb[:, i:i + 1]))
                for hp in range(2):
                    PF[ob[t, hp]] = (ty_[2 * hp + 1],)
                ty.append(stt(YN[:, t, :], SR[:, t, :], shift, YN[:, t, :], ADD, MUL, ty_, list(tsr.values())))
            tT = []
            for g in range(4):
                b = take()
                m = turns([(PS[b][:, 256 * k + 128 * t:256 * k + 128 * t + 128],
                            YN[:, t, 128 * (2 * g + k):128 * (2 * g + k) + 128])
                           for k in range(2) for t in range(2)], PF[b], ty)
                for k in range(2):
                    kt = 2 * g + k
                    th = act(TH[:, kt, :], PS[b][:, 256 * k:256 * k + 256], ACT.Copy, m, scale=gcol[:, kt:kt + 1])
                for k in range(2):
                    kt = 2 * g + k
                    tl = stt(TL[:, kt, :], PS[b][:, 256 * k:256 * k + 256], gcol[:, kt:kt + 1], TH[:, kt, :],
                             MUL, SUB, th)
                    tT.append(tl)
                PF[b] = (tl,)
            tz = []

            def sink(n, t, p, m):
                z = X[:, t, 512 * n:512 * n + 512]
                e = stt(z, z, ALPHA, p, MUL, ADD, m, tx)
                tz.append(e)
                return (e,)

            linear_b(2, 8, tT, sink)
            return tz

        def moe(i, tx, tf):
            nonlocal st
            XH, XL = ar(0, 2, 1024, dt=F32R), ar(2048, 2, 1024, dt=F32R)
            XG = [T2[:, :].rearrange("p (e k s) -> p e k s", e=4, k=8), ar(4096, 4, 8, 128, dt=F32R)]
            PTR = [ar(8192 + 512 * n, 2, 256, dt=F32R) for n in range(2)]
            GF = [ar(9216 + 256 * n, 256) for n in range(2)]
            G2 = [ar(9728 + 512 * n, 4, 2, 64, dt=F32R) for n in range(2)]
            YH, YL = ar(10752, 1024, dt=F32R), ar(11776, 1024, dt=F32R)
            R1 = [ar(12800 + 512 * n, 512) for n in range(2)]
            R3 = [ar(13824 + 512 * n, 512) for n in range(2)]
            PR = FR[:, :].rearrange("p (t e s) -> p t e s", t=2, e=16)
            base = 64

            def tiny(n, *shape):
                nonlocal base
                ap = TINY[:, base:base + n]
                base += n
                return ap

            b = take()
            rt = VE["router"].rearrange("p (k e) -> p k e", k=8)
            m = mms([(PS[b][:, 16 * t:16 * t + 16], F[:, k, 128 * t:128 * t + 128], rt[:, k, :], k == 0, k == 7)
                     for t in range(2) for k in range(8)], PF[b], tf)
            aff, sel, gate = tiny(32), tiny(32), tiny(32)
            t = act(aff, PS[b][:, 0:32], ACT.Tanh, m, scale=0.5)
            PF[b] = (t,)
            t_aff = ts(aff, aff, 0.5, 0.5, MUL, ADD, t)

            def ranks(v, n, o, more, *after):
                a = v.rearrange("p (g e) -> p g e", e=n)
                shape = [128, more, n, n]
                x, y = CMP[:, 0:more * n * n], CMP[:, 128:128 + more * n * n]
                x4, y4 = (z.rearrange("p (g e f) -> p g e f", e=n, f=n) for z in (x, y))
                other, own = a.unsqueeze(2).broadcast_to(shape), a.unsqueeze(3).broadcast_to(shape)
                t1 = tt(x4, other, own, ALU.is_gt, *after)
                t2 = tt(y4, other, own, ALU.is_equal, *after)
                low = C["low"].rearrange("p (e f) -> p e f", e=n).unsqueeze(1).broadcast_to(shape)
                t2 = tt(y4, y4, low, MUL, t2)
                t1 = tt(x, x, y, ADD, t1, t2)
                return V(lambda e: e.tensor_reduce(o.rearrange("p (g e) -> p g e", e=n), x4, AX.X, ADD), t1)

            CMP = R3[0]
            rk, gs, gk = tiny(32), tiny(8), tiny(8)
            t = ranks(aff, 4, rk, 8, t_aff)
            t = ts(sel, rk, 2.0, None, ALU.is_lt, ALU.bypass, t)
            t = tt(gate, aff, sel, MUL, t)
            t = V(lambda e: e.tensor_reduce(gs, gate.rearrange("p (g e) -> p g e", e=4), AX.X, ADD), t)
            t = ranks(gs, 4, gk, 2, t)
            t = ts(gk, gk, 1.0, None, ALU.is_lt, ALU.bypass, t)
            own = gk.unsqueeze(2).broadcast_to([128, 8, 4])
            t_sel = tt(sel.rearrange("p (g e) -> p g e", e=4), sel.rearrange("p (g e) -> p g e", e=4), own, MUL, t)
            t = tt(gate.rearrange("p (g e) -> p g e", e=4), gate.rearrange("p (g e) -> p g e", e=4), own, MUL, t)
            den = tiny(2)
            t = V(lambda e: e.tensor_reduce(den, gate.rearrange("p (t e) -> p t e", t=2), AX.X, ADD), t)
            t = V(lambda e: e.reciprocal(den, den), t)
            t_gate = tt(gate.rearrange("p (t e) -> p t e", t=2), gate.rearrange("p (t e) -> p t e", t=2),
                        den.unsqueeze(2).broadcast_to([128, 2, 16]), MUL, t)
            b = take()
            m = mms([(PS[b][:, 0:16], C["before"], sel[:, 0:16], True, True),
                     (PS[b][:, 16:32], C["ones"], sel[:, 0:16], True, False),
                     (PS[b][:, 16:32], C["before"], sel[:, 16:32], False, True),
                     (PS[b][:, 32:48], C["ones"], sel[:, 0:16], True, False),
                     (PS[b][:, 32:48], C["ones"], sel[:, 16:32], False, True)], PF[b], t_sel)
            pm, most = tiny(32), tiny(1)
            t_pm = stt(pm, PS[b][:, 0:32], 1.0, sel, ADD, MUL, m)
            t = V(lambda e: e.tensor_reduce(most, PS[b][:, 32:48], AX.X, MAX), m)
            PF[b] = (t_pm, t)
            t_flag = ts(FLAG[0:1, i:i + 1], most[0:1, :], 64.0, None, ALU.is_gt, ALU.bypass, t)
            parts[i] = {n: Part(f"full{i}_{n}", FLAG[0:1, i:i + 1], (t_flag,))
                        for n in ("sync", "act", "dve", "pool", "pe")}

            def one_hot(*after):
                return [tt(PR[:, q, :, :], C["slots"].unsqueeze(1).broadcast_to([128, 16, 64]),
                           pm[:, 16 * q:16 * q + 16].unsqueeze(2).broadcast_to([128, 16, 64]), ALU.is_equal, *after)
                        for q in range(2)]

            tP = one_hot(t_pm)
            tXL = [split(X[:, q, :], XH[:, q, :], XL[:, q, :], tx[q]) for q in range(2)]
            GS = tiny(16)

            pinned = [take() for _ in range(4)]
            for p in pinned:
                turn.remove(p)
            YB = {(t, n): pinned[2 * t + n] for t in range(2) for n in range(2)}
            tA, tT, tC, tS, tG, tY = {}, {}, {}, {}, {}, {}
            tXG = {}
            tPT = {}
            tTW, tSM = {}, {}
            TW = [ar(17000 + 512 * n, 2, 2, 2, 64, dt=F32R) for n in range(2)]

            def gather(g, ks):
                for k in ks:
                    b = take()
                    seq = []
                    for hl, src in enumerate((XH, XL)):
                        for q in range(2):
                            seq.append((PS[b][:, 256 * hl:256 * hl + 256], src[:, q, 128 * k:128 * k + 128],
                                        PR[:, q, 4 * g:4 * g + 4, :], q == 0, q == 1))
                    m = mms(seq, PF[b], tP, tXL)
                    o = XG[g % 2][:, :, k, :].rearrange("p e (h s) -> p h e s", h=2)
                    i = PS[b][:, :].rearrange("p (h e s) -> p h e s", h=2, e=4)
                    free = tA[4 * g - 5] if g >= 2 else ()
                    if k % 2:
                        t = cp(o, i, m, free)
                    else:
                        t = act(o, i, ACT.Copy, m, free)
                    PF[b] = (t,)
                    tXG.setdefault(g, []).append(t)

            def double(e):
                for q in range(2):
                    o = TW[e // 2 % 2][:, q, :, :, :]
                    i = PR[:, q, e:e + 2, :].unsqueeze(2).broadcast_to([128, 2, 2, 64])
                    t = G(lambda en, o=o, i=i: en.tensor_copy(o, i), tP, tPT.get(e - 3, ()))
                tTW[e] = tTW[e + 1] = t

            def twice(e, q):
                return TW[e // 2 % 2][:, q, e % 2, :, :].rearrange("p d s -> p (d s)")

            def scatter_maps(e):
                b, bg = take(), take()
                m = mms([(PS[b][:, 256 * d + 128 * q:256 * d + 128 * q + 128], twice(e + d, q), IDR[:, :], True, True)
                         for d in range(2) for q in range(2)], PF[b], tTW[e], t_idr)
                mg = mms([(PS[bg][:, d:d + 1], twice(e + d, q).bitcast(F32),
                           gate[:, 16 * q + e + d:16 * q + e + d + 1], q == 0, q == 1)
                          for d in range(2) for q in range(2)], PF[bg], t_gate)
                t = act(PTR[e // 2 % 2], PS[b][:, :].rearrange("p (d i) -> p d i", d=2), ACT.Copy, m,
                        tS.get(e - 3, ()))
                tg = cp(GS[:, e:e + 2], PS[bg][:, 0:2], mg)
                PF[b], PF[bg] = (t,), (tg,)
                tPT[e] = tPT[e + 1] = mg
                tSM[e] = tSM[e + 1] = (t, tg)

            def up(e):
                tok2 = []
                for r in (R1, R3):
                    b = take()
                    for uu in range(4):
                        u, h, l, tok = unit()
                        seq = []
                        for j in range(2):
                            k = 2 * uu + j
                            x = XG[e // 4 % 2][:, e % 4, k, :]
                            seq += [(PS[b][:, :], x, h[:, 512 * j:512 * j + 512], k == 0, False),
                                    (PS[b][:, :], x, l[:, 512 * j:512 * j + 512], False, k == 7)]
                        m = mms(seq, tok, tXG[e // 4], PF[b] if uu == 0 else ())
                        used(u, m)
                    t = act(r[e % 2], PS[b][:, :], ACT.Copy, m, tT.get(e - 2, ()), t_gate)
                    PF[b] = (t,)
                    tok2.append(t)
                tA[e] = m
                return tok2

            def act_mul(e, tok2):
                b = take()
                m = mms([(PS[b][:, 256 * w + 64 * f:256 * w + 64 * f + 64], r[e % 2][:, 128 * f:128 * f + 128],
                          C["fold"], True, True) for w, r in enumerate((R1, R3)) for f in range(4)], PF[b], tok2)
                tT[e] = m
                gf = GF[e % 2]
                t = act(gf, PS[b][:, 0:256], ACT.Tanh, m, tG.get(e - 2, ()), scale=0.5)
                t = stt(gf, gf, 1.0, PS[b][:, 0:256], ADD, MUL, t)
                t = stt(gf, gf, 0.5, PS[b][:, 256:512], MUL, MUL, t)
                PF[b] = (t,)
                g3 = gf.rearrange("p (f s) -> p f s", f=4)
                th = act(G2[e % 2][:, :, 0, :], g3, ACT.Copy, t, tC.get(e - 2, ()))
                tG[e] = tt(G2[e % 2][:, :, 1, :], g3, G2[e % 2][:, :, 0, :], SUB, th)

            def down(e):
                tY[e] = []
                for n in range(2):
                    b = take()
                    for uu in range(2):
                        u, h, l, tok = unit()
                        seq = []
                        for j in range(2):
                            k = 2 * uu + j
                            x = G2[e % 2][:, k, :, :]
                            seq += [(PS[b][:, :], x, h[:, 512 * j:512 * j + 512], k == 0, False),
                                    (PS[b][:, :], x, l[:, 512 * j:512 * j + 512], False, k == 3)]
                        m = mms(seq, tok, tG[e], PF[b] if uu == 0 else ())
                        used(u, m)
                    yh, yl = YH[:, 512 * n:512 * n + 512], YL[:, 512 * n:512 * n + 512]
                    t = act(yh, PS[b][:, :], ACT.Copy, m, tSM[e][1], tS.get(e - 1, ()), scale=GS[:, e:e + 1])
                    t = stt(yl, PS[b][:, :], GS[:, e:e + 1], yh, MUL, SUB, t)
                    PF[b] = (t,)
                    tY[e].append(t)
                tC[e] = m

            def scatter(e):
                seq = []
                for t in range(2):
                    w = PTR[e // 2 % 2][:, e % 2, 128 * t:128 * t + 128]
                    for n in range(2):
                        o = PS[YB[t, n]][:, :]
                        seq += [(o, w, YH[:, 512 * n:512 * n + 512], first and e == 0, False),
                                (o, w, YL[:, 512 * n:512 * n + 512], False, e == 15)]
                tS[e] = mms(seq, tY[e], tSM[e][0], [PF[p] for p in pinned] if first and e == 0 else ())

            def experts():
                double(0)
                gather(0, range(8))
                for e in range(16):
                    tok2 = up(e)
                    if e % 2 == 0:
                        scatter_maps(e)
                        if e + 2 < 16:
                            double(e + 2)
                    if e:
                        down(e - 1)
                    act_mul(e, tok2)
                    if e:
                        scatter(e - 1)
                    if e % 4 >= 2 and e < 12:
                        gather(e // 4 + 1, range(4 * (e % 4 - 2), 4 * (e % 4 - 2) + 4))
                down(15)
                scatter(15)

            first = True
            experts()
            first = False
            t_main = tS[15]

            queues = {"sync": Y, "act": S, "dve": V, "pool": G, "pe": P}
            now = [(q.sem, q.n) for q in (P, S, V, G)]
            main, banks, order = st, list(PF), list(turn)
            PF[:] = [()] * 8
            for n, q in queues.items():
                q.enter(sem(f"s_x{i}_{n}"))
            for n, q in queues.items():
                q.bare(lambda e: e.nop(), now)
            st = stream(3 * small["moe"][i], [sem(f"s_x{i}_raw{n}") for n in range(NR)], {})
            for _ in range(NR):
                issue()
            for _ in range(3):
                for d in (tA, tT, tC, tS, tG, tY, tXG, tPT, tTW, tSM):
                    d.clear()
                done = [(q.sem, q.n) for q in (P, S, V, G) if q.n]
                t = ts(pm, pm, 64.0, None, SUB, ALU.bypass, done)
                tP = one_hot(t, done)
                t_past = tP[1]
                experts()
            done = [(q.sem, q.n) for q in (P, S, V, G)]
            for n, q in queues.items():
                q.bare(lambda e: e.nop(), done)
                part = parts[i][n]
                part.sem, part.items = q.leave()
                if n != "sync":
                    q.items.append(part)
            st, PF[:], turn[:] = main, banks, order
            st["stops"] = {c: n for c, n in st["stops"].items() if n != i}
            tS[15] = t_main
            tz = []
            for (t, n), p in YB.items():
                z = X[:, t, 512 * n:512 * n + 512]
                e = stt(z, z, ALPHA, PS[p][:, :], MUL, ADD, tS[15])
                PF[p] = (e,)
                tz.append(e)
            turn.extend(pinned)
            return tz

        def mlstm(tx, tT):
            CV, VV, SO = ar(0, 16, 256), ar(4096, 2, 1024), ar(6144, 2, 1024)
            PT, W = ar(8192, 4, 384), ar(9728, 4, 384)
            YN = ar(11264, 2, 1024)
            TQ = ar(13312, 2, 512)
            RO = [ar(14336 + 256 * n, 256) for n in range(2)]
            base = 272

            def tiny(n, g=None):
                nonlocal base
                ap = TINY[:, base:base + n]
                base += n
                return ap if g is None else ap.rearrange("p (t h) -> p t h", t=g)

            b = take()
            mg = VE["mgate"].rearrange("p (k e) -> p k e", k=8)
            seq = []
            for t in range(2):
                seq += [(PS[b][:, 8 * t:8 * t + 8], F[:, k, 128 * t:128 * t + 128], mg[:, k, :], k == 0, False)
                        for k in range(8)]
                seq.append((PS[b][:, 8 * t:8 * t + 8], C["ones"][0:1, :], VE["mbias"][0:1, :], False, True))
            m = mms(seq, PF[b], tT)
            gt = PS[b][:, 0:16].rearrange("p (t g) -> p t g", t=2)
            fg, it, th, z, q, lf = (tiny(8, 2) for _ in range(6))
            t = cp(fg, gt[:, :, 4:8], m)
            ti = cp(it, gt[:, :, 0:4], m)
            PF[b] = (ti,)
            t = stt(th, fg, -1.0, fg, MUL, MAX, t)
            t = act(th, th, ACT.Tanh, t, scale=0.5)
            t1 = ts(z, th, 3.0, None, ADD, ALU.bypass, t)
            t1 = V(lambda e: e.reciprocal(z, z), t1)
            t = ts(th, th, -1.0, 1.0, MUL, ADD, t, t1)
            t = tt(th, th, z, MUL, t, t1)
            t = tt(z, th, th, MUL, t)
            t = ts(q, z, 1.0 / 17.0, None, MUL, ALU.bypass, t)
            for n in (15, 13, 11, 9, 7, 5, 3):
                t = stt(q, q, 1.0 / n, z, ADD, MUL, t)
            t = stt(q, q, 1.0, th, ADD, MUL, t)
            t = ts(q, q, -2.0, None, MUL, ALU.bypass, t)
            t = stt(lf, fg, 0.0, q, MIN, ADD, t)
            causal = C["tri3"][:, 0:128]
            b = take()
            m = mms([(PS[b][:, 0:4], causal, lf[:, 0, :], True, True),
                     (PS[b][:, 4:8], C["ones"], lf[:, 0, :], True, False),
                     (PS[b][:, 4:8], causal, lf[:, 1, :], False, True)], PF[b], t)
            bc, aj = tiny(8, 2), tiny(8, 2)
            t = cp(bc, PS[b][:, 0:8].rearrange("p (t h) -> p t h", t=2), m)
            PF[b] = (t,)
            t_aj = tt(aj, it, bc, SUB, t, ti)
            b = take()
            m = turns([(PS[b][0:4, 128 * q_:128 * q_ + 128], aj[:, q_, :]) for q_ in range(2)], PF[b], t_aj)
            t = cp(RO[0][0:4, :], PS[b][0:4, 0:256], m)
            PF[b] = (t,)
            cur = 0
            for sh in (1, 2, 4, 8, 16, 32, 64, 128):
                a, o = RO[cur][0:4, :], RO[1 - cur][0:4, :]
                t1 = cp(o[:, 0:sh], a[:, 0:sh], t)
                t2 = tt(o[:, sh:256], a[:, sh:256], a[:, 0:256 - sh], MAX, t)
                t = (t1, t2)
                cur = 1 - cur
            MR = RO[cur]
            b = take()
            m = mms([(PS[b][:, 4 * q_:4 * q_ + 4], MR[0:4, 128 * q_:128 * q_ + 128], ident[0:4, 0:4], True, True)
                     for q_ in range(2)], PF[b], t)
            em = tiny(8, 2)
            t2 = tt(em, bc, PS[b][:, 0:8].rearrange("p (t h) -> p t h", t=2), ADD, m)
            PF[b] = (t2,)
            t_em = act(em, em, ACT.Exp, t2, scale=-1.0)
            tp = []
            for hp in range(2):
                b = take()
                m = mms([(PS[b][:, 256 * hh:256 * hh + 256], C["heads"][0:4, 128 * (2 * hp + hh):128 * (2 * hp + hh) + 128],
                          MR[0:4, :], True, True) for hh in range(2)], PF[b], t)
                for hh in range(2):
                    h = 2 * hp + hh
                    p = PS[b][:, 256 * hh:256 * hh + 256]
                    tp.append(ts(PT[:, h, 0:256], p, aj[:, 0, h:h + 1], 0.0, SUB, MAX, m, t_aj))
                    tp.append(ts(PT[:, h, 256:384], p[:, 128:256], aj[:, 1, h:h + 1], 0.0, SUB, MAX, m, t_aj))
                PF[b] = (tp[-1],)
            t = act(PT, PT, ACT.Exp, tp, scale=-1.0)
            t_pt = tt(PT, PT, C["tri3"].unsqueeze(1).broadcast_to([128, 4, 384]), MUL, t)

            cw = VE["conv_w"].rearrange("p (j m) -> p j m", j=4)
            cb = VE["conv_b"]
            tcv = []

            def sink_qk(n, p, m):
                tk = []
                for i in range(2):
                    mt = 2 * n + i
                    tk.append(act(CV[:, mt, :], p[:, 256 * i:256 * i + 256], ACT.Identity, m,
                                  scale=cw[:, 3, mt:mt + 1], bias=cb[:, mt:mt + 1]))
                tk = [tk[1], tk[1]]
                for j in (1, 2, 3):
                    for i in range(2):
                        mt = 2 * n + i
                        o = CV[:, mt, j:256]
                        tk[i] = stt(o, p[:, 256 * i:256 * i + 256 - j], cw[:, 3 - j, mt:mt + 1], o, MUL, ADD, tk[i])
                c2 = CV[:, 2 * n:2 * n + 2, :]
                q2 = TQ[:, n % 2, :].rearrange("p (i j) -> p i j", i=2)
                t = act(q2, c2, ACT.Tanh, tk, tcv[n - 2] if n >= 2 else (), scale=0.5)
                tcv.append(stt(c2, q2, 1.0, c2, ADD, MUL, t))
                return (tk[1],)

            linear_a(16, 8, tT, sink_qk)
            tv = {}

            def sink(n, t, p, m):
                if n < 2:
                    e = act(VV[:, t, 512 * n:512 * n + 512], p, ACT.Copy, m)
                else:
                    e = act(SO[:, t, 512 * (n - 2):512 * (n - 2) + 512], p, ACT.Tanh, m, scale=0.5)
                tv[n, t] = e
                return (e,)

            tw = []

            def scores(h):
                b = take()
                seq = []
                for kk in range(2):
                    kt, qt = CV[:, 8 + 2 * h + kk, :], CV[:, 2 * h + kk, :]
                    seq.append((PS[b][:, 0:256], kt[:, 0:128], qt, kk == 0, kk == 1))
                for kk in range(2):
                    kt, qt = CV[:, 8 + 2 * h + kk, :], CV[:, 2 * h + kk, :]
                    seq.append((PS[b][:, 256:384], kt[:, 128:256], qt[:, 128:256], kk == 0, kk == 1))
                m = mms(seq, PF[b], tcv)
                d = stt(W[:, h, :], PS[b][:, 0:384], 1.0 / 64.0, PT[:, h, :], MUL, MUL, m, t_pt)
                PF[b] = (d,)
                tw.append(d)

            linear_b(4, 8, tT, sink)
            for h in range(4):
                scores(h)
            ob, to = {}, {}
            bd = take()
            md = []
            first = True
            for hp in range(2):
                for t in range(2):
                    ob[t, hp] = take()
                for h in (2 * hp, 2 * hp + 1):
                    for t in range(2):
                        o = PS[ob[t, hp]][:, 256 * (h % 2):256 * (h % 2) + 256]
                        d = PS[bd][:, 4 * t + h:4 * t + h + 1]
                        v = slice(256 * h, 256 * h + 256)
                        one = C["ones"][:, 0:1]
                        if t == 0:
                            seq = [(o, W[:, h, 0:128], VV[:, 0, v], True, True), (d, W[:, h, 0:128], one, True, True)]
                        else:
                            seq = [(o, W[:, h, 128:256], VV[:, 0, v], True, False),
                                   (o, W[:, h, 256:384], VV[:, 1, v], False, True),
                                   (d, W[:, h, 128:256], one, True, False), (d, W[:, h, 256:384], one, False, True)]
                        to[t, h] = mms(seq, PF[ob[t, hp]] if h % 2 == 0 else (), PF[bd] if first else (), tw[h],
                                       tv[0, t], tv[0, 0], tv[1, t], tv[1, 0])
                        first = False
                for t in range(2):
                    to[t, 2 * hp] = to[t, 2 * hp + 1]
            ab, rd = tiny(8), tiny(8)
            t = ts(ab, PS[bd][:, 0:8], 0.0, None, ADD, ALU.bypass, to[1, 3])
            PF[bd] = (t,)
            t = stt(ab, ab, -1.0, ab, MUL, MAX, t)
            t = tt(ab, ab, em.rearrange("p t h -> p (t h)"), MAX, t, t_em)
            t = V(lambda e: e.reciprocal(rd, ab), t)
            return head_out(ob, to, (rd, t), SO, 1.0, tv, YN, halfg[:, 8:16], tx)

        def block2(l, tx):
            QK = ar(0, 17, 256)
            VB = ar(4352, 2, 896)
            ST = [ar(6144 + 1024 * n, 2, 512) for n in range(2)]
            RT = [ar(8192 + 1024 * n, 2, 512) for n in range(2)]
            BB = ar(10240, 2, 512)
            GA = ar(11264, 16, 256)
            TG = ar(15360, 8, 2, 2, 64)
            TB, GN = ar(11264, 2, 2, 2, 64), ar(11264 + 512, 8, 2, 64)
            PB = [ar(6144 + 512 * n, 2, 256) for n in range(6)]
            PTT = [ar(9216 + 512 * n, 2, 256) for n in range(4)]
            MK = F[:, :, :].rearrange("p a b -> p (a b)")[:, 0:1536].rearrange("p (g i) -> p g i", g=3)
            OH = T2[:, 0:1536].rearrange("p (k i) -> p k i", k=6)
            OL = T2[:, 1536:3072].rearrange("p (k i) -> p k i", k=6)
            MH, ML = ar(0, 8, 256, dt=F32R), ar(2048, 8, 256, dt=F32R)
            GT = [ar(6144 + 1024 * n, 1024) for n in range(2)]
            DG = [ar(8192 + 128 * n, 128) for n in range(8)]
            ZT = [ar(9216 + 512 * n, 512) for n in range(4)]
            RR = [ar(512 * n, 512) for n in range(2)]
            RH = [ar(1024 + 512 * n, 2, 256, dt=F32R) for n in range(2)]
            RL = [ar(2048 + 512 * n, 2, 256, dt=F32R) for n in range(2)]
            JK = ar(3072, 2, 1024)
            base = 272

            def tiny(n):
                nonlocal base
                ap = TINY[:, base:base + n]
                base += n
                assert base <= 512
                return ap

            prior = small_ap.get("b2", ())
            ss, rs = tiny(2), tiny(2)
            scg = tiny(8)
            scratch = tiny(4)

            def rms_T(gcol, sc, sh, tx, deps, wait_T, wait_F, wait_J):
                XN = JK
                t2 = [act(XN[:, t, :], X[:, t, :], ACT.Square, tx, wait_J, accum_out=ss[:, t:t + 1]) for t in range(2)]
                t = ts(ss, ss, 1.0 / 1024.0, 1e-6, MUL, ADD, t2)
                t = rsqrt(rs, ss, 2, 512 - 4, t)
                t_s = stt(scg, sc, 1.0, gcol, ADD, MUL, deps)
                xn = [ts(XN[:, q, :], X[:, q, :], rs[:, q:q + 1], None, MUL, ALU.bypass, t) for q in range(2)]
                return transposed(XN, (xn, t_s), scg, sh, True, True, wait_F, wait_T)

            ada = ADA[:, l, :]
            tT, m_last = rms_T(VE["g_mix"][:, 8 * l:8 * l + 8], ada[:, 8:16], ada[:, 0:8], tx,
                               (ada_tok[l, 0],), prior, prior, prior)

            t1 = gload(TB, D["rope"].rearrange("p (a b c d) -> p a b c d", a=2, b=2, c=2), prior)
            t2 = gload(GN[0:1, :, :, :], D["gains"][l:l + 1, :].rearrange("p (a b c) -> p a b c", a=8, b=2), prior)
            gflat = GN.rearrange("p a b c -> p (a b c)")
            t2 = G(lambda e: e.partition_broadcast(gflat, gflat[0:1, :]), t2)
            t_tab = []
            for kind in range(8):
                o = TG[:, kind, :, :, :]
                a = TB[:, 0 if kind < 2 else 1, :, :, :]
                b_ = GN[:, kind, :, :].unsqueeze(2).broadcast_to([128, 2, 2, 64])
                t_tab.append(G(lambda e, o=o, a=a, b_=b_: e.tensor_tensor(o, a, b_, MUL), t1, t2, prior))
            t_mask = gload(MK, D["masks"].rearrange("p (g i) -> p g i", g=3), tT)

            segs = [([(0, 8, 0)], []), ([(0, 2, 1), (128, 4, 2)], [(384, 2, 0)]), ([(0, 4, 3)], [(256, 4, 128)]),
                    ([(0, 4, 4), (256, 4, 5)], []), ([(0, 4, 7)], [(256, 4, 384)]), ([(0, 4, 6)], [(256, 4, 640)])]
            t_qk, t_v = {}, []
            RSV = [tiny(16) for _ in range(2)]
            SSV = [tiny(16) for _ in range(2)]
            RSC = tiny(32)
            npair = 0
            t_free = {"ST": [prior, prior], "RT": [prior, prior], "BB": prior,
                      "SQ": [ada_tok["acc"], ada_tok["acc"]]}
            SQ = [ACC[:, 1024 * n:1024 * n + 1024].rearrange("p (t c) -> p t c", t=2) for n in range(2)]
            raws = {}

            def sink_qkv(n, t, p, m):
                qk, vs = segs[n]
                w = sum(h for _, h, _ in qk) * 64
                par = n % 2
                e = []
                for c, h, o in vs:
                    x = act(VB[:, t, o:o + 64 * h], p[:, c:c + 64 * h], ACT.Copy, m, prior)
                    t_v.append(x)
                e.append(act(ST[par][:, t, 0:w], p[:, 0:w], ACT.Copy, m, t_free["ST"][par]))
                e.append(act(SQ[par][:, t, 0:w], p[:, 0:w], ACT.Square, m, t_free["SQ"][par]))
                raws.setdefault(n, []).extend(e)
                if t == 1:
                    later.append(n)
                return (e[-1],)

            later = []

            def rope(n):
                nonlocal npair
                qk, _ = segs[n]
                nh = sum(h for _, h, _ in qk)
                w = nh * 64
                par = n % 2
                sv, rv = SSV[par][:, 0:2 * nh], RSV[par][:, 0:2 * nh]
                t = V(lambda e: e.tensor_reduce(sv.rearrange("p (t h) -> p t h", t=2),
                                                SQ[par][:, :, 0:w].rearrange("p t (h d) -> p t h d", d=64), AX.X, ADD), raws[n])
                t_free["SQ"][par] = t
                t = ts(sv, sv, 1.0 / 64.0, 1e-6, MUL, ADD, t)
                t = rsqrt(rv, sv, 2 * nh, RSC, t)
                x = ST[par][:, :, 0:w].rearrange("p t (h d) -> p t h d", d=64)
                t = tt(x, x, rv.rearrange("p (t h) -> p t h", t=2).unsqueeze(3).broadcast_to([128, 2, nh, 64]), MUL, t)
                done = []
                for c, h, kind in qk:
                    for q in range(2):
                        xx = ST[par][:, q, c:c + 64 * h]
                        rr = RT[par][:, q, c:c + 64 * h]
                        bb = BB[:, q, c:c + 64 * h]
                        cg = TG[:, kind, 0, q, :].unsqueeze(1).broadcast_to([128, h, 64])
                        done.append(tt(rr.rearrange("p (h d) -> p h d", d=64), xx.rearrange("p (h d) -> p h d", d=64), cg, MUL,
                                       t, t_tab, t_free["RT"][par]))
                        if kind < 2:
                            sg = TG[:, kind, 1, q, :].rearrange("p (b s d) -> p b s d", b=2, s=2)
                            x5 = xx.rearrange("p (h b s d) -> p h b s d", b=2, s=2, d=16)
                            b5 = bb.rearrange("p (h b s d) -> p h b s d", b=2, s=2, d=16)
                            for s_ in range(2):
                                done.append(tt(b5[:, :, :, s_, :], x5[:, :, :, 1 - s_, :],
                                               sg[:, :, s_, :].unsqueeze(1).broadcast_to([128, h, 2, 16]), MUL, t, t_tab,
                                               t_free["BB"]))
                        else:
                            sg = TG[:, kind, 1, q, :].rearrange("p (s d) -> p s d", s=2)
                            x5 = xx.rearrange("p (h s d) -> p h s d", s=2, d=32)
                            b5 = bb.rearrange("p (h s d) -> p h s d", s=2, d=32)
                            for s_ in range(2):
                                done.append(tt(b5[:, :, s_, :], x5[:, :, 1 - s_, :],
                                               sg[:, s_, :].unsqueeze(1).broadcast_to([128, h, 32]), MUL, t, t_tab,
                                               t_free["BB"]))
                t_free["ST"][par] = done[-1]
                t = tt(RT[par][:, :, 0:w], RT[par][:, :, 0:w], BB[:, :, 0:w], ADD, done)
                t_free["BB"] = t
                np_ = nh // 2
                for p0 in range(0, np_, 2):
                    cnt = min(2, np_ - p0)
                    b = take()
                    m = turns([(PS[b][:, 256 * i + 128 * q:256 * i + 128 * q + 128],
                                RT[par][:, q, 128 * (p0 + i):128 * (p0 + i) + 128]) for i in range(cnt) for q in range(2)],
                              PF[b], t)
                    e = act(QK[:, npair:npair + cnt, :],
                            PS[b][:, 0:256 * cnt].rearrange("p (k i) -> p k i", k=cnt), ACT.Copy, m, prior)
                    PF[b] = (e,)
                    for i in range(cnt):
                        t_qk[npair + i] = e
                    npair += cnt
                t_free["RT"][par] = m

            ticks = []

            def tick(n=1):
                pass

            def sink_wrap(n, t, p, m):
                r = sink_qkv(n, t, p, m)
                if t == 1:
                    while len(later) > 1:
                        rope(later.pop(0))
                return r

            linear_b(6, 8, tT, sink_wrap)
            while later:
                rope(later.pop(0))
            t_rt = (t_free["RT"], t_free["ST"], t_free["BB"])
            ada_tok["acc"] = (t_free["SQ"][0], t_free["SQ"][1])

            tga = []

            def sink_gate(n, p, m):
                e = act(GA[:, 2 * n:2 * n + 2, :], p.rearrange("p (k i) -> p k i", k=2), ACT.Tanh, m, t_tab, scale=0.5)
                tga.append(e)
                return (e,)

            linear_a(16, 8, tT, sink_gate)
            t_gates = tga[-1]

            SC = 64 ** -0.5
            MXV = [tiny(8) for _ in range(2)]
            SMV = [tiny(8) for _ in range(2)]
            tP_free = [t_rt] * 6
            tT_free = [t_rt] * 4
            ntt = 0
            heads = [("a", p, s_) for p in range(4) for s_ in range(2)] + [("b", p, s_) for p in range(2) for s_ in range(2)]
            QP = [5, 9, 15]
            KP = [7, 11, 13]
            live = {}
            tmx = [(), ()]

            def score(i):
                kind, p, s_ = heads[i]
                rows = slice(64 * s_, 64 * s_ + 64)
                par = i % 2
                mx, sm = MXV[par], SMV[par]
                if kind == "a":
                    sets = [(p, 4, s_ * 64, None)]
                    slots = [3 * (i % 2)]
                else:
                    sets = [(QP[g] + p, KP[g] + p, 128 + 256 * g + 64 * (2 * p + s_), g) for g in range(3)]
                    slots = [3 * (i % 2) + g for g in range(3)]
                banks, tm = [], []
                for n, (qp, kp, vo, g) in enumerate(sets):
                    b = take()
                    banks.append(b)
                    m = mms([(PS[b][:, 256 * q:256 * q + 256], QK[rows, qp, 128 * q:128 * q + 128], QK[rows, kp, :], True, True)
                             for q in range(2)], PF[b], t_qk[qp], t_qk[kp])
                    sl = slots[n]
                    if g is None:
                        tm.append(V(lambda e, b=b: e.tensor_reduce(mx[:, 0:2], PS[b][:, :].rearrange("p (q k) -> p q k", q=2),
                                                                   AX.X, MAX), m, tmx[par]))
                    else:
                        for q in range(2):
                            tm.append(V(lambda e, b=b, q=q, g=g, n=n, sl=sl: e.tensor_tensor_reduce(
                                PB[sl][:, q, :], PS[b][:, 256 * q:256 * q + 256], MK[:, g, 256 * q:256 * q + 256],
                                1.0, -3e38, ADD, MAX, mx[:, 2 + 2 * n + q:3 + 2 * n + q]), m, tmx[par], t_mask, tP_free[sl]))
                        PF[b] = (tm[-1],)
                t = tm
                if kind == "b":
                    t = V(lambda e: e.tensor_reduce(mx[:, 0:2], mx[:, 2:8].rearrange("p (g q) -> p q g", q=2), AX.X, MAX), tm)
                t = ts(mx[:, 0:2], mx[:, 0:2], -SC, None, MUL, ALU.bypass, t)
                te = []
                for n, (qp, kp, vo, g) in enumerate(sets):
                    sl = slots[n]
                    for q in range(2):
                        src = PS[banks[n]][:, 256 * q:256 * q + 256] if g is None else PB[sl][:, q, :]
                        te.append(act(PB[sl][:, q, :], src, ACT.Exp, t, tP_free[sl], tmx[par], scale=SC, bias=mx[:, q:q + 1],
                                      accum_out=sm[:, 2 + 2 * n + q:3 + 2 * n + q]))
                    if g is None:
                        PF[banks[n]] = (te[-1],)
                if kind == "b":
                    t = V(lambda e: e.tensor_reduce(sm[:, 0:2], sm[:, 2:8].rearrange("p (g q) -> p q g", q=2), AX.X, ADD), te)
                    t = V(lambda e: e.reciprocal(sm[:, 0:2], sm[:, 0:2]), t)
                else:
                    t = V(lambda e: e.reciprocal(sm[:, 0:2], sm[:, 2:4]), te)
                td = []
                for n in range(len(sets)):
                    for q in range(2):
                        td.append(ts(PB[slots[n]][:, q, :], PB[slots[n]][:, q, :], sm[:, q:q + 1], None, MUL, ALU.bypass, t))
                tmx[par] = td[-1]
                live[i] = (sets, slots, td)

            tO = []
            hold = {}

            def value(i):
                nonlocal ntt
                kind, p, s_ = heads[i]
                sets, slots, td = live[i]
                rows = slice(64 * s_, 64 * s_ + 64)
                pts = []
                for n, (qp, kp, vo, g) in enumerate(sets):
                    b = take()
                    sl = slots[n]
                    m = turns([(PS[b][:, 256 * k + 128 * q:256 * k + 128 * q + 128], PB[sl][:, q, 128 * k:128 * k + 128])
                               for k in range(2) for q in range(2)], PF[b], td[2 * n], td[2 * n + 1])
                    tP_free[sl] = m
                    pt = ntt % 4
                    ntt += 1
                    o = PTT[pt]
                    pv = PS[b][:, :].rearrange("p (k i) -> p k i", k=2)
                    if n % 2:
                        e = cp(o, pv, m, tT_free[pt])
                    else:
                        e = act(o, pv, ACT.Copy, m, tT_free[pt])
                    PF[b] = (e,)
                    pts.append((pt, e, vo))
                if s_ == 0:
                    hold["b"] = take()
                b = hold["b"]
                seq = []
                for n, (pt, e, vo) in enumerate(pts):
                    for k in range(2):
                        seq.append((PS[b][rows, 0:256], VB[:, k, vo:vo + 64], PTT[pt][:, k, :],
                                    n == 0 and k == 0, n == len(pts) - 1 and k == 1))
                m = mms(seq, PF[b] if s_ == 0 else (), [e for _, e, _ in pts], t_v)
                for pt, _, _ in pts:
                    tT_free[pt] = m
                if s_ == 1:
                    tile = p if kind == "a" else 4 + p
                    th = act(OH[:, tile, :], PS[b][:, 0:256], ACT.Copy, m, t_gates)
                    tl = tt(OL[:, tile, :], PS[b][:, 0:256], OH[:, tile, :], SUB, th)
                    PF[b] = (tl,)
                    tO.append(tl)

            LAG = 1
            for i in range(len(heads) + LAG):
                if i < len(heads):
                    score(i)
                if i >= LAG:
                    value(i - LAG)
            t_att = (tO, tP_free, tT_free)

            tu = []

            def sink_a(n, p, m):
                g = GA[:, 2 * n:2 * n + 2, :]
                e = stt(g, g, 1.0, p.rearrange("p (k i) -> p k i", k=2), ADD, MUL, m, tga)
                tu.append(e)
                return (e,)

            linear_a(8, 4, tO, sink_a, OH, OL)
            tm = []

            def sink_b(n, p, m):
                g, a = GA[:, 8 + 2 * n:10 + 2 * n, :], GA[:, 2 * n:2 * n + 2, :]
                e0 = stt(g, g, 1.0, p.rearrange("p (k i) -> p k i", k=2), ADD, MUL, m, tga)
                e = tt(g, g, a, ADD, e0, tu[n])
                th = act(MH[:, 2 * n:2 * n + 2, :], g, ACT.Copy, e, scale=0.5)
                tm.append(stt(ML[:, 2 * n:2 * n + 2, :], g, 0.5, MH[:, 2 * n:2 * n + 2, :], MUL, SUB, th))
                return (e0,)

            linear_a(8, 2, tO, sink_b, OH[:, 4:6, :], OL[:, 4:6, :])

            def spread(sec, dst, *after):
                td = [ts(DG[j], ident, ada[:, 8 * sec + j:8 * sec + j + 1], None, MUL, ALU.bypass, *after) for j in range(8)]
                te = []
                for n in range(2):
                    b = take()
                    m = mms([(PS[b][:, 128 * j:128 * j + 128], C["ones"], DG[4 * n + j], True, True) for j in range(4)],
                            PF[b], td)
                    e = act(dst[:, 512 * n:512 * n + 512], PS[b][:, :], ACT.Copy, m, *after)
                    PF[b] = (e,)
                    te.append(e)
                return (te, m)

            tg1 = spread(2, GT[0], t_att, ada_tok[l, 1])
            tg2 = spread(5, GT[1], t_att, ada_tok[l, 2], tg1[1])
            tx2 = []

            def sink_o(n, t, p, m):
                z = X[:, t, 512 * n:512 * n + 512]
                e0 = tt(ZT[2 * t + n], p, GT[0][:, 512 * n:512 * n + 512], MUL, m, tg1, t_att)
                tx2.append(tt(z, z, ZT[2 * t + n], ADD, e0, tx))
                return (e0,)

            linear_b(2, 8, tm, sink_o, MH, ML)

            tT, _ = rms_T(VE["g_mlp"][:, 8 * l:8 * l + 8], ada[:, 32:40], ada[:, 24:32], tx2,
                          (ada_tok[l, 2],), tO, t_att, t_att)

            pinned = [take() for _ in range(4)]
            for p in pinned:
                turn.remove(p)
            tR, tD = {}, {}

            def ff_up(i):
                b = take()
                for w in range(2):
                    u, h, lw, tok = unit()
                    seq = []
                    for k in range(8):
                        seq += three_w(PS[b][:, 256 * w:256 * w + 256], h[:, 128 * k:128 * k + 128],
                                       lw[:, 128 * k:128 * k + 128], TH[:, k, :], TL[:, k, :], k == 0, k == 7)
                    m = mms(seq, tok, tT, PF[b] if w == 0 else ())
                    used(u, m)
                r = RR[i % 2]
                t = act(r, PS[b][:, :], ACT.Relu, m, tR.get(i - 2, ()), tx2)
                PF[b] = (t,)
                t = tt(r, r, r, MUL, t)
                r2 = r.rearrange("p (w i) -> p w i", w=2)
                th = act(RH[i % 2], r2, ACT.Copy, t, tD.get(i - 2, ()))
                tR[i] = tt(RL[i % 2], r2, RH[i % 2], SUB, th)

            def ff_down(i):
                for w in range(2):
                    u, h, lw, tok = unit()
                    seq = []
                    k = 2 * i + w
                    for n in range(2):
                        for t in range(2):
                            seq += three(PS[pinned[2 * t + n]][:, :], RH[i % 2][:, w, 128 * t:128 * t + 128],
                                         RL[i % 2][:, w, 128 * t:128 * t + 128], h[:, 512 * n:512 * n + 512],
                                         lw[:, 512 * n:512 * n + 512], k == 0, k == 31)
                    m = mms(seq, tok, tR[i], [PF[p] for p in pinned] if k == 0 else ())
                    used(u, m)
                tD[i] = m

            for i in range(16):
                ff_up(i)
                if i:
                    ff_down(i - 1)
            ff_down(15)
            tx3 = []
            for t in range(2):
                for n in range(2):
                    p = pinned[2 * t + n]
                    z = X[:, t, 512 * n:512 * n + 512]
                    e0 = tt(ZT[2 * t + n], PS[p][:, :], GT[1][:, 512 * n:512 * n + 512], MUL, tD[15], tg2, tx2)
                    PF[p] = (e0,)
                    tx3.append(tt(z, z, ZT[2 * t + n], ADD, e0))
            turn.extend(pinned)
            small_ap["b2"] = (tx3, tD[15])
            return tx3

        def finish(tok):
            s = sem("s_out")
            Y.bare(lambda e: e.dma_start(out.rearrange("(t p) d -> p t d", p=128), X[:, :, :]).then_inc(s, 16), *tok)
            Y.bare(lambda e: e.wait_ge(s, 16))

        small_ap["lnb"] = ()
        tz = gla()
        tx, tf = ln(0, 0, X, tz, False, True)
        if stop == "gla":
            finish(tx)
        else:
            tz = moe(0, tx, tf)
            tx, tT = ln(0, 1, X, tz, True, False)
            if stop == "moe0":
                finish(tx)
            else:
                tz = mlstm(tx, tT)
                tx, tf = ln(1, 0, X, tz, False, True)
                if stop == "mlstm":
                    finish(tx)
                else:
                    tz = moe(1, tx, tf)
                    tx, _ = ln(1, 1, X, tz, False, True)
                    if stop == "moe1":
                        finish(tx)
                    else:
                        small_ap["b2"] = (tx,)
                        tx = block2(0, tx)
                        if stop == "x1":
                            finish(tx)
                        else:
                            finish(block2(1, tx))

        block = ctx.enter_context(nc.Block())

        @block.sync
        def _(e):
            Y.emit(e)

        @block.scalar
        def _(e):
            S.emit(e)

        @block.vector
        def _(e):
            V.emit(e)

        @block.gpsimd
        def _(e):
            G.emit(e)

        @block.tensor
        def _(e):
            P.emit(e)
    return {"counts": {n: q.n for n, q in (("pe", P), ("act", S), ("dve", V), ("pool", G))}}


def _chunks(u):
    return np.ascontiguousarray(u.reshape(-1, 2, 128, 1024).transpose(0, 2, 1, 3)).reshape(-1, 2048)


def _stat(w):
    k, n = w.shape[0] // 128, w.shape[1] // 128
    u = w.reshape(k, 128, n, 128).transpose(2, 1, 0, 3)
    per = 8 // k
    u = u.reshape(n // per, per, 128, k, 128).transpose(0, 2, 1, 3, 4)
    return _chunks(u.reshape(-1, 128, 1024))


def _move(w):
    k, n = w.shape[0] // 256, w.shape[1] // 512
    return _chunks(w.reshape(k, 2, 128, n, 512).transpose(3, 0, 2, 1, 4).reshape(-1, 128, 1024))


def _col(v):
    return np.ascontiguousarray(np.reshape(v, (-1, 128)).T)


def _table(parts):
    where, at = {}, 0
    for n, a in parts:
        where[n] = (at, a.shape[1])
        at += a.shape[1]
    return where, np.ascontiguousarray(np.concatenate([a for _, a in parts], axis=1))


def _constants():
    f = np.float32
    i = np.arange(128)
    causal = (i[:, None] <= i[None, :]).astype(f)
    ones = np.ones((128, 128), f)
    decay = (causal * (i[:, None] // 64 == i[None, :] // 64) / 16.0).astype(f)
    fold = (i[:, None] % 64 == np.arange(64)[None, :]).astype(f)
    heads = np.zeros((128, 512), f)
    for h in range(4):
        heads[h, 128 * h:128 * h + 128] = 1.0
    return [("ident", np.eye(128, dtype=f)), ("tri3", np.concatenate([causal, ones, causal], 1)),
            ("before", (i[:, None] < i[None, :]).astype(f)), ("ones", ones), ("decay", decay),
            ("fold", fold), ("slots", np.broadcast_to(np.arange(1, 65, dtype=f), (128, 64))),
            ("low", np.broadcast_to(np.tri(4, k=-1, dtype=f).reshape(1, 16), (128, 16))), ("heads", heads)]


def layout(i):
    D = {}
    x = i["x"][0]
    D["x"] = np.ascontiguousarray(x)
    D["xT"] = np.ascontiguousarray(x.reshape(256, 8, 128).transpose(2, 1, 0).reshape(128, 2048))
    cst_at, D["cst"] = _table(_constants())
    gw = i["gla_w_in"][0]
    mw = i["mlstm_w_in"][0]
    vecs = [("gla_g", _col(i["gla_norm_g"][0])), ("mlstm_g", _col(i["mlstm_norm_g"][0])),
            ("conv_w", np.concatenate([_col(i["mlstm_conv_w"][0, j]) for j in range(4)], 1)),
            ("conv_b", _col(i["mlstm_conv_b"][0])),
            ("ln_g", _col(i["ln_g"])), ("ln_b", _col(i["ln_b"])),
            ("g_mix", _col(i["g_mix_2"])), ("g_mlp", _col(i["g_mlp_2"])), ("b_ada", _col(i["b_ada_2"])),
            ("c", _col(i["c_2"][0])),
            ("router", i["router_w"].reshape(8, 128, 16).transpose(1, 0, 2).reshape(128, 128)),
            ("glr", gw[:, 3072:].reshape(8, 128, 16).transpose(1, 0, 2).reshape(128, 128)),
            ("mbias", np.concatenate([i["mlstm_b_gates"], np.zeros((127, 8), np.float32)])),
            ("mgate", mw[:, 4096:].reshape(8, 128, 8).transpose(1, 0, 2).reshape(128, 64))]
    vec_at, D["vec"] = _table(vecs)
    D["wgu"] = np.concatenate([i["gla_w_gate_up"][0], i["gla_b_gate"]], 0)
    D["lnrow"] = np.concatenate([i["ln_g"].reshape(4, 1024), i["ln_b"].reshape(4, 1024)], 1)
    D["gla_qk"] = _stat(gw[:, 0:1024])
    D["gla_vr"] = _move(gw[:, 1024:3072])
    D["gla_o"] = _move(i["gla_w_out"][0])
    for n in range(2):
        up = [np.concatenate([_move(i["moe_w1"][n, e]), _move(i["moe_w3"][n, e])]) for e in range(16)]
        down = [_move(i["moe_w2"][n, e]) for e in range(16)]
        seq = [up[0]]
        for e in range(1, 16):
            seq += [up[e], down[e - 1]]
        D[f"moe{n}"] = np.concatenate(seq + [down[15]])
    D["ml_qk"] = _stat(mw[:, 0:2048])
    D["ml_vo"] = _move(mw[:, 2048:4096])
    D["ml_o"] = _move(i["mlstm_w_out"][0])
    ada = i["w_ada_2"]
    D["ada"] = np.ascontiguousarray(ada.reshape(2, 8, 128, 3, 2048).transpose(0, 3, 1, 2, 4)).reshape(-1, 2048)
    D["rope"], D["masks"] = _rotation(), _dilated()
    qa, ka, qb, kb = i["q_norm_a_2"], i["k_norm_a_2"], i["q_norm_b_2"], i["k_norm_b_2"]
    gains = []
    for l in range(2):
        row = []
        for n, g in enumerate([qa[l], ka[l], qb[l, 0], kb[l, 0], qb[l, 1], kb[l, 1], qb[l, 2], kb[l, 2]]):
            swap = g.reshape(2, 2, 16)[:, ::-1] if n < 2 else g.reshape(2, 32)[::-1]
            row += [g, swap.reshape(64)]
        gains.append(np.concatenate(row))
    D["gains"] = np.stack(gains)
    perm = np.concatenate([np.arange(64) + 64 * h for h in (0, 4, 1, 5, 2, 6, 3, 7)])
    lists = []
    for l in range(2):
        w = i["w_in_2"][l]
        q, k, v = w[:, 0:512][:, perm], w[:, 512:640], w[:, 640:768]
        g3 = [[w[:, 768 + 768 * g + 256 * j:1024 + 768 * g + 256 * j] for j in range(3)] for g in range(3)]
        cols = [q, k, g3[0][0], v, g3[0][1], g3[0][2], g3[1][0], g3[1][1], g3[2][1], g3[1][2], g3[2][0], g3[2][2]]
        D[f"b2_in{l}"] = _move(np.concatenate(cols, axis=1))
        D[f"b2_gate{l}"] = _stat(w[:, 3072:5120])
        D[f"b2_a{l}"] = _stat(i["w_branch_a_2"][l][perm])
        D[f"b2_b{l}"] = _stat(i["w_branch_b_2"][l])
        D[f"b2_o{l}"] = _move(i["w_out_2"][l])
        f1 = _stat(i["w_ff1_2"][l]).reshape(16, 128, 2048)
        f2 = _chunks(i["w_ff2_2"][l].reshape(32, 128, 1024)).reshape(16, 128, 2048)
        seq = [f1[0]]
        for n in range(1, 16):
            seq += [f1[n], f2[n - 1]]
        D[f"b2_ff{l}"] = np.concatenate(seq + [f2[15]])
    order = [("gla_qk", None), ("gla_vr", (0, 0)), ("gla_o", None), ("moe0", None), ("ml_qk", None),
             ("ml_vo", (0, 1)), ("ml_o", None), ("moe1", None)]
    for l in range(2):
        order += [(f"b2_in{l}", None), (f"b2_gate{l}", (0, 2) if l == 0 else None), (f"b2_a{l}", None), (f"b2_b{l}", None),
                  (f"b2_o{l}", None), (f"b2_ff{l}", (1, 0, 1, 2) if l == 0 else None)]
    return D, cst_at, vec_at, order


def _rotation():
    f = np.float32

    def cs(pos, dim):
        inv = (f(10000.0) ** (-np.arange(0, dim, 2, dtype=f) / f(dim))).astype(f)
        ang = pos.astype(f)[:, None] * inv[None, :]
        return np.cos(ang).astype(f), np.sin(ang).astype(f)

    s = np.arange(256)
    (rc, rs), (cc, c_s), (sc, ss) = cs(s // 64, 32), cs(s % 64, 32), cs(s, 64)
    ax = np.stack([np.concatenate([rc, rc, cc, cc], 1), np.concatenate([-rs, rs, -c_s, c_s], 1)])
    seq = np.stack([np.concatenate([sc, sc], 1), np.concatenate([-ss, ss], 1)])
    t = np.stack([ax, seq]).reshape(2, 2, 2, 128, 64)
    return np.ascontiguousarray(t.transpose(3, 0, 1, 2, 4)).reshape(128, 512)


def _dilated():
    i = np.arange(256)
    d = i[None, :] - i[:, None]
    m = [np.abs(d) <= 64, d % 4 == 0, d % 16 == 0]
    m = np.stack([np.where(x, 0.0, -1e30).astype(np.float32) for x in m]).reshape(3, 2, 128, 256)
    return np.ascontiguousarray(m.transpose(2, 0, 1, 3)).reshape(128, 1536)


def build(nc, D, cst_at, vec_at, order, out, stop=None):
    aps = {}
    for n, a in D.items():
        aps[n] = nc.dram_tensor(f"in_{n}", a.shape, mybir.dt.from_np(a.dtype), kind="ExternalInput").ap()
    chunks, stops, moe = [], {}, {}
    for n, extra in order:
        count = D[n].shape[0] // 128
        ada = [(extra[0], blk, k) for blk in extra[1:] for k in range(8)] if extra else []
        sent = 0
        for c in range(count):
            while sent * (count - 3) < len(ada) * (c - 3):
                l, blk, k = ada[sent]
                at = 128 * (24 * l + 8 * blk + k)
                chunks.append(("ada", aps["ada"][at:at + 128, :], l, blk, k))
                sent += 1
            chunks.append(("w", aps[n][128 * c:128 * c + 128, :]))
        for l, blk, k in ada[sent:]:
            at = 128 * (24 * l + 8 * blk + k)
            chunks.append(("ada", aps["ada"][at:at + 128, :], l, blk, k))
        if n.startswith("moe"):
            moe[int(n[3])] = chunks[-count:]
            stops[len(chunks)] = int(n[3])
    small = {"cst": (cst_at, D["cst"].shape[1]), "vec": (vec_at, D["vec"].shape[1]), "chunks": chunks, "stops": stops, "moe": moe}
    return two_block_kernel(nc, aps, out, small, stop)


def kernel(**inputs):
    import concourse.bacc as _bacc
    from concourse.bass_utils import run_bass_kernel_spmd as _run

    nc = _bacc.Bacc("TRN2", target_bir_lowering=False, num_devices=1)
    ins = {k: np.asarray(v) for k, v in inputs.items()}
    D, cst_at, vec_at, order = layout(ins)
    out = nc.dram_tensor("out_dram", (256, 1024), mybir.dt.float32, kind="ExternalOutput").ap()
    build(nc, D, cst_at, vec_at, order, out)
    r = _run(nc, [{f"in_{n}": a for n, a in D.items()}], core_ids=[0])
    return r.results[0]["out_dram"].reshape(1, 256, 1024)
```

```python
import concourse.bass as bass
from concourse import mybir
from contextlib import ExitStack
import numpy as np


class Queue:

    def __init__(self, sem):
        self.sem = sem
        self.n = 0
        self.items = []
        self.outer = None

    def __call__(self, fn, *after):
        self.n += 1
        self.items.append((fn, after, True))
        return (self.sem, self.n)

    def bare(self, fn, *after):
        self.items.append((fn, after, False))

    def enter(self, sem):
        self.outer = (self.sem, self.n, self.items)
        self.sem, self.n, self.items = sem, 0, []

    def leave(self):
        part = (self.sem, self.items)
        self.sem, self.n, self.items = self.outer
        return part

    def emit(self, eng):
        self.run(eng, self.sem, self.items, {})

    def run(self, eng, sem, items, met):
        def wait(tokens):
            for tok in tokens:
                if len(tok) == 2 and isinstance(tok[1], int):
                    if met.get(id(tok[0]), 0) < tok[1]:
                        eng.wait_ge(tok[0], tok[1])
                        met[id(tok[0])] = tok[1]
                else:
                    wait(tok)

        for item in items:
            if isinstance(item, Part):
                wait(item.after)
                with eng.register(item.name) as reg:
                    eng.reg_load(reg, item.flag)
                    with eng.If_ne(reg, 0):
                        self.run(eng, item.sem, item.items, dict(met))
                continue
            fn, after, counted = item
            wait(after)
            ins = fn(eng)
            if counted:
                ins.then_inc(sem, 1)


class Part:

    def __init__(self, name, flag, after):
        self.name, self.flag, self.after = name, flag, after
        self.sem, self.items = None, []


def two_block_kernel(nc, D, out, small, stop=None):
    F32 = mybir.dt.float32
    F32R = mybir.dt.float32r
    I32 = mybir.dt.int32
    ALU = mybir.AluOpType
    ACT = mybir.ActivationFunctionType
    AX = mybir.AxisListType
    MUL, ADD, SUB, MAX, MIN, NOP = ALU.mult, ALU.add, ALU.subtract, ALU.max, ALU.min, ALU.bypass

    ALPHA = float(4 ** 0.25)
    NR = 7
    NC = 4
    NA = 17408
    ctx = ExitStack()
    with ctx:
        def sb(name, shape, dt=F32):
            return ctx.enter_context(nc.sbuf_tensor(name, shape, dt))

        def sem(name):
            return ctx.enter_context(nc.semaphore(name))

        P, S, V, G = (Queue(sem(n)) for n in ("s_pe", "s_act", "s_dve", "s_pool"))
        Y = Queue(None)

        def act(o, i, f, *after, **kw):
            return S(lambda e: e.activation(o, i, f, **kw), *after)

        def tt(o, a, b, op, *after, q=None):
            return (q or V)(lambda e: e.tensor_tensor(o, a, b, op), *after)

        def ts(o, a, s1, s2, op0, op1, *after):
            return V(lambda e: e.tensor_scalar(o, a, s1, s2, op0=op0, op1=op1), *after)

        def stt(o, a, s, b, op0, op1, *after):
            return V(lambda e: e.scalar_tensor_tensor(out=o, in0=a, scalar=s, in1=b, op0=op0, op1=op1), *after)

        def cp(o, a, *after):
            return V(lambda e: e.tensor_copy(o, a), *after)

        def red(o, a, op, *after):
            return V(lambda e: e.tensor_reduce(o, a, AX.X, op), *after)

        def inv(o, a, *after):
            return V(lambda e: e.reciprocal(o, a), *after)

        def mms(seq, *after):
            def go(e):
                for o, l, r, a, z in seq:
                    ins = e.matmul(o, l, r, start=a, stop=z, skip_group_check=True)
                return ins
            return P(go, *after)

        def turns(seq, *after):
            def go(e):
                for o, i in seq:
                    ins = e.transpose(o, i, ident)
                return ins
            return P(go, *after)

        loads = []

        def load(dst, src, *after):
            s = sem(f"s_ld{len(loads)}")
            loads.append(s)
            Y.bare(lambda e: e.dma_start(dst, src).then_inc(s, 16), *after)
            return (s, 16)

        def gload(dst, src, *after):
            s = sem(f"s_ld{len(loads)}")
            loads.append(s)
            G.bare(lambda e: e.dma_start(dst, src).then_inc(s, 16), *after)
            return (s, 16)

        PS = [ctx.enter_context(nc.psum_tensor(f"ps{i}", [128, 512], F32)) for i in range(8)]
        PF = [()] * 8
        free = list(range(8))

        def take():
            return free.pop(0)

        def give(b, *tok):
            PF[b] = tok
            free.append(b)

        def three(o, xh, xl, wh, wl, first, last):
            return [(o, xh, wh, first, False), (o, xh, wl, False, False), (o, xl, wh, False, last)]

        def three_w(o, wh, wl, xh, xl, first, last):
            return [(o, wh, xh, first, False), (o, wh, xl, False, False), (o, wl, xh, False, last)]

        cst = sb("cst", [128, small["cst"][1]])
        vec = sb("vec", [128, small["vec"][1]])
        C = {n: cst[:, o:o + w] for n, (o, w) in small["cst"][0].items()}
        VE = {n: vec[:, o:o + w] for n, (o, w) in small["vec"][0].items()}
        ident = C["ident"]
        raw = [sb(f"raw{i}", [128, 2048]) for i in range(NR)]
        hi = [sb(f"hi{i}", [128, 1024], F32R) for i in range(NC)]
        lo = [sb(f"lo{i}", [128, 1024], F32R) for i in range(NC)]
        X = sb("X", [128, 2, 1024])
        F = sb("F", [128, 8, 256])
        FR = nc.alloc_sbuf_tensor_at("FR", [128, 2048], F32R, offset=nc.sbuf_base - 4 * 2048)
        T2 = sb("T2", [128, 4096], F32R)
        TH = T2[:, 0:2048].rearrange("p (k i) -> p k i", k=8)
        TL = T2[:, 2048:4096].rearrange("p (k i) -> p k i", k=8)
        ACC = sb("ACC", [128, 2048])
        FLAG = sb("FLAG", [1, 2], I32)
        ADA = sb("ADA", [128, 2, 48])
        IDR = sb("IDR", [128, 128], F32R)
        TINY = sb("TINY", [128, 1024])
        AR = sb("AR", [128, NA])
        AF = nc.alloc_sbuf_tensor_at("AF", [128, NA], F32R, offset=nc.sbuf_base - 4 * NA)

        def ar(o, *shape, dt=None):
            n = int(np.prod(shape))
            assert o + n <= NA
            ap = (AR if dt is None else AF)[:, o:o + n]
            if len(shape) == 1:
                return ap
            names = "abcdef"[:len(shape)]
            return ap.rearrange(f"p ({' '.join(names)}) -> p {' '.join(names)}",
                                **{k: v for k, v in zip(names[:-1], shape[:-1])})

        cols = {}
        col_at = [0]

        def tiny(name, n, split=None):
            if name not in cols:
                cols[name] = (col_at[0], n)
                col_at[0] += n
                assert col_at[0] <= 1024
            o, w = cols[name]
            assert w == n
            ap = TINY[:, o:o + n]
            return ap if split is None else ap.rearrange("p (a b) -> p a b", a=split)

        chunks, stops = small["chunks"], small["stops"]

        def stream(chunks, sems, stops):
            events = []
            for c, ch in enumerate(chunks):
                events += [("ada", c, 1)] if ch[0] == "ada" else [("w", c, 0), ("w", c, 1)]
            return {"chunks": chunks, "sems": sems, "events": events, "stops": stops, "ev": 0, "u": 0, "dma": 0,
                    "units": [], "split": [], "used": {}, "left": {}, "head": None}

        st = stream(chunks, [sem(f"s_raw{i}") for i in range(NR)], stops)
        parts = {}
        ada_tok = {"acc": ()}
        sums = []

        def issue(*after):
            c, chunks = st["dma"], st["chunks"]
            if c >= len(chunks):
                return
            st["dma"] += 1
            if c in st["stops"]:
                Y.items.append(parts[st["stops"][c]]["sync"])
            src, s, at = chunks[c][1], st["sems"][c % NR], 1024 if st["head"] and c == 0 else 0
            Y.bare(lambda e: e.dma_start(raw[c % NR][:, at:2048], src[:, at:2048]).then_inc(s, 16), *after)

        def left(c, tok):
            n = st["left"].setdefault(c, [])
            n.append(tok)
            while True:
                c = st["dma"] - NR
                n = st["left"].get(c, ())
                if c < 0 or c >= len(st["chunks"]) or len(n) < (1 if st["chunks"][c][0] == "ada" else 2):
                    return
                issue(n)
                if st["dma"] - NR == c:
                    return

        def landed(c, half=1):
            if st["head"] and c == 0 and half == 0:
                return st["head"]
            return (st["sems"][c % NR], 16 * (c // NR + 1))

        def step():
            kind, c, half = st["events"][st["ev"]]
            st["ev"] += 1
            if kind == "ada":
                left(c, ada_step(c))
                return
            r = raw[c % NR][:, 1024 * half:1024 * half + 1024]
            u = len(st["units"])
            if st["chunks"][c][2] >> half & 1:
                st["units"].append((r, None, landed(c, half), c))
                return
            n = len(st["split"])
            st["split"].append(u)
            h, l = hi[n % NC][:, :], lo[n % NC][:, :]
            th = act(h, r, ACT.Copy, landed(c, half), st["used"][st["split"][n - NC]] if n >= NC else ())
            tl = tt(l, r, h, SUB, th)
            st["units"].append((h, l, tl, None))
            left(c, tl)

        def unit():
            for s in list(sums):
                s[0] -= 1
                if s[0] < 0:
                    sums.remove(s)
                    s[1]()
            u = st["u"]
            st["u"] += 1
            while st["ev"] < len(st["events"]):
                if len(st["units"]) > u:
                    n = len(st["split"])
                    if n >= NC and st["split"][n - NC] >= u:
                        break
                    c = st["events"][st["ev"]][1]
                    if c in st["stops"] or len(st["units"]) > u + NC:
                        break
                step()
            return (u,) + st["units"][u][0:3]

        def ahead(most):
            u = len(st["units"])
            while st["ev"] < len(st["events"]) and len(st["units"]) < u + most:
                n = len(st["split"])
                if n >= NC and st["split"][n - NC] >= st["u"] or st["events"][st["ev"]][1] in st["stops"]:
                    return
                step()

        def used(u, tok):
            st["used"][u] = tok
            c = st["units"][u][3]
            if c is not None:
                left(c, tok)

        def ada_step(c):
            _, _, layer, blk, k = st["chunks"][c]
            w = raw[c % NR][:, :]
            cc = c_act[:, k:k + 1]
            if k == 0:
                for s in list(sums):
                    sums.remove(s)
                    s[1]()
                t = ts(ACC[:, :], w, cc, None, MUL, NOP, landed(c), ready["c"], ada_tok["acc"])
            else:
                t = stt(ACC[:, :], w, cc, ACC[:, :], MUL, ADD, landed(c), ada_tok["acc"])
            ada_tok["acc"] = t
            if k == 7:
                def add_up():
                    b = take()
                    m = mms([(PS[b][:, j:j + 1], ACC[:, 128 * j:128 * j + 128], C["ones"][:, 0:1], True, True)
                             for j in range(16)], PF[b], t)
                    o = layer * 48 + blk * 16
                    e = tt(ADA[:, layer, 16 * blk:16 * blk + 16], PS[b][:, 0:16], VE["b_ada"][:, o:o + 16], ADD, m)
                    give(b, e)
                    ada_tok["acc"] = (m,)
                    ada_tok[layer, blk] = e
                sums.append([3, add_up])
            return t

        side = []

        def advance(n=1):
            while n and side:
                try:
                    next(side[0])
                    n -= 1
                except StopIteration:
                    side.pop(0)

        def drain():
            while side:
                advance()

        tF = [load(F[:, 4 * g:4 * g + 4, :], D["xT"][:, 1024 * g:1024 * g + 1024].rearrange("p (k i) -> p k i", k=4))
              for g in range(2)]
        st["head"] = load(raw[0][:, 0:1024], chunks[0][1][:, 0:1024])
        issue()
        tvec = load(vec[:, :], D["vec"])
        issue()
        tcst = load(cst[:, :], D["cst"])
        WG = ar(16640, 512)[0:17, :]
        tWG = load(WG, D["wgu"])
        for _ in range(NR - 2):
            issue()
        tX = load(X[:, :, :], D["x"].rearrange("(t p) d -> p t d", p=128))

        def split(src, h, l, *after):
            th = act(h, src, ACT.Copy, *after)
            return tt(l, src, h, SUB, th)

        def rsqrt(o, v, n, name, *after):
            two = name if not isinstance(name, str) else tiny(name, 2 * n)
            y, t1 = two[:, 0:n], two[:, n:2 * n]
            t = ts(y.bitcast(I32), v.bitcast(I32), -0.5, 1597463007.0, MUL, ADD, *after)
            for i in range(3):
                t = tt(t1, y, y, MUL, t)
                t = stt(t1, t1, -0.5, v, MUL, MUL, t)
                d = o if i == 2 else y
                t = stt(d, t1, 1.5, y, ADD, MUL, t)
            return t

        def linear_a(mt, kt, waits, sink, th=None, tl=None, tick=None):
            th = TH if th is None else th
            tl = TL if tl is None else tl
            per = 8 // kt
            for n in range(mt // 2):
                b = take()
                for i in range(2):
                    m = 2 * n + i
                    if m % per == 0:
                        u, h, l, tok = unit()
                    for g in range(kt // 2):
                        seq = []
                        for k in (2 * g, 2 * g + 1):
                            c = 128 * (kt * (m % per) + k)
                            seq += three_w(PS[b][:, 256 * i:256 * i + 256], h[:, c:c + 128], l[:, c:c + 128],
                                           th[:, k, :], tl[:, k, :], k == 0, k == kt - 1)
                        done = mms(seq, tok, waits[g], PF[b] if i == 0 and g == 0 else ())
                    if m % per == per - 1:
                        used(u, done)
                        if tick and not (i == 1):
                            tick()
                give(b, *sink(n, PS[b][:, :], done))
                if tick:
                    tick()

        def linear_b(nb, kt, waits, sink, th=None, tl=None, tick=None, last=None, half=None):
            th = TH if th is None else th
            tl = TL if tl is None else tl
            for n in range(nb):
                bk = [take(), take()]
                for g in range(kt // 2):
                    if half and n == 0 and g == kt // 4:
                        half()
                    u, h, l, tok = unit()
                    done = []
                    for t in range(2):
                        seq = []
                        for j in range(2):
                            k = 2 * g + j
                            seq += three(PS[bk[t]][:, :], th[:, k, 128 * t:128 * t + 128],
                                         tl[:, k, 128 * t:128 * t + 128],
                                         h[:, 512 * j:512 * j + 512], l[:, 512 * j:512 * j + 512],
                                         k == 0, k == kt - 1)
                        done.append(mms(seq, tok, waits[g], PF[bk[t]] if g == 0 else ()))
                    used(u, done[1])
                    if tick:
                        tick()
                if last and n == nb - 1:
                    last()
                for t in range(2):
                    give(bk[t], *sink(n, t, PS[bk[t]][:, :], done[t]))

        def transposed(src, tsrc, scale, bias, with_T, tp=()):
            done, fs = [], []
            for g in range(4):
                b = take()
                m = turns([(PS[b][:, 256 * k + 128 * t:256 * k + 128 * t + 128],
                            src[:, t, 128 * (2 * g + k):128 * (2 * g + k) + 128])
                           for t in range(2) for k in range(2)], PF[b], tsrc)
                f = []
                for k in range(2):
                    kt = 2 * g + k
                    o, p = F[:, kt, :], PS[b][:, 256 * k:256 * k + 256]
                    sc, bi = scale[:, kt:kt + 1], bias[:, kt:kt + 1]
                    if with_T and g % 2:
                        f.append(ts(o, p, sc, bi, MUL, ADD, m, tp))
                    else:
                        f.append(act(o, p, ACT.Identity, m, tp, scale=sc, bias=bi))
                give(b, f[1])
                fs.append(f)
                if not with_T:
                    done.append(f[1])
                elif g % 2:
                    for j in (g - 1, g):
                        two = slice(2 * j, 2 * j + 2)
                        done.append(split(F[:, two, :], TH[:, two, :], TL[:, two, :], fs[j]))
            return done, m

        LNS = tiny("ln_stats", 24)

        def ln_rows(i, j, gb, *after):
            t = gload(gb[0:1, :], D["lnrow"][2 * i + j:2 * i + j + 1, :], *after)
            return G(lambda e: e.partition_broadcast(gb, gb[0:1, :]), t)

        def ln_piece(t, n, *after):
            o = 12 * t + 6 * n
            z = X[:, t, 512 * n:512 * n + 512]
            return V(lambda e: e.bn_stats(LNS[:, o:o + 6], z), *after)

        def ln(i, j, tz, gb, tgb, XN=None, txn=(), with_T=False, tp=()):
            o = (2 * i + j) * 8
            mv = tiny("ln_mv", 4, 2)
            tb = [V(lambda e, t=t: e.bn_aggr(mv[:, t, :], LNS[:, 12 * t:12 * t + 12]), tz) for t in range(2)]
            ve, rs, nb = tiny("ln_ve", 2), tiny("ln_rs", 2), tiny("ln_nb", 2)
            t = ts(ve, mv[:, :, 1], 1e-5, None, ADD, NOP, tb)
            tr = rsqrt(rs, ve, 2, "ln_nr", t)
            xn, done = [tr, tr], []
            if XN is not None:
                tn = stt(nb, mv[:, :, 0], -1.0, rs, MUL, MUL, tr)
                xn = [ts(XN[:, 0, :], X[:, 0, :], mv[:, 0, 0:1], rs[:, 0:1], SUB, MUL, tr, txn),
                      act(XN[:, 1, :], X[:, 1, :], ACT.Identity, tn, txn, scale=rs[:, 1:2], bias=nb[:, 1:2])]
                ahead(NC)
                done, _ = transposed(XN, xn, VE["ln_g"][:, o:o + 8], VE["ln_b"][:, o:o + 8], with_T, tp)
            tx = []

            def finish():
                for t in range(2):
                    a = stt(X[:, t, :], X[:, t, :], mv[:, t, 0:1], gb[:, 0:1024], SUB, MUL, tgb, xn[t])
                    yield
                    tx.append(stt(X[:, t, :], X[:, t, :], rs[:, t:t + 1], gb[:, 1024:2048], MUL, ADD, a, tr))
                    yield

            if with_T:
                return tx, done, finish()
            list(finish())
            if XN is None:
                ahead(1)
            return tx, done

        def head_norm(ob, to, rden, YN, res):
            stats = tiny("hn_stats", 48)
            mv = tiny("hn_mv", 16, 8)
            ve, rs, nb = tiny("hn_ve", 8), tiny("hn_rs", 8), tiny("hn_nb", 8)

            def head(t, h):
                return PS[ob[t, h // 2]][:, 256 * (h % 2):256 * (h % 2) + 256]

            ta = []
            for i in range(8):
                t, h = i // 4, i % 4
                ta.append(V(lambda e, i=i, t=t, h=h: e.bn_stats(stats[:, 6 * i:6 * i + 6], head(t, h)), to[t, h // 2]))
                if i % 4 == 3:
                    yield
            tb = [V(lambda e, i=i: e.bn_aggr(mv[:, i, :], stats[:, 6 * i:6 * i + 6]), ta[i]) for i in range(8)]
            if rden is None:
                tv = ts(ve, mv[:, :, 1], 1e-5, None, ADD, NOP, tb)
                tr = rsqrt(rs, ve, 8, "hn_nr", tv)
            else:
                rd, trd = rden
                tv = tt(ve, rd, rd, MUL, trd)
                tv = tt(ve, ve, mv[:, :, 1], MUL, tv, tb)
                tv = ts(ve, ve, 1e-5, None, ADD, NOP, tv)
                tr = rsqrt(rs, ve, 8, "hn_nr", tv)
                tr = tt(rs, rs, rd, MUL, tr)
            tn = stt(nb, mv[:, :, 0], -1.0, rs, MUL, MUL, tr, tb)
            yield
            for hp in range(2):
                for t in range(2):
                    for h in (2 * hp, 2 * hp + 1):
                        i = 4 * t + h
                        tok = act(YN[:, t, 256 * h:256 * h + 256], head(t, h), ACT.Identity, tn,
                                  scale=rs[:, i:i + 1], bias=nb[:, i:i + 1])
                    give(ob[t, hp], tok)
                    res[t, hp] = tok
                yield

        def turn_heads(g, YN, gcol, ty, tT):
            b = take()
            m = turns([(PS[b][:, 256 * k + 128 * t:256 * k + 128 * t + 128],
                        YN[:, t, 128 * (2 * g + k):128 * (2 * g + k) + 128])
                       for t in range(2) for k in range(2)], PF[b], ty)
            for k in range(2):
                kt = 2 * g + k
                th = act(TH[:, kt, :], PS[b][:, 256 * k:256 * k + 256], ACT.Copy, m, scale=gcol[:, kt:kt + 1])
            for k in range(2):
                kt = 2 * g + k
                tl = stt(TL[:, kt, :], PS[b][:, 256 * k:256 * k + 256], gcol[:, kt:kt + 1], TH[:, kt, :], MUL, SUB, th)
            give(b, tl)
            tT.append(tl)

        def mix_out(tT, tx, half):
            tz = []

            def sink(n, t, p, m):
                z = X[:, t, 512 * n:512 * n + 512]
                e = stt(z, z, ALPHA, p, MUL, ADD, m, tx)
                tz.append(ln_piece(t, n, e))
                return (e,)

            linear_b(2, 8, tT, sink, half=half)
            return tz

        ready = {}
        c_act, halfg = tiny("c_act", 8), tiny("halfg", 16)

        def constants():
            th, u = tiny("c_th", 8), tiny("c_u", 8)
            t = act(th, VE["c"], ACT.Tanh, tvec, scale=0.5)
            t = stt(u, th, 1.0, VE["c"], ADD, MUL, t)
            ready["c"] = ts(c_act, u, 0.5, None, MUL, NOP, t)
            g0 = small["vec"][0]["gla_g"][0]
            ts(halfg, vec[:, g0:g0 + 16], 0.5, None, MUL, NOP, tvec)
            ready["idr"] = act(IDR[:, :], ident, ACT.Copy, tcst)

        def gla():
            QT, KT, BT = ar(0, 4, 256), ar(1024, 4, 256), ar(2048, 4, 256)
            KM = ar(3072, 4, 4, 256)
            VV, SR = ar(7168, 2, 1024), ar(9216, 2, 1024)
            PM = ar(11264, 4, 384)
            E1, E3 = ar(12800, 4, 256), ar(13824, 4, 256)
            LA, LB = ar(14848, 2, 512), ar(7168, 2, 512)
            GL = ar(15872, 256)
            YN = ar(3072, 2, 1024)
            ET = tiny("g_et", 16, 4)
            tz = [G(lambda e: e.memset(KM[:, :, 0, 64:128], 0.0)),
                  G(lambda e: e.memset(KM[:, :, 2, 192:256], 0.0))]
            tone = G(lambda e: e.memset(GL[0:17, :], 1.0))
            tT = [split(F[:, 2 * g:2 * g + 2, :], TH[:, 2 * g:2 * g + 2, :], TL[:, 2 * g:2 * g + 2, :], tF[g // 2])
                  for g in range(4)]
            qk, tv, tp, ob, to, ty, res = [], {}, [], {}, {}, [], {}
            km = {}
            r = {}

            def prepare():
                b = take()
                glr = VE["glr"].rearrange("p (k r) -> p k r", k=8)
                m = mms([(PS[b][0:16, 0:256], glr[:, k, :], F[:, k, :], k == 0, k == 7) for k in range(8)],
                        PF[b], tF, tvec)
                t = act(GL[0:16, :], PS[b][0:16, 0:256], ACT.Copy, m, tone)
                give(b, t)
                constants()
                yield
                zb, ta = [take(), take()], []
                for q in range(2):
                    m = mms([(PS[zb[q]][:, :], GL[0:17, 128 * q:128 * q + 128], WG, True, True)], PF[zb[q]], t, tWG)
                    ta.append(act(LA[:, q, :], PS[zb[q]][:, :], ACT.Abs, m))
                yield
                e = act(LA, LA, ACT.Exp, ta, scale=-1.0)
                e = act(LA, LA, ACT.Ln, e, bias=1.0)
                tl = []
                for q in range(2):
                    tl.append(stt(LB[:, q, :], PS[zb[q]][:, :], 0.0, LA[:, q, :], MIN, SUB, e))
                    give(zb[q], tl[q])
                yield
                yield
                tb = []
                for hp in range(2):
                    b = take()
                    m = mms([(PS[b][:, 256 * hh + 128 * q:256 * hh + 128 * q + 128],
                              LB[:, q, 128 * (2 * hp + hh):128 * (2 * hp + hh) + 128], C["decay"], True, True)
                             for hh in range(2) for q in range(2)], PF[b], tl, tcst)
                    e = act(BT[:, 2 * hp:2 * hp + 2, :], PS[b][:, :].rearrange("p (h i) -> p h i", h=2), ACT.Copy, m)
                    give(b, e)
                    tb.append(e)
                r["lb"] = m
                yield
                BC = BT.rearrange("p h (c i) -> p h c i", c=4)
                KM4 = KM.rearrange("p h c (d i) -> p h (c d) i", d=4)
                KC = KT.rearrange("p h (c i) -> p h c i", c=4)
                E1c, E3c = (x.rearrange("p h (c i) -> p h c i", c=4) for x in (E1, E3))
                et = act(ET, BC[:, :, :, 63], ACT.Exp, tb)
                d3 = tt(E3c[:, :, 0:3, :], BC[:, :, 0:3, 63:64].broadcast_to([128, 4, 3, 64]), BC[:, :, 0:3, :], SUB, tb)
                e1 = act(E1, BT, ACT.Exp, tb)
                e3 = act(E3c[:, :, 0:3, :], E3c[:, :, 0:3, :], ACT.Exp, d3)
                yield
                while len(qk) < 4:
                    yield
                tq = tt(QT, QT, E1, MUL, e1, qk)
                e2 = act(E1, BT, ACT.Exp, tq, scale=-1.0)
                yield
                k1 = tt(KM4[:, :, 4:16:5, :], KC[:, :, 0:3, :], E3c[:, :, 0:3, :], MUL, e3, qk)
                k2 = tt(KM[:, :, 2, 0:64], KM[:, :, 1, 0:64], ET[:, :, 1:2].broadcast_to([128, 4, 64]), MUL, k1, et)
                yield
                ki = tt(KM4[:, :, 0:16:5, :], KC, E1c, MUL, e2, tz)
                k3 = tt(KM[:, :, 3, 0:128], KM[:, :, 2, 0:128], ET[:, :, 2:3].broadcast_to([128, 4, 128]), MUL, k2)
                yield
                yield
                for h in range(4):
                    b = take()
                    seq = []
                    for n, (q, kk) in enumerate(((0, 0), (1, 0), (1, 1))):
                        for c in range(2 * q, 2 * q + 2):
                            o = 128 * n + 64 * (c % 2)
                            seq.append((PS[b][:, o:o + 64], KM[:, h, c, 128 * kk:128 * kk + 128],
                                        QT[:, h, 64 * c:64 * c + 64], True, True))
                    m = mms(seq, PF[b], k3, tq, ki)
                    d = tt(PM[:, h, :], PS[b][:, 0:384], C["tri3"], MUL, m)
                    give(b, d)
                    tp.append(d)
                    yield
                r["scores"] = m

            def values():
                for hp in range(2):
                    for t in range(2):
                        b = ob[t, hp] = take()
                        seq = []
                        for h in (2 * hp, 2 * hp + 1):
                            o = PS[b][:, 256 * (h % 2):256 * (h % 2) + 256]
                            v = slice(256 * h, 256 * h + 256)
                            if t == 0:
                                seq += [(o, PM[:, h, 0:128], VV[:, 0, v], True, True)]
                            else:
                                seq += [(o, PM[:, h, 128:256], VV[:, 0, v], True, False),
                                        (o, PM[:, h, 256:384], VV[:, 1, v], False, True)]
                        to[t, hp] = mms(seq, PF[b], tp, list(tv.values()))
                        yield
                yield from head_norm(ob, to, None, YN, res)
                while (0, 1) not in r:
                    yield
                for t in range(2):
                    y, o, e = r[0, t]
                    ty.append(tt(y, y, o, MUL, e, res[t, 0]))

            def sink_qk(n, p, m):
                dst = (QT if n < 2 else KT)[:, 2 * (n % 2):2 * (n % 2) + 2, :]
                e = act(dst, p.rearrange("p (h i) -> p h i", h=2), ACT.Copy, m, scale=128 ** -0.5 if n < 2 else 1.0)
                qk.append(e)
                return (e,)

            def sink_v(n, t, p, m):
                e = act(VV[:, t, 512 * n:512 * n + 512], p, ACT.Copy, m, r["lb"])
                tv[n, t] = e
                return (e,)

            def sink_r(n, t, p, m):
                o = SR[:, t, 512 * n:512 * n + 512]
                e = act(o, p, ACT.Tanh, m, scale=0.5)
                e = stt(o, o, 1.0, p, ADD, MUL, e)
                y = YN[:, t, 512 * n:512 * n + 512]
                r[n, t] = (y, o, e)
                if n == 1:
                    ty.append(tt(y, y, o, MUL, e, res[t, n]))
                return (e,)

            def gate_first():
                drain()
                for g in range(2):
                    turn_heads(g, YN, halfg[:, 0:8], tuple(ty), tO)

            tO = []
            side.append(prepare())
            linear_a(8, 8, tT, sink_qk, tick=advance)
            linear_b(2, 8, tT, sink_v, tick=advance)
            side.append(values())
            linear_b(2, 8, tT, sink_r, tick=lambda: advance(2), last=gate_first)
            tgb = ln_rows(0, 0, LNG, r["scores"])
            tz = mix_out(tO, tX, lambda: [turn_heads(g, YN, halfg[:, 0:8], ty[2:], tO) for g in (2, 3)])
            return tz, tgb, tO

        LNG = ar(12800, 2048)

        def moe(i, tx, tf, free_x):
            nonlocal st
            XG = [T2[:, :].rearrange("p (e k s) -> p e k s", e=4, k=8), ar(4096, 4, 8, 128, dt=F32R)]
            PTR = [ar(8192 + 512 * n, 2, 256, dt=F32R) for n in range(2)]
            GF = [ar(9216 + 256 * n, 256) for n in range(2)]
            G2 = [ar(9728 + 512 * n, 4, 2, 64, dt=F32R) for n in range(2)]
            YH, YL = ar(10752, 1024, dt=F32R), ar(11776, 1024, dt=F32R)
            R1 = [ar(12800 + 512 * n, 512) for n in range(2)]
            R3 = [ar(13824 + 512 * n, 512) for n in range(2)]
            TW = [ar(14848 + 512 * n, 2, 2, 2, 64, dt=F32R) for n in range(2)]
            CMP = ar(9216, 256)
            XH, XL = ar(0, 2, 1024, dt=F32R), ar(2048, 2, 1024, dt=F32R)
            PR = FR[:, :].rearrange("p (t e s) -> p t e s", t=2, e=16)

            tXH = [act(XH[:, q, :], X[:, q, :], ACT.Copy, tx[q], free_x) for q in range(2)]
            tXL = [tt(XL[:, q, :], X[:, q, :], XH[:, q, :], SUB, tXH[q], free_x) for q in range(2)]
            b = take()
            rt = VE["router"].rearrange("p (k e) -> p k e", k=8)
            for g in range(4):
                m = mms([(PS[b][0:16, 0:256], rt[:, k, :], F[:, k, :], k == 0, k == 7) for k in (2 * g, 2 * g + 1)],
                        tf[g], PF[b])
            aff, sel, gate = tiny("m_aff", 32), tiny("m_sel", 32), tiny("m_gate", 32)
            t = act(CMP[0:16, 0:256], PS[b][0:16, 0:256], ACT.Tanh, m, free_x, scale=0.5)
            give(b, t)
            b = take()
            m = mms([(PS[b][:, 16 * q:16 * q + 16], CMP[0:16, 128 * q:128 * q + 128], ident[0:16, 0:16], True, True)
                     for q in range(2)], t, PF[b])
            t_aff = ts(aff, PS[b][:, 0:32], 0.5, 0.5, MUL, ADD, m)
            give(b, t_aff)

            def ranks(v, n, o, more, *after):
                a = v.rearrange("p (g e) -> p g e", e=n)
                shape = [128, more, n, n]
                x4 = CMP[:, 0:more * n * n].rearrange("p (g e f) -> p g e f", e=n, f=n)
                other, own = a.unsqueeze(2).broadcast_to(shape), a.unsqueeze(3).broadcast_to(shape)
                bar = C["bar"].rearrange("p (e f) -> p e f", e=n).unsqueeze(1).broadcast_to(shape)
                t = tt(x4, other, own, SUB, *after)
                t = tt(x4, x4, bar, ALU.is_gt, t)
                return red(o.rearrange("p (g e) -> p g e", e=n), x4, ADD, t)

            rk, gs, gk = tiny("m_rk", 32), tiny("m_gs", 8), tiny("m_gk", 8)
            t = ranks(aff, 4, rk, 8, t_aff)
            t = ts(sel, rk, 2.0, None, ALU.is_lt, NOP, t)
            t = tt(gate, aff, sel, MUL, t)
            t = red(gs, gate.rearrange("p (g e) -> p g e", e=4), ADD, t)
            t = ranks(gs, 4, gk, 2, t)
            t = ts(gk, gk, 1.0, None, ALU.is_lt, NOP, t)
            own = gk.unsqueeze(2).broadcast_to([128, 8, 4])
            t_sel = tt(sel.rearrange("p (g e) -> p g e", e=4), sel.rearrange("p (g e) -> p g e", e=4), own, MUL, t)
            b, bm = take(), take()
            m = mms([(PS[b][:, 0:16], C["before"], sel[:, 0:16], True, True),
                     (PS[b][:, 16:32], C["ones"], sel[:, 0:16], True, False),
                     (PS[b][:, 16:32], C["before"], sel[:, 16:32], False, True)], PF[b], t_sel)
            mc = mms([(PS[bm][:, 0:16], C["ones"], sel[:, 0:16], True, False),
                      (PS[bm][:, 0:16], C["ones"], sel[:, 16:32], False, True)], PF[bm])
            pm, most = tiny("m_pm", 32), tiny("m_most", 1)
            t_pm = stt(pm, PS[b][:, 0:32], 1.0, sel, ADD, MUL, m)
            give(b, t_pm)

            def one_hot(g, *after):
                return [tt(PR[:, q, 4 * g:4 * g + 4, :], C["slots"].unsqueeze(1).broadcast_to([128, 4, 64]),
                           pm[:, 16 * q + 4 * g:16 * q + 4 * g + 4].unsqueeze(2).broadcast_to([128, 4, 64]), ALU.is_equal,
                           *after) for q in range(2)]

            tP = {0: one_hot(0, t_pm)}
            t = red(most, PS[bm][:, 0:16], MAX, mc)
            give(bm, t)
            t_flag = ts(FLAG[0:1, i:i + 1], most[0:1, :], 64.0, None, ALU.is_gt, NOP, t)
            parts[i] = {n: Part(f"full{i}_{n}", FLAG[0:1, i:i + 1], (t_flag,))
                        for n in ("sync", "act", "dve", "pool", "pe")}
            tP.update({g: one_hot(g, t_pm) for g in range(1, 4)})
            t = tt(gate.rearrange("p (g e) -> p g e", e=4), gate.rearrange("p (g e) -> p g e", e=4), own, MUL, t_sel)
            den = tiny("m_den", 2)
            t = red(den, gate.rearrange("p (t e) -> p t e", t=2), ADD, t)
            t = inv(den, den, t)
            t_gate = tt(gate.rearrange("p (t e) -> p t e", t=2), gate.rearrange("p (t e) -> p t e", t=2),
                        den.unsqueeze(2).broadcast_to([128, 2, 16]), MUL, t)
            GS = tiny("m_gs16", 16)

            pinned = [take() for _ in range(4)]
            YB = {(t, n): pinned[2 * t + n] for t in range(2) for n in range(2)}
            tA, tT, tC, tS, tG, tY = {}, {}, {}, {}, {}, {}
            tXG, tPT, tTW, tSM, tM = {}, {}, {}, {}, {}

            def gather(g, j):
                t = []
                for k in (2 * j, 2 * j + 1):
                    b = take()
                    m = mms([(PS[b][:, 256 * hl:256 * hl + 256], src[:, q, 128 * k:128 * k + 128],
                              PR[:, q, 4 * g:4 * g + 4, :], q == 0, q == 1)
                             for hl, src in enumerate((XH, XL)) for q in range(2)], PF[b], tP[g], tXL)
                    o = XG[g % 2][:, :, k, :].rearrange("p e (h s) -> p h e s", h=2)
                    src = PS[b][:, :].rearrange("p (h e s) -> p h e s", h=2, e=4)
                    ok = tA[4 * g - 5] if g >= 2 else ()
                    t.append(cp(o, src, m, ok) if g == 0 and k % 2 else act(o, src, ACT.Copy, m, ok))
                    give(b, t[-1])
                tXG[g, j] = tuple(t)

            def double(e):
                for q in range(2):
                    o = TW[e // 2 % 2][:, q, :, :, :]
                    s = PR[:, q, e:e + 2, :].unsqueeze(2).broadcast_to([128, 2, 2, 64])
                    t = G(lambda en, o=o, s=s: en.tensor_copy(o, s), tP[e // 4], tx, tPT.get(e - 3, ()))
                tTW[e] = tTW[e + 1] = t

            def twice(e, q):
                return TW[e // 2 % 2][:, q, e % 2, :, :].rearrange("p d s -> p (d s)")

            def scatter_maps(e):
                b, bg = take(), take()
                m = mms([(PS[b][:, 256 * d + 128 * q:256 * d + 128 * q + 128], twice(e + d, q), IDR[:, :], True, True)
                         for d in range(2) for q in range(2)], PF[b], tTW[e], ready["idr"])
                mg = mms([(PS[bg][:, d:d + 1], twice(e + d, q).bitcast(F32),
                           gate[:, 16 * q + e + d:16 * q + e + d + 1], q == 0, q == 1)
                          for d in range(2) for q in range(2)], PF[bg], t_gate)
                t = act(PTR[e // 2 % 2], PS[b][:, :].rearrange("p (d i) -> p d i", d=2), ACT.Copy, m,
                        tS.get(e - 3, ()))
                tg = act(GS[:, e:e + 2], PS[bg][:, 0:2], ACT.Copy, mg)
                give(b, t)
                give(bg, tg)
                tPT[e] = tPT[e + 1] = mg
                tSM[e] = tSM[e + 1] = (t, tg)

            def product(o, x, h, l, first, last):
                if l is None:
                    return [(o, x.bitcast(F32), h, first, last)]
                return [(o, x, h, first, False), (o, x, l, False, last)]

            def up(e):
                tok2 = []
                for r in (R1, R3):
                    b = take()
                    for uu in range(4):
                        u, h, l, tok = unit()
                        seq = []
                        for j in range(2):
                            k = 2 * uu + j
                            w = slice(512 * j, 512 * j + 512)
                            seq += product(PS[b][:, :], XG[e // 4 % 2][:, e % 4, k, :], h[:, w], None if l is None else l[:, w],
                                           k == 0, k == 7)
                        if e == 0 and r is R1 and uu < 3:
                            gather(0, uu + 1)
                        m = mms(seq, tok, tXG[e // 4, uu], PF[b] if uu == 0 else ())
                        used(u, m)
                    t = act(r[e % 2], PS[b][:, :], ACT.Copy, m, tT.get(e - 2, ()), t_gate, tx)
                    give(b, t)
                    tok2.append(t)
                tA[e] = m
                return tok2

            def act_mul(e, tok2):
                b = take()
                m = mms([(PS[b][:, 256 * w + 64 * f:256 * w + 64 * f + 64], r[e % 2][:, 128 * f:128 * f + 128],
                          C["fold"], True, True) for w, r in enumerate((R1, R3)) for f in range(4)], PF[b], tok2)
                tT[e] = m
                gf = GF[e % 2]
                t = act(gf, PS[b][:, 0:256], ACT.Tanh, m, tG.get(e - 2, ()), scale=0.5)
                t = stt(gf, gf, 1.0, PS[b][:, 0:256], ADD, MUL, t)
                t = stt(gf, gf, 0.5, PS[b][:, 256:512], MUL, MUL, t)
                give(b, t)
                g3 = gf.rearrange("p (f s) -> p f s", f=4)
                th = act(G2[e % 2][:, :, 0, :], g3, ACT.Copy, t, tC.get(e - 2, ()))
                tG[e] = tt(G2[e % 2][:, :, 1, :], g3, G2[e % 2][:, :, 0, :], SUB, th)

            def down(e):
                tY[e] = []
                for n in range(2):
                    b = take()
                    for uu in range(2):
                        u, h, l, tok = unit()
                        seq = []
                        for j in range(2):
                            k = 2 * uu + j
                            w = slice(512 * j, 512 * j + 512)
                            seq += product(PS[b][:, :], G2[e % 2][:, k, :, :].rearrange("p h s -> p (h s)"), h[:, w],
                                           None if l is None else l[:, w], k == 0, k == 3)
                        m = mms(seq, tok, tG[e], PF[b] if uu == 0 else ())
                        used(u, m)
                    yh, yl = YH[:, 512 * n:512 * n + 512], YL[:, 512 * n:512 * n + 512]
                    t = act(yh, PS[b][:, :], ACT.Copy, m, tSM[e][1], tS.get(e - 1, ()), scale=GS[:, e:e + 1])
                    t = stt(yl, PS[b][:, :], GS[:, e:e + 1], yh, MUL, SUB, t)
                    give(b, t)
                    tY[e].append(t)
                tC[e] = m

            def scatter(e):
                for n in range(2):
                    seq = []
                    for t in range(2):
                        w = PTR[e // 2 % 2][:, e % 2, 128 * t:128 * t + 128]
                        o = PS[YB[t, n]][:, :]
                        seq += [(o, w, YH[:, 512 * n:512 * n + 512], first and e == 0, False),
                                (o, w, YL[:, 512 * n:512 * n + 512], False, e == 15)]
                    tS[e] = mms(seq, tY[e][n], tSM[e][0], [PF[p] for p in pinned] if first and e == 0 else ())
                    tM[n] = tS[e]

            def experts():
                gather(0, 0)
                double(0)
                for e in range(16):
                    tok2 = up(e)
                    if e % 2 == 0:
                        scatter_maps(e)
                        if e + 2 < 16:
                            double(e + 2)
                    if e:
                        down(e - 1)
                    act_mul(e, tok2)
                    if e:
                        scatter(e - 1)
                    if e < 12:
                        gather(e // 4 + 1, e % 4)
                down(15)
                scatter(15)

            first = True
            experts()
            first = False
            t_main, t_up, t_fold = dict(tM), tA[15], tT[15]

            queues = {"sync": Y, "act": S, "dve": V, "pool": G, "pe": P}
            now = [(q.sem, q.n) for q in (P, S, V, G)]
            main, banks, order = st, list(PF), list(free)
            PF[:] = [()] * 8
            for n, q in queues.items():
                q.enter(sem(f"s_x{i}_{n}"))
            for n, q in queues.items():
                q.bare(lambda e: e.nop(), now)
            st = stream(3 * small["moe"][i], [sem(f"s_x{i}_raw{n}") for n in range(NR)], {})
            for _ in range(NR):
                issue()
            for _ in range(3):
                for d in (tA, tT, tC, tS, tG, tY, tXG, tPT, tTW, tSM):
                    d.clear()
                done = [(q.sem, q.n) for q in (P, S, V, G) if q.n]
                t = ts(pm, pm, 64.0, None, SUB, NOP, done)
                tP = {g: one_hot(g, t, done) for g in range(4)}
                experts()
            done = [(q.sem, q.n) for q in (P, S, V, G)]
            for n, q in queues.items():
                q.bare(lambda e: e.nop(), done)
                part = parts[i][n]
                part.sem, part.items = q.leave()
                if n != "sync":
                    q.items.append(part)
            st, PF[:], free[:] = main, banks, order
            st["stops"] = {c: n for c, n in st["stops"].items() if n != i}
            tgb = ln_rows(i, 1, LNG, t_fold, t_main[1])
            tz = []
            for n in range(2):
                for t in range(2):
                    z = X[:, t, 512 * n:512 * n + 512]
                    e = stt(z, z, ALPHA, PS[YB[t, n]][:, :], MUL, ADD, t_main[n])
                    give(YB[t, n], e)
                    tz.append(ln_piece(t, n, e))
            return tz, tgb, t_up

        def mlstm(tx, tT, rest):
            CV, VV, SO = ar(0, 16, 256), ar(4096, 2, 1024), ar(6144, 2, 1024)
            PT, W = ar(8192, 4, 384), ar(9728, 4, 384)
            YN = ar(11264, 2, 1024)
            TQ = ar(6144, 2, 512)
            RO = [ar(7168 + 256 * n, 256) for n in range(2)]
            GB = ar(15104, 2048)
            tcv, tw, tv, ty, res, r = {}, [], {}, [], {}, {}
            tO = []
            em = tiny("l_em", 8, 2)

            def gates():
                yield
                b = take()
                mg = VE["mgate"].rearrange("p (k e) -> p k e", k=8)
                m = mms([(PS[b][0:8, 0:256], mg[:, k, :], F[:, k, :], k == 0, k == 7) for k in range(8)], PF[b], tT)
                t = act(RO[1][0:8, :], PS[b][0:8, 0:256], ACT.Identity, m, bias=VE["mbias"][0:8, :])
                give(b, t)
                yield
                b = take()
                m = mms([(PS[b][:, 8 * q_:8 * q_ + 8], RO[1][0:8, 128 * q_:128 * q_ + 128], ident[0:8, 0:8], True, True)
                         for q_ in range(2)], PF[b], t)
                gt = PS[b][:, 0:16].rearrange("p (t g) -> p t g", t=2)
                fg, it, th, z, q, lf = (tiny(f"l_{n}", 8, 2) for n in ("fg", "it", "th", "z", "q", "lf"))
                t = cp(fg, gt[:, :, 4:8], m)
                ti = cp(it, gt[:, :, 0:4], m)
                give(b, ti)
                yield
                t = stt(th, fg, -1.0, fg, MUL, MAX, t)
                t = act(th, th, ACT.Tanh, t, scale=0.5)
                t1 = ts(z, th, 3.0, None, ADD, NOP, t)
                t1 = inv(z, z, t1)
                t = ts(th, th, -1.0, 1.0, MUL, ADD, t, t1)
                t = tt(th, th, z, MUL, t, t1)
                t = tt(z, th, th, MUL, t)
                yield
                t = ts(q, z, 1.0 / 17.0, None, MUL, NOP, t)
                for n in (15, 13, 11, 9, 7, 5, 3):
                    t = stt(q, q, 1.0 / n, z, ADD, MUL, t)
                t = stt(q, q, 1.0, th, ADD, MUL, t)
                t = ts(q, q, -2.0, None, MUL, NOP, t)
                t = stt(lf, fg, 0.0, q, MIN, ADD, t)
                yield
                yield
                causal = C["tri3"][:, 0:128]
                b = take()
                m = mms([(PS[b][:, 0:4], causal, lf[:, 0, :], True, True),
                         (PS[b][:, 4:8], C["ones"], lf[:, 0, :], True, False),
                         (PS[b][:, 4:8], causal, lf[:, 1, :], False, True)], PF[b], t)
                bc, aj = tiny("l_bc", 8, 2), tiny("l_aj", 8, 2)
                t = cp(bc, PS[b][:, 0:8].rearrange("p (t h) -> p t h", t=2), m)
                give(b, t)
                t_aj = tt(aj, it, bc, SUB, t, ti)
                yield
                b = take()
                m = turns([(PS[b][0:4, 128 * q_:128 * q_ + 128], aj[:, q_, :]) for q_ in range(2)], PF[b], t_aj)
                t = cp(RO[0][0:4, :], PS[b][0:4, 0:256], m)
                give(b, t)
                yield
                cur = 0
                for sh in (1, 2, 4, 8, 16, 32, 64, 128):
                    a, o = RO[cur][0:4, :], RO[1 - cur][0:4, :]
                    t1 = cp(o[:, 0:sh], a[:, 0:sh], t)
                    t2 = tt(o[:, sh:256], a[:, sh:256], a[:, 0:256 - sh], MAX, t)
                    t = (t1, t2)
                    cur = 1 - cur
                    if sh in (4, 32):
                        yield
                MR = RO[cur]
                yield
                yield
                b = take()
                m = mms([(PS[b][:, 4 * q_:4 * q_ + 4], MR[0:4, 128 * q_:128 * q_ + 128], ident[0:4, 0:4], True, True)
                         for q_ in range(2)], PF[b], t)
                t2 = tt(em, bc, PS[b][:, 0:8].rearrange("p (t h) -> p t h", t=2), ADD, m)
                give(b, t2)
                r["em"] = act(em, em, ACT.Exp, t2, scale=-1.0)
                tp = []
                for hp in range(2):
                    b = take()
                    m = mms([(PS[b][:, 256 * hh:256 * hh + 256],
                              ident[0:4, 2 * hp + hh:2 * hp + hh + 1].broadcast_to([4, 128]),
                              MR[0:4, :], True, True) for hh in range(2)], PF[b], t)
                    for hh in range(2):
                        h = 2 * hp + hh
                        p = PS[b][:, 256 * hh:256 * hh + 256]
                        tp.append(ts(PT[:, h, 0:256], p, aj[:, 0, h:h + 1], 0.0, SUB, MAX, m, t_aj))
                        tp.append(ts(PT[:, h, 256:384], p[:, 128:256], aj[:, 1, h:h + 1], 0.0, SUB, MAX, m, t_aj))
                    give(b, tp[-1])
                    yield
                t = act(PT, PT, ACT.Exp, tp, scale=-1.0)
                yield
                r["pt"] = tt(PT, PT, C["tri3"].unsqueeze(1).broadcast_to([128, 4, 384]), MUL, t)
                yield

            cw = VE["conv_w"].rearrange("p (j m) -> p j m", j=4)
            cb = VE["conv_b"]

            def sink_qk(n, p, m):
                tk = []
                for i in range(2):
                    mt = 2 * n + i
                    tk.append(act(CV[:, mt, :], p[:, 256 * i:256 * i + 256], ACT.Identity, m,
                                  scale=cw[:, 3, mt:mt + 1], bias=cb[:, mt:mt + 1]))
                tk = [tk[1], tk[1]]
                for j in (1, 2, 3):
                    for i in range(2):
                        mt = 2 * n + i
                        o = CV[:, mt, j:256]
                        tk[i] = stt(o, p[:, 256 * i:256 * i + 256 - j], cw[:, 3 - j, mt:mt + 1], o, MUL, ADD, tk[i])
                c2 = CV[:, 2 * n:2 * n + 2, :]
                q2 = TQ[:, n % 2, :].rearrange("p (i j) -> p i j", i=2)
                t = act(q2, c2, ACT.Tanh, tk, tcv.get(n - 2, ()), scale=0.5)
                tcv[n] = stt(c2, q2, 1.0, c2, ADD, MUL, t)
                return (tk[1],)

            def scores():
                for h in range(4):
                    while 2 * h + 1 not in tcv:
                        yield
                    yield
                    b = take()
                    seq = []
                    for o, w, js in ((0, 256, slice(0, 128)), (256, 128, slice(128, 256))):
                        for kk in range(2):
                            seq.append((PS[b][:, o:o + w], CV[:, 4 * h + 2 + kk, js], CV[:, 4 * h + kk, 256 - w:256],
                                        kk == 0, kk == 1))
                    m = mms(seq, PF[b], tcv[2 * h], tcv[2 * h + 1])
                    d = stt(W[:, h, :], PS[b][:, 0:384], 1.0 / 64.0, PT[:, h, :], MUL, MUL, m, r["pt"])
                    give(b, d)
                    tw.append(d)
                    yield
                r["cv"] = m

            def values():
                ob, to = {}, {}
                bd = take()
                td = []
                one = C["ones"][:, 0:1]
                for hp in range(2):
                    for t in range(2):
                        b = ob[t, hp] = take()
                        seq, den = [], []
                        for h in (2 * hp, 2 * hp + 1):
                            o = PS[b][:, 256 * (h % 2):256 * (h % 2) + 256]
                            d = PS[bd][:, 4 * t + h:4 * t + h + 1]
                            v = slice(256 * h, 256 * h + 256)
                            if t == 0:
                                seq += [(o, W[:, h, 0:128], VV[:, 0, v], True, True)]
                                den += [(d, W[:, h, 0:128], one, True, True)]
                            else:
                                seq += [(o, W[:, h, 128:256], VV[:, 0, v], True, False),
                                        (o, W[:, h, 256:384], VV[:, 1, v], False, True)]
                                den += [(d, W[:, h, 128:256], one, True, False), (d, W[:, h, 256:384], one, False, True)]
                        td.append(mms(den, PF[bd], tw))
                        to[t, hp] = mms(seq, PF[b], tw, list(tv.values()))
                        next(rest)
                        yield
                ab, rd = tiny("l_ab", 8), tiny("l_rd", 8)
                t = cp(ab, PS[bd][:, 0:8], td[-1], tx)
                give(bd, t)
                t = stt(ab, ab, -1.0, ab, MUL, MAX, t)
                t = tt(ab, ab, em.rearrange("p t h -> p (t h)"), MAX, t, r["em"])
                t = inv(rd, ab, t)
                yield
                yield from head_norm(ob, to, (rd, t), YN, res)
                while (0, 1) not in r:
                    yield
                for t in range(2):
                    y, o, e = r[0, t]
                    ty.append(stt(y, o, 1.0, y, ADD, MUL, e, res[t, 0]))

            def sink_v(n, t, p, m):
                e = act(VV[:, t, 512 * n:512 * n + 512], p, ACT.Copy, m)
                tv[n, t] = e
                return (e,)

            def sink_o(n, t, p, m):
                o = SO[:, t, 512 * n:512 * n + 512]
                e = act(o, p, ACT.Tanh, m, scale=0.5)
                y = YN[:, t, 512 * n:512 * n + 512]
                r[n, t] = (y, o, e)
                if n == 1:
                    ty.append(stt(y, o, 1.0, y, ADD, MUL, e, res[t, n]))
                return (e,)

            def gate_first():
                drain()
                for g in range(2):
                    turn_heads(g, YN, halfg[:, 8:16], tuple(ty), tO)

            side.append(gates())
            linear_b(2, 8, tT, sink_v, tick=advance)
            side.append(scores())
            linear_a(16, 8, tT, sink_qk, tick=advance)
            side.append(values())
            tgb = ln_rows(1, 0, GB)
            linear_b(2, 8, tT, sink_o, tick=lambda: advance(3), last=gate_first)
            tz = mix_out(tO, tx, lambda: [turn_heads(g, YN, halfg[:, 8:16], ty[2:], tO) for g in (2, 3)])
            return tz, tgb, GB, tO

        def block2(l, tx, prior, tsq):
            QK = ar(0, 17, 256)
            VB = ar(4352, 2, 896)
            ST = [ar(6144 + 1024 * n, 2, 512) for n in range(2)]
            RT = [ar(8192 + 1024 * n, 2, 512) for n in range(2)]
            BB = ar(10240, 2, 512)
            GA = ar(11264, 16, 256)
            TG = ar(15360, 8, 2, 2, 64)
            TB, GN = ar(11264, 2, 2, 2, 64), ar(11264 + 512, 8, 2, 64)
            spots = [ar(6144 + 512 * n, 2, 256) for n in range(10)] + [ar(15360 + 512 * n, 2, 256) for n in range(4)]
            PB, PTT = spots[0:8], spots[8:14]
            FF = F[:, :, :].rearrange("p a b -> p (a b)")
            MK = FF[:, 0:1536].rearrange("p (g i) -> p g i", g=3)
            DG = FF[:, 1536:2048].rearrange("p (j i) -> p j i", j=4)
            OH, OL = ar(1280, 6, 256, dt=F32R), ar(2816, 6, 256, dt=F32R)
            MH, ML = TH, TL
            GT = ar(15360, 2, 1024)
            ZT = [ar(6144 + 512 * n, 512) for n in range(4)]
            XN = ar(8192, 2, 1024)
            RR = [ar(512 * n, 512) for n in range(2)]
            RH = [ar(1024 + 512 * n, 2, 256, dt=F32R) for n in range(2)]
            RL = [ar(2048 + 512 * n, 2, 256, dt=F32R) for n in range(2)]
            SQ = [ar(13312 + 1024 * n, 2, 512) for n in range(2)]
            ada = ADA[:, l, :]

            def rms_T(gcol, sc, sh, name, tsq, deps, wait):
                ss, rs, scg = tiny("b_ss", 2), tiny("b_rs", 2), tiny("b_scg", 8)
                t = tt(ss, SSP[:, :, 0], SSP[:, :, 1], ADD, tsq)
                t = ts(ss, ss, 1.0 / 1024.0, 1e-6, MUL, ADD, t)
                t = rsqrt(rs, ss, 2, "b_nr", t)
                xn = [ts(XN[:, 0, :], X[:, 0, :], rs[:, 0:1], None, MUL, NOP, t, wait),
                      act(XN[:, 1, :], X[:, 1, :], ACT.Copy, t, wait, scale=rs[:, 1:2])]
                t_s = stt(scg, sc, 1.0, gcol, ADD, MUL, deps)
                ahead(3)
                return transposed(XN, (xn, t_s), scg, sh, True, wait)

            tT, m_last = rms_T(VE["g_mix"][:, 8 * l:8 * l + 8], ada[:, 8:16], ada[:, 0:8], "b1", tsq,
                               (ada_tok[l, 0],), prior)

            t1 = gload(TB, D["rope"].rearrange("p (a b c d) -> p a b c d", a=2, b=2, c=2), prior)
            t2 = gload(GN[0:1, :, :, :], D["gains"][l:l + 1, :].rearrange("p (a b c) -> p a b c", a=8, b=2), prior)
            gflat = GN.rearrange("p a b c -> p (a b c)")
            t2 = G(lambda e: e.partition_broadcast(gflat, gflat[0:1, :]), t2)
            t_tab = []
            for kind in range(8):
                t_tab.append(tt(TG[:, kind, :, :, :], TB[:, 0 if kind < 2 else 1, :, :, :],
                                GN[:, kind, :, :].unsqueeze(2).broadcast_to([128, 2, 2, 64]), MUL, t1, t2, prior, q=G))
            t_mask = gload(MK, D["masks"].rearrange("p (g i) -> p g i", g=3), tT)

            segs = [([(0, 8, 0)], []), ([(0, 2, 1), (128, 4, 2)], [(384, 2, 0)]), ([(0, 4, 3)], [(256, 4, 128)]),
                    ([(0, 4, 4), (256, 4, 5)], []), ([(0, 4, 7)], [(256, 4, 384)]), ([(0, 4, 6)], [(256, 4, 640)])]
            t_qk, t_v, raws = {}, [], {}
            t_free = {"ST": [prior, prior], "RT": [prior, prior], "BB": prior, "SQ": [prior, prior]}
            npair, pending, LAG = [0], [], 2

            def sink_qkv(n, t, p, m):
                qk, vs = segs[n]
                w = sum(h for _, h, _ in qk) * 64
                par = n % 2
                for c, h, o in vs:
                    t_v.append(act(VB[:, t, o:o + 64 * h], p[:, c:c + 64 * h], ACT.Copy, m, prior))
                e = [act(ST[par][:, t, 0:w], p[:, 0:w], ACT.Copy, m, t_free["ST"][par]),
                     act(SQ[par][:, t, 0:w], p[:, 0:w], ACT.Square, m, t_free["SQ"][par])]
                raws.setdefault(n, []).extend(e)
                if t == 1:
                    side.append(rope(n))
                return (e[-1],)

            def rope(n):
                qk, _ = segs[n]
                nh = sum(h for _, h, _ in qk)
                w = nh * 64
                par = n % 2
                sv, rv = tiny(f"b_sv{par}", 16)[:, 0:2 * nh], tiny(f"b_rv{par}", 16)[:, 0:2 * nh]
                t = red(sv.rearrange("p (t h) -> p t h", t=2), SQ[par][:, :, 0:w].rearrange("p t (h d) -> p t h d", d=64),
                        ADD, raws[n])
                t_free["SQ"][par] = t
                t = ts(sv, sv, 1.0 / 64.0, 1e-6, MUL, ADD, t)
                yield
                t = rsqrt(rv, sv, 2 * nh, tiny(f"b_rn{par}", 32), t)
                yield
                x = ST[par][:, :, 0:w].rearrange("p t (h d) -> p t h d", d=64)
                t = tt(x, x, rv.rearrange("p (t h) -> p t h", t=2).unsqueeze(3).broadcast_to([128, 2, nh, 64]), MUL, t)
                yield
                done = []
                for c, h, kind in qk:
                    xx, rr, bb = (z[:, :, c:c + 64 * h] for z in (ST[par], RT[par], BB))
                    cg = TG[:, kind, 0, :, :].unsqueeze(2).broadcast_to([128, 2, h, 64])
                    done.append(tt(rr.rearrange("p q (h d) -> p q h d", d=64), xx.rearrange("p q (h d) -> p q h d", d=64),
                                   cg, MUL, t, t_tab, t_free["RT"][par]))
                    b = 2 if kind < 2 else 1
                    w_ = 32 // b
                    for s_ in range(2):
                        for i in range(b):
                            at = 2 * w_ * i
                            o, x_ = (z.rearrange("p q (h d) -> p q h d", d=64) for z in (bb, xx))
                            sg = TG[:, kind, 1, :, at + w_ * s_:at + w_ * s_ + w_].unsqueeze(2).broadcast_to([128, 2, h, w_])
                            done.append(tt(o[:, :, :, at + w_ * s_:at + w_ * s_ + w_],
                                           x_[:, :, :, at + w_ * (1 - s_):at + w_ * (1 - s_) + w_], sg,
                                           MUL, t, t_tab, t_free["BB"]))
                    yield
                t_free["ST"][par] = done[-1]
                t = tt(RT[par][:, :, 0:w], RT[par][:, :, 0:w], BB[:, :, 0:w], ADD, done)
                t_free["BB"] = t
                np_ = nh // 2
                sums.append([LAG, lambda: turn(npair[0], np_, par, t)])
                pending.append(n)
                yield

            def turn(first, np_, par, t):
                for p0 in range(0, np_, 2):
                    cnt = min(2, np_ - p0)
                    b = take()
                    m = turns([(PS[b][:, 256 * i + 128 * q:256 * i + 128 * q + 128],
                                RT[par][:, q, 128 * (p0 + i):128 * (p0 + i) + 128]) for i in range(cnt) for q in range(2)],
                              PF[b], t)
                    e = act(QK[:, first + p0:first + p0 + cnt, :],
                            PS[b][:, 0:256 * cnt].rearrange("p (k i) -> p k i", k=cnt), ACT.Copy, m, prior)
                    give(b, e)
                    for i in range(cnt):
                        t_qk[first + p0 + i] = e
                npair[0] = first + np_
                t_free["RT"][par] = m
                pending.pop(0)

            linear_b(6, 8, tT, sink_qkv, tick=lambda: advance(2))

            SC, D1, D2 = 64 ** -0.5, 5, 7
            heads = [("b", p, s_) for p in range(2) for s_ in range(2)] + [("a", p, s_) for p in range(4) for s_ in range(2)]
            QP, KP = [5, 9, 15], [7, 11, 13]
            tP_free, tT_free = [()] * 8, [()] * 6
            tmx, tO, hold = [(), ()], [], {}
            tga = []
            sets = []
            for i, (kind, p, s_) in enumerate(heads):
                if kind == "a":
                    sets.append((i, 0, 1, p, 4, s_ * 64, None))
                else:
                    sets += [(i, g, 3, QP[g] + p, KP[g] + p, 128 + 256 * g + 64 * (2 * p + s_), g) for g in range(3)]
            soft, pt_tok, bank_of = {}, {}, {}

            def attention():
                while pending:
                    yield
                t_rt = (t_free["RT"], t_free["ST"], t_free["BB"], t_tab)
                tP_free[:] = [t_rt] * 8
                tT_free[:] = [t_rt] * 6
                for j in range(len(sets) + D2):
                    if j < len(sets):
                        score(j)
                        yield
                    if 0 <= j - D1 < len(sets):
                        probs_T(j - D1)
                        yield
                    if j - D2 >= 0:
                        value(j - D2)
                        yield

            def spread(which, dg, after, ready):
                sec = (2, 5)[which]
                while (l, 1 + which) not in ada_tok:
                    yield
                for n in range(2):
                    td = [ts(dg[:, j, :], ident, ada[:, 8 * sec + 4 * n + j:8 * sec + 4 * n + j + 1], None, MUL, NOP,
                             ada_tok[l, 1 + which], after) for j in range(4)]
                    yield
                    b = take()
                    m = after = hold["dg", which] = mms([(PS[b][:, 128 * j:128 * j + 128], C["ones"], dg[:, j, :], True, True)
                                                         for j in range(4)], PF[b], td)
                    e = act(GT[:, which, 512 * n:512 * n + 512], PS[b][:, :], ACT.Copy, m, ready)
                    give(b, e)
                    hold["gt", which, n] = e
                    yield

            def score(j):
                i, n, cnt, qp, kp, vo, g = sets[j]
                kind, p, s_ = heads[i]
                rows = slice(64 * s_, 64 * s_ + 64)
                mx, sm = tiny(f"b_mx{i % 2}", 8), tiny(f"b_sm{i % 2}", 8)
                pb = PB[j % 8]
                b = bank_of[j] = take()
                m = mms([(PS[b][:, 256 * q:256 * q + 256], QK[rows, qp, 128 * q:128 * q + 128], QK[rows, kp, :], True, True)
                         for q in range(2)], PF[b], t_qk[qp], t_qk[kp])
                if kind == "a":
                    t = red(mx[:, 0:2], PS[b][:, :].rearrange("p (q k) -> p q k", q=2), MAX, m, tmx[i % 2])
                else:
                    for q in range(2):
                        t = V(lambda e, q=q: e.tensor_tensor_reduce(
                            pb[:, q, :], PS[b][:, 256 * q:256 * q + 256], MK[:, g, 256 * q:256 * q + 256],
                            1.0, -3e38, ADD, MAX, mx[:, 2 + 2 * n + q:3 + 2 * n + q]), m, tmx[i % 2], t_mask, tP_free[j % 8])
                    give(b, t)
                    if n < 2:
                        return
                    t = red(mx[:, 0:2], mx[:, 2:8].rearrange("p (g q) -> p q g", q=2), MAX, t)
                t = ts(mx[:, 0:2], mx[:, 0:2], -SC, None, MUL, NOP, t)
                te = []
                for k in range(cnt):
                    jj = j - cnt + 1 + k
                    for q in range(2):
                        o = PB[jj % 8][:, q, :]
                        src = PS[b][:, 256 * q:256 * q + 256] if kind == "a" else o
                        te.append(act(o, src, ACT.Exp, t, tP_free[jj % 8], scale=SC, bias=mx[:, q:q + 1],
                                      accum_out=sm[:, 2 + 2 * k + q:3 + 2 * k + q]))
                if kind == "a":
                    give(b, te[-1])
                    t = inv(sm[:, 0:2], sm[:, 2:4], te)
                else:
                    t = red(sm[:, 0:2], sm[:, 2:8].rearrange("p (g q) -> p q g", q=2), ADD, te)
                    t = inv(sm[:, 0:2], sm[:, 0:2], t)
                for k in range(cnt):
                    jj = j - cnt + 1 + k
                    soft[jj] = [ts(PB[jj % 8][:, q, :], PB[jj % 8][:, q, :], sm[:, q:q + 1], None, MUL, NOP, t)
                                for q in range(2)]
                tmx[i % 2] = soft[j][1]

            def probs_T(j):
                b = take()
                m = turns([(PS[b][:, 256 * k + 128 * q:256 * k + 128 * q + 128], PB[j % 8][:, q, 128 * k:128 * k + 128])
                           for q in range(2) for k in range(2)], PF[b], soft[j])
                tP_free[j % 8] = m
                pt_tok[j] = act(PTT[j % 6], PS[b][:, :].rearrange("p (k i) -> p k i", k=2), ACT.Copy, m, tT_free[j % 6])
                give(b, pt_tok[j])

            def value(j):
                i, n, cnt, qp, kp, vo, g = sets[j]
                kind, p, s_ = heads[i]
                rows = slice(64 * s_, 64 * s_ + 64)
                if s_ == 0 and n == 0:
                    hold["b", i // 2] = take()
                b = hold["b", i // 2]
                m = mms([(PS[b][rows, 0:256], VB[:, k, vo:vo + 64], PTT[j % 6][:, k, :], n == 0 and k == 0,
                          n == cnt - 1 and k == 1) for k in range(2)],
                        PF[b] if s_ == 0 and n == 0 else (), pt_tok[j], t_v)
                tT_free[j % 6] = m
                if s_ == 1 and n == cnt - 1:
                    tile = p if kind == "a" else 4 + p
                    th = act(OH[:, tile, :], PS[b][:, 0:256], ACT.Copy, m)
                    tl = tt(OL[:, tile, :], PS[b][:, 0:256], OH[:, tile, :], SUB, th)
                    give(b, tl)
                    tO.append(tl)

            def sink_gate(n, p, m):
                e = act(GA[:, 2 * n:2 * n + 2, :], p.rearrange("p (k i) -> p k i", k=2), ACT.Tanh, m, t_tab, tuple(t_free["SQ"]), scale=0.5)
                tga.append(e)
                return (e,)

            side.append(attention())
            linear_a(16, 8, tT, sink_gate, tick=lambda: advance(4))
            drain()
            t_att = (tO, tP_free, tT_free)

            tu = []

            def sink_a(n, p, m):
                g = GA[:, 2 * n:2 * n + 2, :]
                e = stt(g, g, 1.0, p.rearrange("p (k i) -> p k i", k=2), ADD, MUL, m, tga)
                tu.append(e)
                return (e,)

            side.append(spread(0, DG, tT, (tP_free, tT_free)))
            linear_a(8, 4, [tO] * 2, sink_a, OH, OL, tick=advance)
            tm = []

            def sink_b(n, p, m):
                g, a = GA[:, 8 + 2 * n:10 + 2 * n, :], GA[:, 2 * n:2 * n + 2, :]
                e0 = stt(g, g, 1.0, p.rearrange("p (k i) -> p k i", k=2), ADD, MUL, m, tga)
                e = tt(g, g, a, ADD, e0, tu[n])
                th = act(MH[:, 2 * n:2 * n + 2, :], g, ACT.Copy, e, scale=0.5)
                tm.append(stt(ML[:, 2 * n:2 * n + 2, :], g, 0.5, MH[:, 2 * n:2 * n + 2, :], MUL, SUB, th))
                return (e0,)

            linear_a(8, 2, [tO], sink_b, OH[:, 4:6, :], OL[:, 4:6, :], tick=advance)
            drain()

            tx2, tsq2 = [], []

            def residual(which, n, t, p, deps):
                z = X[:, t, 512 * n:512 * n + 512]
                zt = ZT[2 * t + n]
                e0 = tt(zt, p, GT[:, which, 512 * n:512 * n + 512], MUL, deps)
                e1 = tt(z, z, zt, ADD, e0, tx)
                e2 = act(zt, z, ACT.Square, e1, accum_out=SSP[:, t, n:n + 1])
                return e0, e1, e2

            def sink_o(n, t, p, m):
                e0, e1, e2 = residual(0, n, t, p, (m, hold["gt", 0, n], t_att))
                tx2.append(e1)
                tsq2.append(e2)
                return (e0,)

            linear_b(2, 8, tm, sink_o, MH, ML)

            tT, _ = rms_T(VE["g_mlp"][:, 8 * l:8 * l + 8], ada[:, 32:40], ada[:, 24:32], "b2", tsq2,
                          (ada_tok[l, 2],), (t_att, tO, hold["dg", 0]))
            DG2 = ar(4096, 4, 128)
            side.append(spread(1, DG2, tx2, t_att))

            pinned = [take() for _ in range(4)]
            tR, tD = {}, {}

            def ff_up(i):
                b = take()
                for w in range(2):
                    u, h, lw, tok = unit()
                    for g in range(4):
                        seq = []
                        for k in (2 * g, 2 * g + 1):
                            seq += three_w(PS[b][:, 256 * w:256 * w + 256], h[:, 128 * k:128 * k + 128],
                                           lw[:, 128 * k:128 * k + 128], TH[:, k, :], TL[:, k, :], k == 0, k == 7)
                        m = mms(seq, tok, tT[g], PF[b] if w == 0 and g == 0 else ())
                    used(u, m)
                r = RR[i % 2]
                t = act(r, PS[b][:, :], ACT.Relu, m, tR.get(i - 2, ()), tx2)
                give(b, t)
                t = tt(r, r, r, MUL, t)
                r2 = r.rearrange("p (w i) -> p w i", w=2)
                th = act(RH[i % 2], r2, ACT.Copy, t, tD.get(i - 2, ()))
                tR[i] = tt(RL[i % 2], r2, RH[i % 2], SUB, th)

            def ff_down(i):
                for w in range(2):
                    u, h, lw, tok = unit()
                    seq = []
                    k = 2 * i + w
                    for n in range(2):
                        for t in range(2):
                            seq += three(PS[pinned[2 * t + n]][:, :], RH[i % 2][:, w, 128 * t:128 * t + 128],
                                         RL[i % 2][:, w, 128 * t:128 * t + 128], h[:, 512 * n:512 * n + 512],
                                         lw[:, 512 * n:512 * n + 512], k == 0, k == 31)
                    m = mms(seq, tok, tR[i], [PF[p] for p in pinned] if k == 0 else ())
                    used(u, m)
                tD[i] = m

            for i in range(16):
                ff_up(i)
                if i:
                    advance()
                    ff_down(i - 1)
            ff_down(15)
            tx3, tsq3 = [], []
            for n in range(2):
                for t in range(2):
                    p = pinned[2 * t + n]
                    e0, e1, e2 = residual(1, n, t, PS[p][:, :], (tD[15], hold["gt", 1, n], tsq2))
                    give(p, e0)
                    tx3.append(e1)
                    tsq3.append(e2)
            return tx3, (tx3, tD[15], tR[15]), tsq3

        SSP = tiny("b_ssp", 4, 2)
        def finish(tok):
            s = sem("s_out")
            Y.bare(lambda e: e.dma_start(out.rearrange("(t p) d -> p t d", p=128), X[:, :, :]).then_inc(s, 16), *tok)
            Y.bare(lambda e: e.wait_ge(s, 16))

        def program():
            tz, tgb, tO = gla()
            tx, tf = ln(0, 0, tz, LNG, tgb, ar(5120, 2, 1024), tO, False, tO)
            tz, tgb, t_up = moe(0, tx, tf, tO)
            tx, tT, rest = ln(0, 1, tz, LNG, tgb, ar(0, 2, 1024), t_up, True, t_up)
            tz, tgb, gb, tO = mlstm(tx, tT, rest)
            tx, tf = ln(1, 0, tz, gb, tgb, ar(5120, 2, 1024), tO, False, tO)
            tz, tgb, t_up = moe(1, tx, tf, tO)
            tx, _ = ln(1, 1, tz, LNG, tgb)
            if stop == "moe1":
                return tx
            tsq = [act(ar(0, 2, 1024)[:, t, 512 * n:512 * n + 512], X[:, t, 512 * n:512 * n + 512], ACT.Square, tx[t],
                       accum_out=SSP[:, t, n:n + 1]) for t in range(2) for n in range(2)]
            prior = (tx, tsq)
            for l in range(2):
                tx, prior, tsq = block2(l, tx, prior, tsq)
                if stop == "x1":
                    return tx
            return tx

        finish(program())
        block = ctx.enter_context(nc.Block())

        @block.sync
        def _(e):
            Y.emit(e)

        @block.scalar
        def _(e):
            S.emit(e)

        @block.vector
        def _(e):
            V.emit(e)

        @block.gpsimd
        def _(e):
            G.emit(e)

        @block.tensor
        def _(e):
            P.emit(e)
    return {"counts": {n: q.n for n, q in (("pe", P), ("act", S), ("dve", V), ("pool", G))}}


def _chunks(u):
    return np.ascontiguousarray(u.reshape(-1, 2, 128, 1024).transpose(0, 2, 1, 3)).reshape(-1, 2048)


def _stat(w):
    k, n = w.shape[0] // 128, w.shape[1] // 128
    u = w.reshape(k, 128, n, 128).transpose(2, 1, 0, 3)
    per = 8 // k
    u = u.reshape(n // per, per, 128, k, 128).transpose(0, 2, 1, 3, 4)
    return _chunks(u.reshape(-1, 128, 1024))


def _move(w):
    k, n = w.shape[0] // 256, w.shape[1] // 512
    return _chunks(w.reshape(k, 2, 128, n, 512).transpose(3, 0, 2, 1, 4).reshape(-1, 128, 1024))


def _col(v):
    return np.ascontiguousarray(np.reshape(v, (-1, 128)).T)


def _table(parts):
    where, at = {}, 0
    for n, a in parts:
        where[n] = (at, a.shape[1])
        at += a.shape[1]
    return where, np.ascontiguousarray(np.concatenate([a for _, a in parts], axis=1))


def _constants():
    f = np.float32
    i = np.arange(128)
    causal = (i[:, None] <= i[None, :]).astype(f)
    ones = np.ones((128, 128), f)
    decay = (causal * (i[:, None] // 64 == i[None, :] // 64) / 16.0).astype(f)
    fold = (i[:, None] % 64 == np.arange(64)[None, :]).astype(f)
    return [("ident", np.eye(128, dtype=f)), ("tri3", np.concatenate([causal, ones, causal], 1)),
            ("before", (i[:, None] < i[None, :]).astype(f)), ("ones", ones), ("decay", decay),
            ("fold", fold), ("slots", np.broadcast_to(np.arange(1, 65, dtype=f), (128, 64))),
            ("bar", np.broadcast_to(f(-1e-30) * np.tri(4, k=-1, dtype=f).reshape(1, 16), (128, 16)))]


def layout(i):
    D = {}
    x = i["x"][0]
    D["x"] = np.ascontiguousarray(x)
    D["xT"] = np.ascontiguousarray(x.reshape(256, 8, 128).transpose(2, 1, 0).reshape(128, 2048))
    cst_at, D["cst"] = _table(_constants())
    gw = i["gla_w_in"][0]
    mw = i["mlstm_w_in"][0]
    heads = np.concatenate([np.arange(256) + 256 * h + 1024 * j for h in range(4) for j in range(2)])
    vecs = [("gla_g", _col(i["gla_norm_g"][0])), ("mlstm_g", _col(i["mlstm_norm_g"][0])),
            ("conv_w", np.concatenate([_col(i["mlstm_conv_w"][0, j][heads]) for j in range(4)], 1)),
            ("conv_b", _col(i["mlstm_conv_b"][0][heads])),
            ("ln_g", _col(i["ln_g"])), ("ln_b", _col(i["ln_b"])),
            ("g_mix", _col(i["g_mix_2"])), ("g_mlp", _col(i["g_mlp_2"])), ("b_ada", _col(i["b_ada_2"])),
            ("c", _col(i["c_2"][0])),
            ("router", i["router_w"].reshape(8, 128, 16).transpose(1, 0, 2).reshape(128, 128)),
            ("glr", gw[:, 3072:].reshape(8, 128, 16).transpose(1, 0, 2).reshape(128, 128)),
            ("mbias", np.concatenate([i["mlstm_b_gates"][0], np.zeros(120, np.float32)]).reshape(128, 1)),
            ("mgate", mw[:, 4096:].reshape(8, 128, 8).transpose(1, 0, 2).reshape(128, 64))]
    vec_at, D["vec"] = _table(vecs)
    D["wgu"] = np.concatenate([i["gla_w_gate_up"][0], i["gla_b_gate"]], 0)
    D["lnrow"] = np.concatenate([i["ln_g"].reshape(4, 1024), i["ln_b"].reshape(4, 1024)], 1)
    D["gla_qk"] = _stat(gw[:, 0:1024])
    D["gla_v"], D["gla_r"] = _move(gw[:, 1024:2048]), _move(gw[:, 2048:3072])
    D["gla_o"] = _move(i["gla_w_out"][0])
    for n in range(2):
        up = [np.concatenate([_move(i["moe_w1"][n, e]), _move(i["moe_w3"][n, e])]) for e in range(16)]
        down = [_move(i["moe_w2"][n, e]) for e in range(16)]
        seq = [up[0]]
        for e in range(1, 16):
            seq += [up[e], down[e - 1]]
        D[f"moe{n}"] = np.concatenate(seq + [down[15]])
    D["ml_qk"] = _stat(mw[:, heads])
    D["ml_v"], D["ml_gate"] = _move(mw[:, 2048:3072]), _move(mw[:, 3072:4096])
    D["ml_o"] = _move(i["mlstm_w_out"][0])
    ada = i["w_ada_2"]
    D["ada"] = np.ascontiguousarray(ada.reshape(2, 8, 128, 3, 2048).transpose(0, 3, 1, 2, 4)).reshape(-1, 2048)
    D["rope"], D["masks"] = _rotation(), _dilated()
    qa, ka, qb, kb = i["q_norm_a_2"], i["k_norm_a_2"], i["q_norm_b_2"], i["k_norm_b_2"]
    gains = []
    for l in range(2):
        row = []
        for n, g in enumerate([qa[l], ka[l], qb[l, 0], kb[l, 0], qb[l, 1], kb[l, 1], qb[l, 2], kb[l, 2]]):
            swap = g.reshape(2, 2, 16)[:, ::-1] if n < 2 else g.reshape(2, 32)[::-1]
            row += [g, swap.reshape(64)]
        gains.append(np.concatenate(row))
    D["gains"] = np.stack(gains)
    perm = np.concatenate([np.arange(64) + 64 * h for h in (0, 4, 1, 5, 2, 6, 3, 7)])
    lists = []
    for l in range(2):
        w = i["w_in_2"][l]
        q, k, v = w[:, 0:512][:, perm], w[:, 512:640], w[:, 640:768]
        g3 = [[w[:, 768 + 768 * g + 256 * j:1024 + 768 * g + 256 * j] for j in range(3)] for g in range(3)]
        cols = [q, k, g3[0][0], v, g3[0][1], g3[0][2], g3[1][0], g3[1][1], g3[2][1], g3[1][2], g3[2][0], g3[2][2]]
        D[f"b2_in{l}"] = _move(np.concatenate(cols, axis=1))
        D[f"b2_gate{l}"] = _stat(w[:, 3072:5120])
        D[f"b2_a{l}"] = _stat(i["w_branch_a_2"][l][perm])
        D[f"b2_b{l}"] = _stat(i["w_branch_b_2"][l])
        D[f"b2_o{l}"] = _move(i["w_out_2"][l])
        f1 = _stat(i["w_ff1_2"][l]).reshape(16, 128, 2048)
        f2 = _chunks(i["w_ff2_2"][l].reshape(32, 128, 1024)).reshape(16, 128, 2048)
        seq = [f1[0]]
        for n in range(1, 16):
            seq += [f1[n], f2[n - 1]]
        D[f"b2_ff{l}"] = np.concatenate(seq + [f2[15]])
    order = [("gla_qk", [2, 3]), ("gla_v", [0, 1, 2, 3]), ("gla_r", [0, 1]), ("gla_o", [2, 3]), ("moe0", []),
             ("ml_v", [2, 3]), ("ml_qk", []), ("ml_gate", []), ("ml_o", [2, 3]), ("moe1", [])]
    for l in range(2):
        order += [(f"b2_in{l}", []), (f"b2_gate{l}", [] if l else list(range(8))), (f"b2_a{l}", [] if l else [0, 1]),
                  (f"b2_b{l}", []), (f"b2_o{l}", []), (f"b2_ff{l}", [] if l else [1 + n for n in range(24)])]
    return D, cst_at, vec_at, order


def _rotation():
    f = np.float32

    def cs(pos, dim):
        inv = (f(10000.0) ** (-np.arange(0, dim, 2, dtype=f) / f(dim))).astype(f)
        ang = pos.astype(f)[:, None] * inv[None, :]
        return np.cos(ang).astype(f), np.sin(ang).astype(f)

    s = np.arange(256)
    (rc, rs), (cc, c_s), (sc, ss) = cs(s // 64, 32), cs(s % 64, 32), cs(s, 64)
    ax = np.stack([np.concatenate([rc, rc, cc, cc], 1), np.concatenate([-rs, rs, -c_s, c_s], 1)])
    seq = np.stack([np.concatenate([sc, sc], 1), np.concatenate([-ss, ss], 1)])
    t = np.stack([ax, seq]).reshape(2, 2, 2, 128, 64)
    return np.ascontiguousarray(t.transpose(3, 0, 1, 2, 4)).reshape(128, 512)


def _dilated():
    i = np.arange(256)
    d = i[None, :] - i[:, None]
    m = [np.abs(d) <= 64, d % 4 == 0, d % 16 == 0]
    m = np.stack([np.where(x, 0.0, -1e30).astype(np.float32) for x in m]).reshape(3, 2, 128, 256)
    return np.ascontiguousarray(m.transpose(2, 0, 1, 3)).reshape(128, 1536)


def whole(name, c):
    return 2 if name.startswith("moe") and c % 2 == 1 else 0


def build(nc, D, cst_at, vec_at, order, out, stop=None):
    aps = {}
    for n, a in D.items():
        aps[n] = nc.dram_tensor(f"in_{n}", a.shape, mybir.dt.from_np(a.dtype), kind="ExternalInput").ap()
    chunks, stops, moe, sent = [], {}, {}, 0
    for n, extra in order:
        count = D[n].shape[0] // 128
        for c in range(count):
            for _ in range(extra.count(c)):
                at = 128 * sent
                chunks.append(("ada", aps["ada"][at:at + 128, :], sent // 24, sent // 8 % 3, sent % 8))
                sent += 1
            chunks.append(("w", aps[n][128 * c:128 * c + 128, :], whole(n, c)))
        if n.startswith("moe"):
            moe[int(n[3])] = chunks[-count:]
            stops[len(chunks)] = int(n[3])
    small = {"cst": (cst_at, D["cst"].shape[1]), "vec": (vec_at, D["vec"].shape[1]), "chunks": chunks, "stops": stops, "moe": moe}
    return two_block_kernel(nc, aps, out, small, stop)


def kernel(**inputs):
    import concourse.bacc as _bacc
    from concourse.bass_utils import run_bass_kernel_spmd as _run

    nc = _bacc.Bacc("TRN2", target_bir_lowering=False, num_devices=1)
    ins = {k: np.asarray(v) for k, v in inputs.items()}
    D, cst_at, vec_at, order = layout(ins)
    out = nc.dram_tensor("out_dram", (256, 1024), mybir.dt.float32, kind="ExternalOutput").ap()
    build(nc, D, cst_at, vec_at, order, out)
    r = _run(nc, [{f"in_{n}": a for n, a in D.items()}], core_ids=[0])
    return r.results[0]["out_dram"].reshape(1, 256, 1024)
```

```python
import concourse.bass as bass
from concourse import mybir
from contextlib import ExitStack
import numpy as np


class Queue:

    def __init__(self, sem):
        self.sem = sem
        self.n = 0
        self.items = []
        self.outer = None

    def __call__(self, fn, *after):
        self.n += 1
        self.items.append((fn, after, True))
        return (self.sem, self.n)

    def bare(self, fn, *after):
        self.items.append((fn, after, False))

    def enter(self, sem):
        self.outer = (self.sem, self.n, self.items)
        self.sem, self.n, self.items = sem, 0, []

    def leave(self):
        part = (self.sem, self.items)
        self.sem, self.n, self.items = self.outer
        return part

    def emit(self, eng):
        self.run(eng, self.sem, self.items, {})

    def run(self, eng, sem, items, met):
        def wait(tokens):
            for tok in tokens:
                if len(tok) == 2 and isinstance(tok[1], int):
                    if met.get(id(tok[0]), 0) < tok[1]:
                        eng.wait_ge(tok[0], tok[1])
                        met[id(tok[0])] = tok[1]
                else:
                    wait(tok)

        for item in items:
            if isinstance(item, Part):
                wait(item.after)
                with eng.register(item.name) as reg:
                    eng.reg_load(reg, item.flag)
                    with eng.If_ne(reg, 0):
                        self.run(eng, item.sem, item.items, dict(met))
                continue
            fn, after, counted = item
            wait(after)
            ins = fn(eng)
            if counted:
                ins.then_inc(sem, 1)


class Part:

    def __init__(self, name, flag, after):
        self.name, self.flag, self.after = name, flag, after
        self.sem, self.items = None, []


def two_block_kernel(nc, D, out, small):
    F32 = mybir.dt.float32
    F32R = mybir.dt.float32r
    I32 = mybir.dt.int32
    ALU = mybir.AluOpType
    ACT = mybir.ActivationFunctionType
    AX = mybir.AxisListType
    MUL, ADD, SUB, MAX, MIN, NOP = ALU.mult, ALU.add, ALU.subtract, ALU.max, ALU.min, ALU.bypass

    ALPHA = float(4 ** 0.25)
    NR = 6
    NC = 5
    NA = 17408
    ctx = ExitStack()
    with ctx:
        def sb(name, shape, dt=F32):
            return ctx.enter_context(nc.sbuf_tensor(name, shape, dt))

        def sem(name):
            return ctx.enter_context(nc.semaphore(name))

        P, S, V, G = (Queue(sem(n)) for n in ("s_pe", "s_act", "s_dve", "s_pool"))
        Y = Queue(None)

        def act(o, i, f, *after, **kw):
            return S(lambda e: e.activation(o, i, f, **kw), *after)

        def tt(o, a, b, op, *after, q=None):
            return (q or V)(lambda e: e.tensor_tensor(o, a, b, op), *after)

        def ts(o, a, s1, s2, op0, op1, *after):
            return V(lambda e: e.tensor_scalar(o, a, s1, s2, op0=op0, op1=op1), *after)

        def stt(o, a, s, b, op0, op1, *after):
            return V(lambda e: e.scalar_tensor_tensor(out=o, in0=a, scalar=s, in1=b, op0=op0, op1=op1), *after)

        def cp(o, a, *after):
            return V(lambda e: e.tensor_copy(o, a), *after)

        def red(o, a, op, *after):
            return V(lambda e: e.tensor_reduce(o, a, AX.X, op), *after)

        def inv(o, a, *after):
            return V(lambda e: e.reciprocal(o, a), *after)

        def mms(seq, *after):
            def go(e):
                for o, l, r, a, z in seq:
                    ins = e.matmul(o, l, r, start=a, stop=z, skip_group_check=True)
                return ins
            return P(go, *after)

        def turns(seq, *after):
            def go(e):
                for o, i in seq:
                    ins = e.transpose(o, i, ident)
                return ins
            return P(go, *after)

        loads = []

        def load(dst, src, *after):
            s = sem(f"s_ld{len(loads)}")
            loads.append(s)
            Y.bare(lambda e: e.dma_start(dst, src).then_inc(s, 16), *after)
            return (s, 16)

        def gload(dst, src, *after):
            s = sem(f"s_ld{len(loads)}")
            loads.append(s)
            G.bare(lambda e: e.dma_start(dst, src).then_inc(s, 16), *after)
            return (s, 16)

        PS = [ctx.enter_context(nc.psum_tensor(f"ps{i}", [128, 512], F32)) for i in range(8)]
        PF = [()] * 8
        free = list(range(8))

        def take():
            return free.pop(0)

        def give(b, *tok):
            PF[b] = tok
            free.append(b)

        def three(o, xh, xl, wh, wl, first, last):
            return [(o, xh, wh, first, False), (o, xh, wl, False, False), (o, xl, wh, False, last)]

        def three_w(o, wh, wl, xh, xl, first, last):
            return [(o, wh, xh, first, False), (o, wh, xl, False, False), (o, wl, xh, False, last)]

        cst = sb("cst", [128, small["cst"][1]])
        vec = sb("vec", [128, small["vec"][1]])
        PTC = nc.alloc_sbuf_tensor_at("PTC", [128, 256], F32R, offset=nc.sbuf_base - 4 * (small["vec"][1] + 128))
        C = {n: cst[:, o:o + w] for n, (o, w) in small["cst"][0].items()}
        VE = {n: vec[:, o:o + w] for n, (o, w) in small["vec"][0].items()}
        ident = C["ident"]
        raw = [sb(f"raw{i}", [128, 2048]) for i in range(NR)]
        hi = [sb(f"hi{i}", [128, 1024], F32R) for i in range(NC)]
        lo = [sb(f"lo{i}", [128, 1024], F32R) for i in range(NC)]
        X = sb("X", [128, 2, 1024])
        XR = nc.alloc_sbuf_tensor_at("XR", [128, 2, 1024], F32R, offset=nc.sbuf_base - 4 * 2048)
        F = sb("F", [128, 8, 256])
        FR = nc.alloc_sbuf_tensor_at("FR", [128, 2048], F32R, offset=nc.sbuf_base - 4 * 2048)
        T2 = sb("T2", [128, 4096], F32R)
        TH = T2[:, 0:2048].rearrange("p (k i) -> p k i", k=8)
        TL = T2[:, 2048:4096].rearrange("p (k i) -> p k i", k=8)
        ACC = sb("ACC", [128, 2048])
        FLAG = sb("FLAG", [1, 2], I32)
        ADA = sb("ADA", [128, 2, 48])
        IDR = sb("IDR", [128, 128], F32R)
        GHL = sb("GHL", [128, 64], F32R)
        SEL = sb("SEL", [128, 32], F32R)
        TINY = sb("TINY", [128, 1024])
        AR = sb("AR", [128, NA])
        AF = nc.alloc_sbuf_tensor_at("AF", [128, NA], F32R, offset=nc.sbuf_base - 4 * NA)

        def ar(o, *shape, dt=None):
            n = int(np.prod(shape))
            assert o + n <= NA
            ap = (AR if dt is None else AF)[:, o:o + n]
            if len(shape) == 1:
                return ap
            names = "abcdef"[:len(shape)]
            return ap.rearrange(f"p ({' '.join(names)}) -> p {' '.join(names)}",
                                **{k: v for k, v in zip(names[:-1], shape[:-1])})

        cols = {}
        col_at = [0]

        def tiny(name, n, split=None):
            if name not in cols:
                cols[name] = (col_at[0], n)
                col_at[0] += n
                assert col_at[0] <= 1024
            o, w = cols[name]
            assert w == n
            ap = TINY[:, o:o + n]
            return ap if split is None else ap.rearrange("p (a b) -> p a b", a=split)

        chunks, stops = small["chunks"], small["stops"]

        def stream(chunks, sems, stops, spare=()):
            events, place, before, turn, uses = [], [], [], [], {}
            for c, ch in enumerate(chunks):
                events += [("ada", c, 1)] if ch[0] == "ada" else [("w", c, 0), ("w", c, 1)]
                open_ = [NR + p for p, first, last in spare if first < c <= last] + list(range(NR))
                p = [NR + p for p, first, last in spare if first == c] or [min(open_, key=lambda q: uses.get(q, [q - NR])[-1])]
                n = uses.setdefault(p[0], [])
                place.append(p[0])
                before.append(n[-1] if n else None)
                n.append(c)
                turn.append(len(n))
            return {"chunks": chunks, "sems": sems, "events": events, "stops": stops, "ev": 0, "u": 0, "dma": 0,
                    "units": [], "split": [], "used": {}, "left": {}, "head": None, "place": place, "before": before,
                    "turn": turn, "uses": uses, "spare": [s[1] for s in spare], "room": {}}

        raw += [ACC, ar(4096, 2048), ar(6144, 2048), ar(11264, 2048), ar(13312, 2048), ar(15360, 2048),
                ar(2048, 2048)]
        st = stream(chunks, [sem(f"s_raw{i}") for i in range(NR + 7)], stops, [s for i in range(2) for s in small["spare"][i]])
        parts = {}
        ada_tok = {("acc", 0): ()}
        ACCS = [ACC[:, :], ar(11264, 2048), ar(13312, 2048)]
        sums, kept, after = [], [], []

        def gone(c):
            return len(st["left"].get(c, ())) >= (1 if st["chunks"][c][0] == "ada" else 2)

        def issue(most=None):
            while st["dma"] < len(st["chunks"]) and most != 0:
                c = st["dma"]
                old, p, room = st["before"][c], st["place"][c], ()
                if old is not None and not gone(old):
                    return
                if c in st["spare"]:
                    if c not in st["room"]:
                        return
                    room = st["room"][c]
                st["dma"] += 1
                if c in st["stops"]:
                    Y.items.append(parts[st["stops"][c]]["sync"])
                src, s, at = st["chunks"][c][1], st["sems"][p], 1024 if st["head"] and c == 0 else 0
                Y.bare(lambda e, o=raw[p][:, at:2048], i=src[:, at:2048], s=s: e.dma_start(o, i).then_inc(s, 16),
                       () if old is None else st["left"][old], room)
                most = most and most - 1

        def left(c, tok):
            st["left"].setdefault(c, []).append(tok)
            issue()

        def landed(c, half=1):
            if st["head"] and c == 0 and half == 0:
                return st["head"]
            return (st["sems"][st["place"][c]], 16 * st["turn"][c])

        def spare_rooms(i, *tok):
            later(True)
            for p, n, _ in small["spare"][i]:
                if p == 0:
                    after.append(lambda n=n: st["room"].update({n: ada_tok["acc", 0]}) or issue())
                elif p < 6:
                    st["room"][n] = tok
            issue()

        def step(put_off=None):
            kind, c, half = st["events"][st["ev"]]
            st["ev"] += 1
            if kind == "ada":
                left(c, ada_step(c))
                return
            r = raw[st["place"][c]][:, 1024 * half:1024 * half + 1024]
            u = len(st["units"])
            if st["chunks"][c][2] >> half & 1:
                st["units"].append((r, None, landed(c, half), c))
                return
            n = len(st["split"])
            st["split"].append(u)
            h, l = hi[n % NC][:, :], lo[n % NC][:, :]
            th = act(h, r, ACT.Copy, landed(c, half), st["used"][st["split"][n - NC]] if n >= NC else ())
            st["units"].append(None)

            def rest():
                tl = tt(l, r, h, SUB, th)
                st["units"][u] = (h, l, tl, None)
                left(c, tl)

            if put_off is None:
                rest()
            else:
                put_off.append(rest)

        def unit(early=True):
            u = st["u"]
            st["u"] += 1
            while st["ev"] < len(st["events"]):
                if len(st["units"]) > u:
                    if not early:
                        break
                    n = len(st["split"])
                    if n >= NC and st["split"][n - NC] >= u:
                        break
                    c = st["events"][st["ev"]][1]
                    if c in st["stops"] or len(st["units"]) > u + NC:
                        break
                step()
            later()
            return (u,) + st["units"][u][0:3]

        def later(all_of_them=False):
            while sums:
                for s in list(sums):
                    s[0] -= 1
                    if s[0] < 0 or all_of_them:
                        sums.remove(s)
                        more = s[1]()
                        if callable(more):
                            sums.append([0, more])
                if not all_of_them:
                    return

        def ahead(most):
            u, put_off = len(st["units"]), []
            while st["ev"] < len(st["events"]) and len(st["units"]) < u + most:
                n, (kind, c, _) = len(st["split"]), st["events"][st["ev"]]
                if kind == "ada" or c in st["stops"] or n >= NC and st["split"][n - NC] >= st["u"]:
                    break
                step(put_off)
            return (rest() for rest in put_off)

        def used(u, tok):
            st["used"][u] = tok
            c = st["units"][u][3]
            if c is not None:
                left(c, tok)

        def ada_step(c):
            _, _, layer, blk, k = st["chunks"][c]
            n = (1 + blk) % 3 if layer else 0
            acc, key = ACCS[n], ("acc", n)
            w = raw[st["place"][c]][:, :]
            cc = c_act[:, k:k + 1]
            if k == 0:
                later(True)
                t = ts(acc, w, cc, None, MUL, NOP, landed(c), ready["c"], ada_tok[key])
            else:
                t = stt(acc, w, cc, acc, MUL, ADD, landed(c), ada_tok[key])
            ada_tok[key] = t
            if k == 7:
                def add_up():
                    b = take()
                    m = mms([(PS[b][:, j:j + 1], acc[:, 128 * j:128 * j + 128], C["ones"][:, 0:1], True, True)
                             for j in range(16)], PF[b], t)
                    ada_tok[key] = (m,)

                    def out():
                        o = layer * 48 + blk * 16
                        e = tt(ADA[:, layer, 16 * blk:16 * blk + 16], PS[b][:, 0:16], VE["b_ada"][:, o:o + 16], ADD, m)
                        give(b, e)
                        ada_tok[layer, blk] = e
                    return out
                if (layer, blk) in KEPT:
                    kept.append(((layer, blk), add_up))
                else:
                    sums.append([6, add_up])
            return t

        KEPT = ((0, 0), (0, 1), (0, 2), (1, 0), (1, 1), (1, 2))

        def add_kept(last=(1, 2)):
            outs = []
            while kept and kept[0][0] <= last:
                outs.append(kept.pop(0)[1]())
            while after:
                after.pop(0)()
            return outs

        side = []

        def advance(n=1):
            while n and side:
                try:
                    next(side[0])
                    n -= 1
                except StopIteration:
                    side.pop(0)

        def drain():
            while side:
                advance()

        tF = []
        for g in range(2):
            tF.append(load(F[:, 4 * g:4 * g + 4, :],
                           D["xT"][:, 1024 * g:1024 * g + 1024].rearrange("p (k i) -> p k i", k=4)))
            if g == 0:
                st["head"] = load(raw[0][:, 0:1024], chunks[0][1][:, 0:1024])
        issue(1)
        tvec = load(vec[:, :], D["vec"])
        issue(1)
        tcst = load(cst[:, :], D["cst"])
        WG = ar(16640, 512)[0:17, :]
        tWG = load(WG, D["wgu"])
        issue()
        tX = load(X[:, :, :], D["x"].rearrange("(t p) d -> p t d", p=128))

        def split(src, h, l, *after):
            th = act(h, src, ACT.Copy, *after)
            return tt(l, src, h, SUB, th)

        def rsqrt(o, v, n, name, *after):
            two = name if not isinstance(name, str) else tiny(name, 2 * n)
            y, p = two[:, 0:n], two[:, n:2 * n]
            t = ts(y.bitcast(I32), v.bitcast(I32), -0.5, 1597463007.0, MUL, ADD, *after)
            tw = ts(o, v, -27.0 / 1024.0, None, MUL, NOP, *after)
            t = tt(p, y, y, MUL, t)
            t = tt(p, p, v, MUL, t)
            t = stt(p, p, -10.0 / 3.0, p, ADD, MUL, t)
            t = stt(y, p, 5.0, y, ADD, MUL, t)
            t = tt(p, y, y, MUL, t)
            t = tt(p, p, o, MUL, t, tw)
            return stt(o, p, 9.0 / 16.0, y, ADD, MUL, t)

        def linear_a(mt, kt, waits, sink, th=None, tl=None, tick=None):
            th = TH if th is None else th
            tl = TL if tl is None else tl
            per = 8 // kt
            for n in range(mt // 2):
                b = take()
                for i in range(2):
                    m = 2 * n + i
                    if m % per == 0:
                        u, h, l, tok = unit()
                    for g in range(kt // 2):
                        seq = []
                        for k in (2 * g, 2 * g + 1):
                            c = 128 * (kt * (m % per) + k)
                            o, w, ends = PS[b][:, 256 * i:256 * i + 256], h[:, c:c + 128], (k == 0, k == kt - 1)
                            seq += [(o, w, F[:, k, :], *ends)] if l is None else three_w(o, w, l[:, c:c + 128], th[:, k, :],
                                                                                     tl[:, k, :], *ends)
                        done = mms(seq, tok, waits[g], PF[b] if i == 0 and g == 0 else ())
                    if m % per == per - 1:
                        used(u, done)
                        if tick and not (i == 1):
                            tick()
                give(b, *sink(n, PS[b][:, :], done))
                if tick:
                    tick()

        def linear_b(nb, kt, waits, sink, th=None, tl=None, tick=None, last=None, halved=False, half=None, staggered=False):
            th = TH if th is None else th
            tl = TL if tl is None else tl
            ng = kt // 2
            order = [(n, g) for n in range(nb) for g in range(ng)]
            if halved:
                order.sort(key=lambda x: x[1] * 2 // ng)
            middle = len(order) // 2 - 1
            if staggered:
                order.pop()
            bk = {}
            for at, (n, g) in enumerate(order):
                if half and at == middle:
                    half()
                if n not in bk:
                    bk[n] = [take(), take()]
                final = n == nb - 1
                tail = staggered and at == len(order) - 1
                early = not (final and g >= ng - 2 and staggered)
                us = [(j, *unit(early)) for j in ((g, g + 1) if tail else (g,))]
                done = []
                for t in range(2):
                    for i, u, h, l, tok in us:
                        seq = []
                        for j in range(2):
                            k = 2 * i + j
                            seq += three(PS[bk[n][t]][:, :], th[:, k, 128 * t:128 * t + 128],
                                         tl[:, k, 128 * t:128 * t + 128],
                                         h[:, 512 * j:512 * j + 512], l[:, 512 * j:512 * j + 512],
                                         k == 0, k == kt - 1)
                        m = mms(seq, tok, waits[i], PF[bk[n][t]] if i == 0 else ())
                        if t:
                            used(u, m)
                    done.append(m)
                if tick:
                    tick()
                if tail or g == ng - 1:
                    if last and final:
                        last()
                    for t in range(2):
                        give(bk[n][t], *sink(n, t, PS[bk[n][t]][:, :], done[t]))

        def transposed(src, tsrc, scale, bias, with_T, tp=()):
            done, fs = [], []
            for g in range(4):
                b = take()
                m = turns([(PS[b][:, 256 * k + 128 * t:256 * k + 128 * t + 128],
                            src[:, t, 128 * (2 * g + k):128 * (2 * g + k) + 128])
                           for t in range(2) for k in range(2)], PF[b], tsrc[g // 2])
                f = []
                for k in range(2):
                    kt = 2 * g + k
                    o, p = F[:, kt, :], PS[b][:, 256 * k:256 * k + 256]
                    sc, bi = scale[:, kt:kt + 1], bias[:, kt:kt + 1]
                    if with_T and g % 2:
                        f.append(ts(o, p, sc, bi, MUL, ADD, m, tp))
                    else:
                        f.append(act(o, p, ACT.Identity, m, tp, scale=sc, bias=bi))
                give(b, f[1])
                fs.append(f)
                if not with_T:
                    done.append(f[1])
                elif g % 2:
                    for j in (g - 1, g):
                        two = slice(2 * j, 2 * j + 2)
                        done.append(split(F[:, two, :], TH[:, two, :], TL[:, two, :], fs[j]))
            return done, m

        LNS = tiny("ln_stats", 24)

        def ln_rows(i, j, gb, *after):
            t = gload(gb[0:1, :], D["lnrow"][2 * i + j:2 * i + j + 1, :], *after)
            return G(lambda e: e.partition_broadcast(gb, gb[0:1, :]), t)

        def ln_piece(t, n, z, *after):
            o = 12 * t + 6 * n
            return V(lambda e: e.bn_stats(LNS[:, o:o + 6], z), *after)

        def ln(i, j, tz, gb, tgb, zb=None, XN=None, txn=(), with_T=False, tp=()):
            o = (2 * i + j) * 8
            mv = tiny("ln_mv", 4, 2)
            extra = ahead(NC)
            tb = [V(lambda e, t=t: e.bn_aggr(mv[:, t, :], LNS[:, 12 * t:12 * t + 12]), tz) for t in range(2)]
            ve, rs, nb = tiny("ln_ve", 2), tiny("ln_rs", 2), tiny("ln_nb", 2)
            t = ts(ve, mv[:, :, 1], 1e-5, None, ADD, NOP, tb)
            tr = rsqrt(rs, ve, 2, "ln_nr", t)
            xn, tx, done, halves = [], [], [], (slice(0, 512), slice(512, 1024))

            def z(t, n):
                return PS[zb[t, n]][:, :] if zb else X[:, t, halves[n]]

            if XN is not None:
                tn = stt(nb[:, 1:2], mv[:, 1, 0:1], -1.0, rs[:, 1:2], MUL, MUL, tr)
                for n, w in enumerate(halves):
                    xn.append([ts(XN[:, 0, w], z(0, n), mv[:, 0, 0:1], rs[:, 0:1], SUB, MUL, tr, txn),
                               act(XN[:, 1, w], z(1, n), ACT.Identity, tn, txn, scale=rs[:, 1:2], bias=nb[:, 1:2])])
                    for t in range(2):
                        if zb:
                            give(zb[t, n], xn[n][t])

            def finish():
                for t in range(2):
                    if not zb:
                        a = stt(X[:, t, :], X[:, t, :], mv[:, t, 0:1], gb[:, 0:1024], SUB, MUL, tgb, [x[t] for x in xn], tr)
                    elif XN is not None:
                        a = tt(X[:, t, :], XN[:, t, :], gb[:, 0:1024], MUL, tgb, [x[t] for x in xn])
                    else:
                        a = []
                        for n, w in enumerate(halves):
                            a.append(stt(X[:, t, w], z(t, n), mv[:, t, 0:1], gb[:, w], SUB, MUL, tgb, tr))
                            give(zb[t, n], a[n])
                    yield
                    if zb and XN is not None:
                        tx.append(tt(X[:, t, :], X[:, t, :], gb[:, 1024:2048], ADD, a))
                    elif zb:
                        tx.append([stt(X[:, t, w], X[:, t, w], rs[:, t:t + 1], gb[:, 1024 + w.start:1024 + w.stop], MUL, ADD,
                                       a[n]) for n, w in enumerate(halves)])
                    else:
                        tx.append(stt(X[:, t, :], X[:, t, :], rs[:, t:t + 1], gb[:, 1024:2048], MUL, ADD, a))
                    yield

            if with_T:
                for _ in range(2):
                    next(extra, None)
            else:
                list(finish())
            outs = add_kept()
            if XN is not None:
                done, _ = transposed(XN, xn, VE["ln_g"][:, o:o + 8], VE["ln_b"][:, o:o + 8], with_T, tp)
            for out in outs:
                out()
            if not with_T:
                return tx, done, extra
            list(extra)
            return tx, done, finish()

        def head_norm(ob, to, rden, YN, res):
            stats = tiny("hn_stats", 48)
            mv = tiny("hn_mv", 16, 8)
            ve, rs, nb = tiny("hn_ve", 8), tiny("hn_rs", 8), tiny("hn_nb", 8)

            def head(t, h):
                return PS[ob[t, h // 2]][:, 256 * (h % 2):256 * (h % 2) + 256]

            ta = []
            for i in range(8):
                t, h = i // 4, i % 4
                ta.append(V(lambda e, i=i, t=t, h=h: e.bn_stats(stats[:, 6 * i:6 * i + 6], head(t, h)), to[t, h // 2]))
                if i % 4 == 3:
                    yield
            tb = [V(lambda e, i=i: e.bn_aggr(mv[:, i, :], stats[:, 6 * i:6 * i + 6]), ta[i]) for i in range(8)]
            if rden is None:
                tv = ts(ve, mv[:, :, 1], 1e-5, None, ADD, NOP, tb)
                tr = rsqrt(rs, ve, 8, "hn_nr", tv)
            else:
                rd, trd = rden
                tv = tt(ve, rd, rd, MUL, trd)
                tv = tt(ve, ve, mv[:, :, 1], MUL, tv, tb)
                tv = ts(ve, ve, 1e-5, None, ADD, NOP, tv)
                tr = rsqrt(rs, ve, 8, "hn_nr", tv)
                tr = tt(rs, rs, rd, MUL, tr)
            tn = stt(nb, mv[:, :, 0], -1.0, rs, MUL, MUL, tr, tb)
            yield
            for hp in range(2):
                for t in range(2):
                    for h in (2 * hp, 2 * hp + 1):
                        i = 4 * t + h
                        tok = act(YN[:, t, 256 * h:256 * h + 256], head(t, h), ACT.Identity, tn,
                                  scale=rs[:, i:i + 1], bias=nb[:, i:i + 1])
                    give(ob[t, hp], tok)
                    res[t, hp] = tok
                yield

        def turn_heads(g, YN, gcol, ty, tT):
            b = take()
            m = turns([(PS[b][:, 256 * k + 128 * t:256 * k + 128 * t + 128],
                        YN[:, t, 128 * (2 * g + k):128 * (2 * g + k) + 128])
                       for t in range(2) for k in range(2)], PF[b], ty)
            for k in range(2):
                kt = 2 * g + k
                th = act(TH[:, kt, :], PS[b][:, 256 * k:256 * k + 256], ACT.Copy, m, scale=gcol[:, kt:kt + 1])
            for k in range(2):
                kt = 2 * g + k
                tl = stt(TL[:, kt, :], PS[b][:, 256 * k:256 * k + 256], gcol[:, kt:kt + 1], TH[:, kt, :], MUL, SUB, th)
            give(b, tl)
            tT.append(tl)

        def mix_out(tT, tx, half):
            tz = []

            def sink(n, t, p, m):
                z = X[:, t, 512 * n:512 * n + 512]
                e = stt(z, z, ALPHA, p, MUL, ADD, m, tx)
                tz.append(ln_piece(t, n, z, e))
                return (e,)

            linear_b(2, 8, tT, sink, halved=True, half=half, staggered=True)
            return tz

        ready = {}
        c_act, halfg = tiny("c_act", 8), tiny("halfg", 16)

        def constants():
            th, u = tiny("c_th", 8), tiny("c_u", 8)
            t = act(th, VE["c"], ACT.Tanh, tvec, scale=0.5)
            t = stt(u, th, 1.0, VE["c"], ADD, MUL, t)
            ready["c"] = ts(c_act, u, 0.5, None, MUL, NOP, t)
            g0 = small["vec"][0]["gla_g"][0]
            ts(halfg, vec[:, g0:g0 + 16], 0.5, None, MUL, NOP, tvec)
            ready["idr"] = act(IDR[:, :], ident, ACT.Copy, tcst)

        def gla():
            QT, KT, BT = ar(0, 4, 256), ar(1024, 4, 256), ar(2048, 4, 256)
            KM = ar(3072, 4, 4, 256)
            VV, SR = ar(7168, 2, 1024), ar(9216, 2, 1024)
            PM = ar(11264, 4, 384)
            E1, E3 = ar(12800, 4, 256), ar(13824, 4, 256)
            LA, LB = ar(14848, 2, 512), ar(7168, 2, 512)
            GL = ar(15872, 256)
            YN = ar(0, 2, 1024)
            ET = tiny("g_et", 16, 4)
            tz = [G(lambda e: e.memset(KM[:, :, 0, 64:128], 0.0)),
                  G(lambda e: e.memset(KM[:, :, 2, 192:256], 0.0))]
            tone = G(lambda e: e.memset(GL[0:17, :], 1.0))
            tT = []
            for g in range(4):
                two = slice(2 * g, 2 * g + 2)
                tT.append(split(F[:, two, :], TH[:, two, :], TL[:, two, :], tF[g // 2]))
                if g == 1:
                    list(ahead(1))
            qk, tv, tp, ob, to, ty, res = [], {}, [], {}, {}, [], {}
            r = {}

            def prepare():
                b = take()
                glr = VE["glr"].rearrange("p (k r) -> p k r", k=8)
                m = mms([(PS[b][0:16, 0:256], glr[:, k, :], F[:, k, :], k == 0, k == 7) for k in range(8)],
                        PF[b], tF, tvec)
                t = act(GL[0:16, :], PS[b][0:16, 0:256], ACT.Copy, m, tone)
                give(b, t)
                constants()
                yield
                zb, ta = [take(), take()], []
                for q in range(2):
                    m = mms([(PS[zb[q]][:, :], GL[0:17, 128 * q:128 * q + 128], WG, True, True)], PF[zb[q]], t, tWG)
                    ta.append(act(LA[:, q, :], PS[zb[q]][:, :], ACT.Abs, m))
                yield
                e = act(LA, LA, ACT.Exp, ta, scale=-1.0)
                e = act(LA, LA, ACT.Ln, e, bias=1.0)
                tl = []
                for q in range(2):
                    tl.append(stt(LB[:, q, :], PS[zb[q]][:, :], 0.0, LA[:, q, :], MIN, SUB, e))
                    give(zb[q], tl[q])
                yield
                yield
                tb = []
                for hp in range(2):
                    b = take()
                    m = mms([(PS[b][:, 256 * hh + 128 * q:256 * hh + 128 * q + 128],
                              LB[:, q, 128 * (2 * hp + hh):128 * (2 * hp + hh) + 128], C["decay"], True, True)
                             for hh in range(2) for q in range(2)], PF[b], tl, tcst)
                    e = act(BT[:, 2 * hp:2 * hp + 2, :], PS[b][:, :].rearrange("p (h i) -> p h i", h=2), ACT.Copy, m)
                    give(b, e)
                    tb.append(e)
                r["lb"] = m
                yield
                BC = BT.rearrange("p h (c i) -> p h c i", c=4)
                KM4 = KM.rearrange("p h c (d i) -> p h (c d) i", d=4)
                KC = KT.rearrange("p h (c i) -> p h c i", c=4)
                E1c, E3c = (x.rearrange("p h (c i) -> p h c i", c=4) for x in (E1, E3))
                et = act(ET, BC[:, :, :, 63], ACT.Exp, tb)
                d3 = tt(E3c[:, :, 0:3, :], BC[:, :, 0:3, 63:64].broadcast_to([128, 4, 3, 64]), BC[:, :, 0:3, :], SUB, tb)
                e1 = act(E1, BT, ACT.Exp, tb)
                e3 = act(E3c[:, :, 0:3, :], E3c[:, :, 0:3, :], ACT.Exp, d3)
                yield
                while len(qk) < 4:
                    yield
                tq = tt(QT, QT, E1, MUL, e1, qk)
                e2 = act(E1, BT, ACT.Exp, tq, scale=-1.0)
                yield
                k1 = tt(KM4[:, :, 4:16:5, :], KC[:, :, 0:3, :], E3c[:, :, 0:3, :], MUL, e3, qk)
                k2 = tt(KM[:, :, 2, 0:64], KM[:, :, 1, 0:64], ET[:, :, 1:2].broadcast_to([128, 4, 64]), MUL, k1, et)
                yield
                ki = tt(KM4[:, :, 0:16:5, :], KC, E1c, MUL, e2, tz)
                k3 = tt(KM[:, :, 3, 0:128], KM[:, :, 2, 0:128], ET[:, :, 2:3].broadcast_to([128, 4, 128]), MUL, k2)
                yield
                yield
                for h in range(4):
                    b = take()
                    seq = []
                    for n, (q, kk) in enumerate(((0, 0), (1, 0), (1, 1))):
                        for c in range(2 * q, 2 * q + 2):
                            o = 128 * n + 64 * (c % 2)
                            seq.append((PS[b][:, o:o + 64], KM[:, h, c, 128 * kk:128 * kk + 128],
                                        QT[:, h, 64 * c:64 * c + 64], True, True))
                    m = mms(seq, PF[b], k3, tq, ki)
                    d = tt(PM[:, h, :], PS[b][:, 0:384], C["tri3"], MUL, m)
                    give(b, d)
                    tp.append(d)
                    yield
                r["scores"] = m

            def values():
                for hp in range(2):
                    for t in range(2):
                        b = ob[t, hp] = take()
                        seq = []
                        for h in (2 * hp, 2 * hp + 1):
                            o = PS[b][:, 256 * (h % 2):256 * (h % 2) + 256]
                            v = slice(256 * h, 256 * h + 256)
                            if t == 0:
                                seq += [(o, PM[:, h, 0:128], VV[:, 0, v], True, True)]
                            else:
                                seq += [(o, PM[:, h, 128:256], VV[:, 0, v], True, False),
                                        (o, PM[:, h, 256:384], VV[:, 1, v], False, True)]
                        to[t, hp] = mms(seq, PF[b], tp, list(tv.values()))
                        yield
                spare_rooms(0, tuple(to.values()))
                yield from head_norm(ob, to, None, YN, res)
                while (0, 1) not in r:
                    yield
                for t in range(2):
                    y, o, e = r[0, t]
                    ty.append(tt(y, y, o, MUL, e, res[t, 0]))

            def sink_qk(n, p, m):
                dst = (QT if n < 2 else KT)[:, 2 * (n % 2):2 * (n % 2) + 2, :]
                e = act(dst, p.rearrange("p (h i) -> p h i", h=2), ACT.Copy, m, scale=128 ** -0.5 if n < 2 else 1.0)
                qk.append(e)
                return (e,)

            def sink_v(n, t, p, m):
                e = act(VV[:, t, 512 * n:512 * n + 512], p, ACT.Copy, m, r["lb"])
                tv[n, t] = e
                return (e,)

            def sink_r(n, t, p, m):
                o = SR[:, t, 512 * n:512 * n + 512]
                e = act(o, p, ACT.Tanh, m, scale=0.5)
                e = stt(o, o, 1.0, p, ADD, MUL, e)
                y = YN[:, t, 512 * n:512 * n + 512]
                r[n, t] = (y, o, e)
                if n == 1:
                    ty.append(tt(y, y, o, MUL, e, res[t, n]))
                return (e,)

            def gate_first():
                drain()
                for g in range(2):
                    turn_heads(g, YN, halfg[:, 0:8], tuple(ty), tO)

            tO = []
            side.append(prepare())
            linear_a(8, 8, tT, sink_qk, tick=advance)
            linear_b(2, 8, tT, sink_v, tick=advance)
            side.append(values())
            linear_b(2, 8, tT, sink_r, tick=lambda: advance(2), last=gate_first, staggered=True)
            tgb = ln_rows(0, 0, LNG, r["scores"])

            def second_half():
                for g in (2, 3):
                    turn_heads(g, YN, halfg[:, 0:8], ty[2:], tO)

            tz = mix_out(tO, tX, second_half)
            return tz, tgb, tO

        LNG = ar(2048, 2048)

        def moe(i, tx, tf, free_x, extra):
            nonlocal st
            XG = T2[:, :].rearrange("p (e k s) -> p e k s", e=4, k=8)
            PTR = [ar(8192 + 512 * n, 2, 256, dt=F32R) for n in range(2)]
            G2 = ar(9216, 4, 2, 64, dt=F32R)
            RS = [ar(9728, 512), ar(10240, 512)]
            GF = ar(9728, 256)
            TW = ar(10752, 2, 2, 2, 64, dt=F32R)
            YH, YL = ar(11264, 1024, dt=F32R), ar(12288, 1024, dt=F32R)
            GB = ar(15360, 2048)
            CMP = ar(9216, 256)
            XH, XL = ar(0, 2, 1024, dt=F32R), XR[:, :, :]
            PR = FR[:, :].rearrange("p (t e s) -> p t e s", t=2, e=16)

            tXH = [act(XH[:, q, :], X[:, q, :], ACT.Copy, tx[q], free_x) for q in range(2)]
            tXL = {}
            st["room"].update({n: tx for p, n, _ in small["spare"][i] if p == 6})
            issue()

            def lo_parts(n):
                w = slice(512 * n, 512 * n + 512)
                tXL[n] = [tt(XL[:, q, w], X[:, q, w], XH[:, q, w], SUB, tXH[q], free_x) for q in range(2)]

            for _ in range(2):
                next(extra, None)
            rt = VE["router"].rearrange("p (k e) -> p k e", k=8)
            b = take()
            for g in range(4):
                m = mms([(PS[b][:, 64 * q:64 * q + 64].rearrange("p (r e) -> p r e", e=16), F[:, k, 128 * q:128 * q + 128],
                          rt[:, k, :].unsqueeze(1).broadcast_to([128, 4, 16]), k == q == 0, k == 7)
                         for k in (2 * g, 2 * g + 1) for q in range(2)], tf[g], PF[b])
            aff, gate, sel = tiny("m_aff", 32), tiny("m_gate", 32), SEL[:, :]
            logits = PS[b][:, 0:128].rearrange("p (q r) -> p q r", q=2)[:, :, 0:16]
            t = act(aff.rearrange("p (q e) -> p q e", q=2), logits, ACT.Tanh, m, scale=0.5)
            give(b, t)
            t_aff = ts(aff, aff, 0.5, 0.5, MUL, ADD, t)
            pinned = [take() for _ in range(4)]
            YB = {(t, n): pinned[2 * t + n] for t in range(2) for n in range(2)}
            AH, AL = ar(9472, 128, dt=F32R), ar(9600, 128, dt=F32R)
            t_ah = act(AH, ident, ACT.Copy, free_x, scale=ALPHA)
            t_al = stt(AL, ident, ALPHA, AH, MUL, SUB, t_ah)

            def residual(parts, x, *after):
                mms([(PS[YB[t, n]][:, :], w, x[:, t, 512 * n:512 * n + 512], k == 0 and x is XH, False)
                     for t in range(2) for n in range(2) for k, w in enumerate(parts)], after, [PF[p] for p in pinned])

            residual([AH, AL], XH, t_al, tXH)
            BO = T2[:, 0:256]
            b0 = small["cst"][0]["before"][0]
            t_bo = act(BO, cst[:, b0:b0 + 256], ACT.Copy, tx)

            def ranks(v, n, o, more, *after):
                a = v.rearrange("p (g e) -> p g e", e=n)
                shape = [128, more, n, n]
                x4 = CMP[:, 0:more * n * n].rearrange("p (g e f) -> p g e f", e=n, f=n)
                other, own = a.unsqueeze(2).broadcast_to(shape), a.unsqueeze(3).broadcast_to(shape)
                bar = C["bar"].rearrange("p (e f) -> p e f", e=n).unsqueeze(1).broadcast_to(shape)
                t = tt(x4, other, own, SUB, *after)
                t = tt(x4, x4, bar, ALU.is_gt, t)
                return red(o.rearrange("p (g e) -> p g e", e=n), x4, ADD, t)

            rk, gs, gk = tiny("m_rk", 32), tiny("m_gs", 8), tiny("m_gk", 8)
            t = ranks(aff, 4, rk, 8, t_aff, free_x)
            t = stt(gate, rk, 2.0, aff, ALU.is_lt, MUL, t)
            t = red(gs, gate.rearrange("p (g e) -> p g e", e=4), ADD, t)
            t = ranks(gs, 4, gk, 2, t)
            t = ts(gk, gk, 1.0, None, ALU.is_lt, NOP, t)
            own = gk.unsqueeze(2).broadcast_to([128, 8, 4])
            t_sel = stt(sel.rearrange("p (g e) -> p g e", e=4), rk.rearrange("p (g e) -> p g e", e=4), 2.0, own,
                        ALU.is_lt, MUL, t)
            b, bm = take(), take()
            m = mms([(PS[b][:, 0:16], BO[:, 0:128], sel[:, 0:16], True, True),
                     (PS[b][:, 16:32], BO[:, 128:256], sel[:, 0:16], True, False),
                     (PS[b][:, 16:32], BO[:, 0:128], sel[:, 16:32], False, True)], PF[b], t_sel, t_bo)
            mc = mms([(PS[bm][:, 0:16], BO[:, 128:256], sel[:, 0:16], True, False),
                      (PS[bm][:, 0:16], BO[:, 128:256], sel[:, 16:32], False, True)], PF[bm])
            lo_parts(0)
            pm, most = tiny("m_pm", 32), tiny("m_most", 1)
            t_pm = stt(pm, PS[b][:, 0:32], 1.0, sel.bitcast(F32), ADD, MUL, m)
            give(b, t_pm)

            def one_hot(g, *after):
                return [tt(PR[:, q, 4 * g:4 * g + 4, :], C["slots"].unsqueeze(1).broadcast_to([128, 4, 64]),
                           pm[:, 16 * q + 4 * g:16 * q + 4 * g + 4].unsqueeze(2).broadcast_to([128, 4, 64]), ALU.is_equal,
                           *after) for q in range(2)]

            tP = {0: one_hot(0, t_pm)}
            lo_parts(1)
            list(extra)

            def gates():
                t = red(most, PS[bm][:, 0:16], MAX, mc)
                give(bm, t)
                t_flag = ts(FLAG[0:1, i:i + 1], most[0:1, :], 64.0, None, ALU.is_gt, NOP, t)
                parts[i] = {n: Part(f"full{i}_{n}", FLAG[0:1, i:i + 1], (t_flag,))
                            for n in ("sync", "act", "dve", "pool", "pe")}
                t = tt(gate.rearrange("p (g e) -> p g e", e=4), gate.rearrange("p (g e) -> p g e", e=4), own, MUL, t_sel)
                den = tiny("m_den", 2)
                t = red(den, gate.rearrange("p (t e) -> p t e", t=2), ADD, t)
                t = inv(den, den, t)
                t = tt(gate.rearrange("p (t e) -> p t e", t=2), gate.rearrange("p (t e) -> p t e", t=2),
                       den.unsqueeze(2).broadcast_to([128, 2, 16]), MUL, t)
                t = cp(ghl[:, :, 0], gate, t, free_x)
                t_gate.append(tt(ghl[:, :, 1], gate, ghl[:, :, 0], SUB, t))

            t_gate = []
            ghl = GHL[:, :].rearrange("p (n h) -> p n h", h=2)
            GS = tiny("m_gs16", 16)

            tA, tU, tR, tT, tC, tS, tG, tY, tGF, tGS = {}, {}, {}, {}, {}, {}, {}, {}, {}, {}
            tXG, tPT, tTW, tSM, tM, tSC = {}, {}, {}, {}, {}, {}

            def gather(g, k):
                b = take()
                m = mms([(PS[b][:, 256 * hl:256 * hl + 256], src[:, q, 128 * k:128 * k + 128],
                          PR[:, q, 4 * g:4 * g + 4, :], q == 0, q == 1)
                         for hl, src in enumerate((XH, XL)) for q in range(2)], PF[b], tP[g], tXL[k // 4])
                o = XG[:, :, k, :].rearrange("p e (h s) -> p h e s", h=2)
                src = PS[b][:, :].rearrange("p (h e s) -> p h e s", h=2, e=4)
                ok = tU[4 * g - 1, k // 2] if g else ()

                def out():
                    tXG[g, k] = cp(o, src, m, ok) if g == 0 and k % 2 and k > 1 else act(o, src, ACT.Copy, m, ok)
                    give(b, tXG[g, k])

                return out

            def double(e):
                for q in range(2):
                    o = TW[:, q, :, :, :]
                    s = PR[:, q, e:e + 2, :].unsqueeze(2).broadcast_to([128, 2, 2, 64])
                    t = G(lambda en, o=o, s=s: en.tensor_copy(o, s), tP[e // 4], tx, tPT.get(e - 1, ()))
                tTW[e] = tTW[e + 1] = t

            def twice(e, q):
                return TW[:, q, e % 2, :, :].rearrange("p d s -> p (d s)")

            def maps(e):
                b = take()
                m = mms([(PS[b][:, 256 * d + 128 * q:256 * d + 128 * q + 128], twice(e + d, q), IDR[:, :], True, True)
                         for d in range(2) for q in range(2)], PF[b], tTW[e], ready["idr"])

                def out():
                    tSM[e] = tSM[e + 1] = act(PTR[e // 2 % 2], PS[b][:, :].rearrange("p (d i) -> p d i", d=2), ACT.Copy,
                                              m, tS.get(e - 3, ()))
                    give(b, tSM[e])
                    if e == 0:
                        both(0)

                return out

            def both(e):
                t = G(lambda en: en.tensor_copy(PTC[:, :], PTR[e // 2 % 2][:, 0, :]), tSM[e], tS.get(e - 1, ()))
                tSC[0] = G(lambda en: en.tensor_copy(PTC[64:128, :], PTR[e // 2 % 2][64:128, 1, :]), t)
                G.bare(lambda en: en.nop(), tSC[0])

            def gains(e):
                b = take()
                m = mms([(PS[b][:, 2 * d:2 * d + 2], twice(e + d, q), ghl[:, 16 * q + e + d, :], q == 0, q == 1)
                         for d in range(2) for q in range(2)], PF[b], t_gate, tTW[e])
                tPT[e] = tPT[e + 1] = m

                def out():
                    two = PS[b][:, 0:4].rearrange("p (d h) -> p d h", h=2)
                    tGS[e] = tGS[e + 1] = red(GS[:, e:e + 2], two, ADD, m)
                    give(b, tGS[e])
                    if e == 14 and first:
                        tgb.append(ln_rows(i, 1, GB, m, tXG[0, 0], lent[5]))
                    if e + 2 < 16:
                        double(e + 2)

                return out

            def product(o, x, h, l, first, last):
                if l is None:
                    return [(o, x.bitcast(F32), h, first, last)]
                return [(o, x, h, first, False), (o, x, l, False, last)]

            def up_out(e, n, b, m):
                tR[e, n] = act(RS[n], PS[b][:, :], ACT.Copy, m, tT.get((e - 1, n), ()), tG.get(e - 1, ()), t_gate, tx)
                give(b, tR[e, n])

            def up(e, job):
                for n in range(2):
                    b = take()
                    for uu in range(4):
                        u, h, l, tok = unit()
                        seq = []
                        for j in range(2):
                            k = 2 * uu + j
                            w = slice(512 * j, 512 * j + 512)
                            seq += product(PS[b][:, :], XG[:, e % 4, k, :], h[:, w], None if l is None else l[:, w],
                                           k == 0, k == 7)
                        m = mms(seq, tok, [tXG[e // 4, k] for k in (2 * uu, 2 * uu + 1)], PF[b] if uu == 0 else ())
                        used(u, m)
                        tU[e, uu] = m
                        if uu == 3:
                            if e == 15 and n == 1:
                                later(True)
                                up_out(e, n, b, m)
                            else:
                                sums.append([0, lambda b=b, m=m, n=n: up_out(e, n, b, m)])
                        job(4 * n + uu)
                tA[e] = m

            def turned(e):
                return XG[:, 0, 0:4, :].rearrange("p k (h s) -> p k h s", h=2) if e == 15 else G2

            def fold(e, n):
                b = take()
                r = RS[n]
                m = mms([(PS[b][:, 64 * f:64 * f + 64], r[:, 128 * f:128 * f + 128], C["fold"], True, True)
                         for f in range(4)], PF[b], tR[e, n])
                tT[e, n] = m
                gf = GF

                g3 = gf.rearrange("p (f s) -> p f s", f=4)

                def first_out():
                    t = act(gf, PS[b][:, 0:256], ACT.Tanh, m, scale=0.5)

                    def last():
                        tGF[e] = stt(gf, gf, 1.0, PS[b][:, 0:256], ADD, MUL, t)
                        give(b, tGF[e])
                    return last

                def second_out():
                    t = stt(gf, gf, 0.5, PS[b][:, 0:256], MUL, MUL, m, tGF[e])
                    give(b, t)

                    def hi_part():
                        gh, gl = turned(e)[:, :, e % 2, :], turned(e)[:, :, 1 - e % 2, :]
                        th = act(gh, g3, ACT.Copy, t, tC.get(e - 1, ()) if e < 15 else ())

                        def lo_part():
                            tG[e] = tt(gl, g3, gh, SUB, th)
                        return lo_part
                    return hi_part

                return (first_out, second_out)[n]

            def down_out(e, b, m, n):
                yh, r = YH[:, 512 * n:512 * n + 512], slice(64 * (e % 2), 64 * (e % 2) + 64)
                th = act(yh, PS[b][:, :], ACT.Copy, m, tGS[e], tS.get(e - 1, lent[3] if first else ()), tY[e - 1][n] if e else (),
                         scale=GS[:, e:e + 1])

                def lo_part():
                    tl = stt(YL[r, 512 * n:512 * n + 512], PS[b][r, :], GS[r, e:e + 1], yh[r, :], MUL, SUB, th)
                    give(b, tl)
                    tY[e].append((th, tl))
                return lo_part

            def down(e, job):
                tY[e] = []
                for n in range(2):
                    b = take()
                    for uu in range(2):
                        u, h, l, tok = unit()
                        seq = []
                        for j in range(2):
                            k = 2 * uu + j
                            w = slice(512 * j, 512 * j + 512)
                            seq += product(PS[b][:, :], turned(e)[:, k, :, :].rearrange("p h s -> p (h s)"), h[:, w],
                                           None if l is None else l[:, w], k == 0, k == 3)
                        m = mms(seq, tok, tG[e], PF[b] if uu == 0 else ())
                        used(u, m)
                        if uu == 1:
                            sums.append([0, lambda b=b, m=m, n=n: down_out(e, b, m, n)])
                        job(8 + 2 * n + uu)
                tC[e] = m

            def scatter(e, n):
                seq = []
                for t in range(2):
                    w = PTR[e // 2 % 2][:, e % 2, 128 * t:128 * t + 128]
                    o = PS[YB[t, n]][:, :]
                    seq.append((o, w, YH[:, 512 * n:512 * n + 512], False, False))
                    if e % 2:
                        seq.append((o, PTC[:, 128 * t:128 * t + 128], YL[:, 512 * n:512 * n + 512], False, e == 15))
                if e % 2:
                    tS[e] = tM[n] = mms(seq, tY[e - 1][n][1], tY[e][n], tSC[0])
                    if n and e < 15:
                        both(e + 1)
                else:
                    tS[e] = mms(seq, tY[e][n][0], tSM[e])

            def experts():
                def plan(e):
                    jobs = {n: [] for n in range(12)}
                    if e > 1:
                        at = (3, 5) if e < 16 else (8, 9)
                        for n in range(2):
                            jobs[at[n]].append(lambda n=n: scatter(e - 2, n))
                    if e < 16:
                        if e == 0:
                            for n in range(2):
                                jobs[n] += [lambda n=n: (gather(0, 2 * n + 4)(), gather(0, 2 * n + 5)())]
                            if first:
                                jobs[1].append(gates)
                        if e in (1, 5, 9) and first:
                            jobs[6].append(lambda: tP.update({e // 4 + 1: one_hot(e // 4 + 1, t_pm)}) or ())
                        if e % 4 == 3 and e < 12:
                            for k, n in enumerate((4, 5, 5, 6, 6, 7, 8, 9)):
                                jobs[n].append(lambda k=k: gather(e // 4 + 1, k))
                        if e % 2 == 0:
                            jobs[3 if e == 0 else 2].append(lambda: maps(e))
                            jobs[4 if e == 0 else 3].append(lambda: gains(e))
                        if e == 0 and first:
                            jobs[3].append(lambda: residual([AH], XL, tXL[0], tXL[1]))
                        jobs[5].append(lambda: fold(e, 0))
                        if e == 15:
                            jobs[7].append(lambda: tail.append(fold(15, 1)()()))
                            jobs[8].append(lambda: tail.pop()())
                        else:
                            jobs[10 if e else 7].append(lambda: fold(e, 1))
                        if e == 0:
                            jobs[7].insert(0, lambda: later(True))

                    def job(n):
                        for fn in jobs[n]:
                            more = fn()
                            if callable(more):
                                sums.append([0, more])
                    return job

                tail = []
                for k in range(4):
                    gather(0, k)()
                double(0)
                for e in range(17):
                    job = plan(e)
                    if e == 16:
                        later(True)
                    if e < 16:
                        up(e, job)
                    if e:
                        down(e - 1, job)
                later(True)
                for n in range(2):
                    scatter(15, n)

            first, tgb = True, []
            lent = {p: st["left"].setdefault(max(c for c in st["uses"][NR + p] if c <= last), [])
                    for p, _, last in small["spare"][i]}
            experts()
            first = False
            t_main, t_up = dict(tM), tA[15]

            queues = {"sync": Y, "act": S, "dve": V, "pool": G, "pe": P}
            now = [(q.sem, q.n) for q in (P, S, V, G)]
            main, banks, order = st, list(PF), list(free)
            PF[:] = [()] * 8
            for n, q in queues.items():
                q.enter(sem(f"s_x{i}_{n}"))
            for n, q in queues.items():
                q.bare(lambda e: e.nop(), now)
            st = stream(3 * small["moe"][i], [sem(f"s_x{i}_raw{n}") for n in range(NR)], {})
            issue()
            for _ in range(3):
                for d in (tA, tU, tR, tT, tC, tS, tG, tY, tGF, tGS, tXG, tPT, tTW, tSM):
                    d.clear()
                done = [(q.sem, q.n) for q in (P, S, V, G) if q.n]
                t = ts(pm, pm, 64.0, None, SUB, NOP, done)
                tP = {g: one_hot(g, t, done) for g in range(4)}
                experts()
            done = [(q.sem, q.n) for q in (P, S, V, G)]
            ln_rows(i, 1, GB, done)
            done = [(q.sem, q.n) for q in (P, S, V, G)]
            for n, q in queues.items():
                q.bare(lambda e: e.nop(), done)
                part = parts[i][n]
                part.sem, part.items = q.leave()
                if n != "sync":
                    q.items.append(part)
            st, PF[:], free[:] = main, banks, order
            ada_tok["acc", 0] = lent[0]
            st["stops"] = {c: n for c, n in st["stops"].items() if n != i}
            tz = []
            for n in range(2):
                for t in range(2):
                    tz.append(ln_piece(t, n, PS[YB[t, n]][:, :], t_main[n]))
            return tz, tgb, GB, YB, t_up

        def mlstm(tx, tT, rest):
            CV, VV, SO = ar(0, 16, 256), ar(4096, 2, 1024), ar(6144, 2, 1024)
            PT, W = ar(8192, 4, 384), ar(9728, 4, 384)
            YN = ar(11264, 2, 1024)
            TQ = ar(6144, 2, 512)
            RO = [ar(7168 + 256 * n, 256) for n in range(2)]
            tcv, tw, tv, ty, res, r = {}, [], {}, [], {}, {}
            tO, tgb = [], []
            em = tiny("l_em", 8, 2)

            def gates():
                yield
                b = take()
                mg = VE["mgate"].rearrange("p (k e) -> p k e", k=8)
                m = mms([(PS[b][0:8, 0:256], mg[:, k, :], F[:, k, :], k == 0, k == 7) for k in range(8)], PF[b], tT)
                t = act(RO[1][0:8, :], PS[b][0:8, 0:256], ACT.Identity, m, bias=VE["mbias"][0:8, :])
                give(b, t)
                yield
                b = take()
                m = mms([(PS[b][:, 8 * q_:8 * q_ + 8], RO[1][0:8, 128 * q_:128 * q_ + 128], ident[0:8, 0:8], True, True)
                         for q_ in range(2)], PF[b], t)
                gt = PS[b][:, 0:16].rearrange("p (t g) -> p t g", t=2)
                fg, it, th, z, q, lf = (tiny(f"l_{n}", 8, 2) for n in ("fg", "it", "th", "z", "q", "lf"))
                t = cp(fg, gt[:, :, 4:8], m)
                ti = cp(it, gt[:, :, 0:4], m)
                give(b, ti)
                yield
                t = stt(th, fg, -1.0, fg, MUL, MAX, t)
                t = act(th, th, ACT.Tanh, t, scale=0.5)
                t1 = ts(z, th, 3.0, None, ADD, NOP, t)
                t1 = inv(z, z, t1)
                t = ts(th, th, -1.0, 1.0, MUL, ADD, t, t1)
                t = tt(th, th, z, MUL, t, t1)
                t = tt(z, th, th, MUL, t)
                yield
                t = ts(q, z, 1.0 / 17.0, None, MUL, NOP, t)
                for n in (15, 13, 11, 9, 7, 5, 3):
                    t = stt(q, q, 1.0 / n, z, ADD, MUL, t)
                t = stt(q, q, 1.0, th, ADD, MUL, t)
                t = ts(q, q, -2.0, None, MUL, NOP, t)
                t = stt(lf, fg, 0.0, q, MIN, ADD, t)
                yield
                yield
                causal = C["tri3"][:, 0:128]
                b = take()
                m = mms([(PS[b][:, 0:4], causal, lf[:, 0, :], True, True),
                         (PS[b][:, 4:8], C["ones"], lf[:, 0, :], True, False),
                         (PS[b][:, 4:8], causal, lf[:, 1, :], False, True)], PF[b], t)
                bc, aj = tiny("l_bc", 8, 2), tiny("l_aj", 8, 2)
                t = cp(bc, PS[b][:, 0:8].rearrange("p (t h) -> p t h", t=2), m)
                give(b, t)
                t_aj = tt(aj, it, bc, SUB, t, ti)
                yield
                b = take()
                m = turns([(PS[b][0:4, 128 * q_:128 * q_ + 128], aj[:, q_, :]) for q_ in range(2)], PF[b], t_aj)
                t = cp(RO[0][0:4, :], PS[b][0:4, 0:256], m)
                give(b, t)
                yield
                cur = 0
                for sh in (1, 2, 4, 8, 16, 32, 64, 128):
                    a, o = RO[cur][0:4, :], RO[1 - cur][0:4, :]
                    t1 = cp(o[:, 0:sh], a[:, 0:sh], t)
                    t2 = tt(o[:, sh:256], a[:, sh:256], a[:, 0:256 - sh], MAX, t)
                    t = (t1, t2)
                    cur = 1 - cur
                    if sh in (4, 32):
                        yield
                MR = RO[cur]
                yield
                yield
                b = take()
                m = mms([(PS[b][:, 4 * q_:4 * q_ + 4], MR[0:4, 128 * q_:128 * q_ + 128], ident[0:4, 0:4], True, True)
                         for q_ in range(2)], PF[b], t)
                t2 = tt(em, bc, PS[b][:, 0:8].rearrange("p (t h) -> p t h", t=2), ADD, m)
                give(b, t2)
                r["em"] = act(em, em, ACT.Exp, t2, scale=-1.0)
                tp = []
                for hp in range(2):
                    b = take()
                    m = mms([(PS[b][:, 256 * hh:256 * hh + 256],
                              ident[0:4, 2 * hp + hh:2 * hp + hh + 1].broadcast_to([4, 128]),
                              MR[0:4, :], True, True) for hh in range(2)], PF[b], t)
                    for hh in range(2):
                        h = 2 * hp + hh
                        p = PS[b][:, 256 * hh:256 * hh + 256]
                        tp.append(ts(PT[:, h, 0:256], p, aj[:, 0, h:h + 1], 0.0, SUB, MAX, m, t_aj))
                        tp.append(ts(PT[:, h, 256:384], p[:, 128:256], aj[:, 1, h:h + 1], 0.0, SUB, MAX, m, t_aj))
                    give(b, tp[-1])
                    yield
                t = act(PT, PT, ACT.Exp, tp, scale=-1.0)
                yield
                r["pt"] = tt(PT, PT, C["tri3"].unsqueeze(1).broadcast_to([128, 4, 384]), MUL, t)
                yield

            cw = VE["conv_w"].rearrange("p (j m) -> p j m", j=4)
            cb = VE["conv_b"]

            def sink_qk(n, p, m):
                tk = []
                for i in range(2):
                    mt = 2 * n + i
                    tk.append(act(CV[:, mt, :], p[:, 256 * i:256 * i + 256], ACT.Identity, m,
                                  scale=cw[:, 3, mt:mt + 1], bias=cb[:, mt:mt + 1]))
                tk = [tk[1], tk[1]]
                for j in (1, 2, 3):
                    for i in range(2):
                        mt = 2 * n + i
                        o = CV[:, mt, j:256]
                        tk[i] = stt(o, p[:, 256 * i:256 * i + 256 - j], cw[:, 3 - j, mt:mt + 1], o, MUL, ADD, tk[i])
                c2 = CV[:, 2 * n:2 * n + 2, :]
                q2 = TQ[:, n % 2, :].rearrange("p (i j) -> p i j", i=2)
                t = act(q2, c2, ACT.Tanh, tk, tcv.get(n - 2, ()), scale=0.5)
                tcv[n] = stt(c2, q2, 1.0, c2, ADD, MUL, t)
                return (tk[1],)

            def scores():
                for h in range(4):
                    while 2 * h + 1 not in tcv:
                        yield
                    yield
                    b = take()
                    seq = []
                    for o, w, js in ((0, 256, slice(0, 128)), (256, 128, slice(128, 256))):
                        for kk in range(2):
                            seq.append((PS[b][:, o:o + w], CV[:, 4 * h + 2 + kk, js], CV[:, 4 * h + kk, 256 - w:256],
                                        kk == 0, kk == 1))
                    m = mms(seq, PF[b], tcv[2 * h], tcv[2 * h + 1])
                    d = stt(W[:, h, :], PS[b][:, 0:384], 1.0 / 64.0, PT[:, h, :], MUL, MUL, m, r["pt"])
                    give(b, d)
                    tw.append(d)
                    yield
                r["cv"] = m

            def values():
                ob, to = {}, {}
                bd = take()
                td = []
                one = C["ones"][:, 0:1]
                for hp in range(2):
                    for t in range(2):
                        b = ob[t, hp] = take()
                        seq, den = [], []
                        for h in (2 * hp, 2 * hp + 1):
                            o = PS[b][:, 256 * (h % 2):256 * (h % 2) + 256]
                            d = PS[bd][:, 4 * t + h:4 * t + h + 1]
                            v = slice(256 * h, 256 * h + 256)
                            if t == 0:
                                seq += [(o, W[:, h, 0:128], VV[:, 0, v], True, True)]
                                den += [(d, W[:, h, 0:128], one, True, True)]
                            else:
                                seq += [(o, W[:, h, 128:256], VV[:, 0, v], True, False),
                                        (o, W[:, h, 256:384], VV[:, 1, v], False, True)]
                                den += [(d, W[:, h, 128:256], one, True, False), (d, W[:, h, 256:384], one, False, True)]
                        td.append(mms(den, PF[bd], tw))
                        to[t, hp] = mms(seq, PF[b], tw, list(tv.values()))
                        next(rest)
                        yield
                ab, rd = tiny("l_ab", 8), tiny("l_rd", 8)
                t = cp(ab, PS[bd][:, 0:8], td[-1], tx)
                give(bd, t)
                t = stt(ab, ab, -1.0, ab, MUL, MAX, t)
                t = tt(ab, ab, em.rearrange("p t h -> p (t h)"), MAX, t, r["em"])
                t = inv(rd, ab, t)
                yield
                yield from head_norm(ob, to, (rd, t), YN, res)
                while (0, 1) not in r:
                    yield
                for t in range(2):
                    y, o, e = r[0, t]
                    ty.append(stt(y, o, 1.0, y, ADD, MUL, e, res[t, 0]))

            def sink_v(n, t, p, m):
                e = act(VV[:, t, 512 * n:512 * n + 512], p, ACT.Copy, m)
                tv[n, t] = e
                return (e,)

            def sink_o(n, t, p, m):
                o = SO[:, t, 512 * n:512 * n + 512]
                e = act(o, p, ACT.Tanh, m, scale=0.5)
                y = YN[:, t, 512 * n:512 * n + 512]
                r[n, t] = (y, o, e)
                if n == 1:
                    ty.append(stt(y, o, 1.0, y, ADD, MUL, e, res[t, n]))
                return (e,)

            def gate_first():
                drain()
                tgb.append(ln_rows(1, 0, LNG, r["cv"]))
                for g in range(2):
                    turn_heads(g, YN, halfg[:, 8:16], tuple(ty), tO)

            side.append(gates())
            linear_b(2, 8, tT, sink_v, tick=advance)
            side.append(scores())
            linear_a(16, 8, tT, sink_qk, tick=advance)
            side.append(values())
            linear_b(2, 8, tT, sink_o, tick=lambda at=iter((0, 1, 2) + 13 * (3,)): advance(next(at)), last=gate_first,
                     staggered=True)

            def second_half():
                for g in (2, 3):
                    turn_heads(g, YN, halfg[:, 8:16], ty[2:], tO)
                spare_rooms(1, tuple(tO))

            tz = mix_out(tO, tx, second_half)
            return tz, tgb, tO

        def block2(l, tx, prior, tsq, extra=None):
            QK = ar(0, 17, 256)
            VB = ar(4352, 2, 896)
            ST = [ar(6144 + 1024 * n, 2, 512) for n in range(2)]
            RT = [ar(8192 + 1024 * n, 2, 512) for n in range(2)]
            BB = ar(10240, 2, 512)
            GA = ar(11264, 16, 256)
            TG = ar(15360, 8, 2, 2, 64)
            TB, GN = ar(11264, 2, 2, 2, 64), ar(11264 + 512, 8, 2, 64)
            spots = [ar(6144 + 512 * n, 2, 256) for n in range(10)] + [ar(15360 + 512 * n, 2, 256) for n in range(4)]
            PB, PTT = spots[0:8], spots[8:14]
            FF = F[:, :, :].rearrange("p a b -> p (a b)")
            MK = FF[:, 0:1536].rearrange("p (g i) -> p g i", g=3)
            DG = FF[:, 1024:2048].rearrange("p (j i) -> p j i", j=8)
            OH, OL = ar(1280, 6, 256, dt=F32R), ar(2816, 6, 256, dt=F32R)
            MH, ML = TH, TL
            GT = ar(15360, 2, 1024)
            ZT = [ar(6144 + 512 * n, 512) for n in range(4)]
            XN = ar(8192, 2, 1024)
            RR = [ar(512 * n, 512) for n in range(2)]
            RH = [ar(1024 + 512 * n, 2, 256, dt=F32R) for n in range(2)]
            RL = [ar(2048 + 512 * n, 2, 256, dt=F32R) for n in range(2)]
            SQ = [ar(13312 + 1024 * n, 2, 512) for n in range(2)]
            ada = ADA[:, l, :]

            def rms_T(gcol, sc, sh, blk, tsq, wait, extra=None):
                ss, rs, scg = tiny("b_ss", 2), tiny("b_rs", 2), tiny("b_scg", 8)
                extra = extra or ahead(3)
                outs = add_kept((l, blk + 1))
                t = tt(ss, SSP[:, :, 0], SSP[:, :, 1], ADD, tsq)
                t = ts(ss, ss, 1.0 / 1024.0, 1e-6, MUL, ADD, t)
                t = rsqrt(rs, ss, 2, "b_nr", t)
                xn = [[ts(XN[:, 0, w], X[:, 0, w], rs[:, 0:1], None, MUL, NOP, t, wait),
                       act(XN[:, 1, w], X[:, 1, w], ACT.Copy, t, wait, scale=rs[:, 1:2])]
                      for w in (slice(0, 512), slice(512, 1024))]
                for out in outs:
                    out()
                t_s = stt(scg, sc, 1.0, gcol, ADD, MUL, ada_tok[l, blk])
                xn = [x + [t_s] for x in xn]
                next(extra, None)
                done = transposed(XN, xn, scg, sh, True, wait)
                list(extra)
                return done

            tT, _ = rms_T(VE["g_mix"][:, 8 * l:8 * l + 8], ada[:, 8:16], ada[:, 0:8], 0, tsq, prior, extra)

            if l == 1:
                prior = (prior, ada_tok["acc", 1], ada_tok["acc", 2])

            t1 = gload(TB, D["rope"].rearrange("p (a b c d) -> p a b c d", a=2, b=2, c=2), prior)
            t2 = gload(GN[0:1, :, :, :], D["gains"][l:l + 1, :].rearrange("p (a b c) -> p a b c", a=8, b=2), prior)
            gflat = GN.rearrange("p a b c -> p (a b c)")
            t2 = G(lambda e: e.partition_broadcast(gflat, gflat[0:1, :]), t2)
            t_tab = []
            for kind in range(8):
                t_tab.append(tt(TG[:, kind, :, :, :], TB[:, 0 if kind < 2 else 1, :, :, :],
                                GN[:, kind, :, :].unsqueeze(2).broadcast_to([128, 2, 2, 64]), MUL, t1, t2, prior, q=G))
            t_mask = gload(MK, D["masks"].rearrange("p (g i) -> p g i", g=3), tT)

            segs = [([(0, 8, 0)], []), ([(0, 2, 1), (128, 4, 2)], [(384, 2, 0)]), ([(0, 4, 3)], [(256, 4, 128)]),
                    ([(0, 4, 4), (256, 4, 5)], []), ([(0, 4, 7)], [(256, 4, 384)]), ([(0, 4, 6)], [(256, 4, 640)])]
            t_qk, t_v, raws = {}, [], {}
            t_free = {"ST": [prior, prior], "RT": [prior, prior], "BB": prior, "SQ": [prior, prior]}
            npair, pending, LAG = [0], [], 2

            def sink_qkv(n, t, p, m):
                qk, vs = segs[n]
                w = sum(h for _, h, _ in qk) * 64
                par = n % 2
                for c, h, o in vs:
                    t_v.append(act(VB[:, t, o:o + 64 * h], p[:, c:c + 64 * h], ACT.Copy, m, prior))
                e = [act(ST[par][:, t, 0:w], p[:, 0:w], ACT.Copy, m, t_free["ST"][par]),
                     act(SQ[par][:, t, 0:w], p[:, 0:w], ACT.Square, m, t_free["SQ"][par])]
                raws.setdefault(n, []).extend(e)
                if t == 1:
                    side.append(rope(n))
                return (e[-1],)

            def rope(n):
                qk, _ = segs[n]
                nh = sum(h for _, h, _ in qk)
                w = nh * 64
                par = n % 2
                sv, rv = tiny(f"b_sv{par}", 16)[:, 0:2 * nh], tiny(f"b_rv{par}", 16)[:, 0:2 * nh]
                t = red(sv.rearrange("p (t h) -> p t h", t=2), SQ[par][:, :, 0:w].rearrange("p t (h d) -> p t h d", d=64),
                        ADD, raws[n])
                t_free["SQ"][par] = t
                t = ts(sv, sv, 1.0 / 64.0, 1e-6, MUL, ADD, t)
                yield
                t = rsqrt(rv, sv, 2 * nh, tiny(f"b_rn{par}", 32), t)
                yield
                x = ST[par][:, :, 0:w].rearrange("p t (h d) -> p t h d", d=64)
                t = tt(x, x, rv.rearrange("p (t h) -> p t h", t=2).unsqueeze(3).broadcast_to([128, 2, nh, 64]), MUL, t)
                yield
                done = []
                for c, h, kind in qk:
                    xx, rr, bb = (z[:, :, c:c + 64 * h] for z in (ST[par], RT[par], BB))
                    cg = TG[:, kind, 0, :, :].unsqueeze(2).broadcast_to([128, 2, h, 64])
                    done.append(tt(rr.rearrange("p q (h d) -> p q h d", d=64), xx.rearrange("p q (h d) -> p q h d", d=64),
                                   cg, MUL, t, t_tab, t_free["RT"][par]))
                    b = 2 if kind < 2 else 1
                    w_ = 32 // b
                    for s_ in range(2):
                        for i in range(b):
                            at = 2 * w_ * i
                            o, x_ = (z.rearrange("p q (h d) -> p q h d", d=64) for z in (bb, xx))
                            sg = TG[:, kind, 1, :, at + w_ * s_:at + w_ * s_ + w_].unsqueeze(2).broadcast_to([128, 2, h, w_])
                            done.append(tt(o[:, :, :, at + w_ * s_:at + w_ * s_ + w_],
                                           x_[:, :, :, at + w_ * (1 - s_):at + w_ * (1 - s_) + w_], sg,
                                           MUL, t, t_tab, t_free["BB"]))
                    yield
                t_free["ST"][par] = done[-1]
                t = tt(RT[par][:, :, 0:w], RT[par][:, :, 0:w], BB[:, :, 0:w], ADD, done)
                t_free["BB"] = t
                np_ = nh // 2
                sums.append([LAG, lambda: turn(npair[0], np_, par, t)])
                pending.append(n)
                yield

            def turn(first, np_, par, t):
                for p0 in range(0, np_, 2):
                    cnt = min(2, np_ - p0)
                    b = take()
                    m = turns([(PS[b][:, 256 * i + 128 * q:256 * i + 128 * q + 128],
                                RT[par][:, q, 128 * (p0 + i):128 * (p0 + i) + 128]) for i in range(cnt) for q in range(2)],
                              PF[b], t)
                    e = act(QK[:, first + p0:first + p0 + cnt, :],
                            PS[b][:, 0:256 * cnt].rearrange("p (k i) -> p k i", k=cnt), ACT.Copy, m, prior)
                    give(b, e)
                    for i in range(cnt):
                        t_qk[first + p0 + i] = e
                npair[0] = first + np_
                t_free["RT"][par] = m
                pending.pop(0)

            linear_b(6, 8, tT, sink_qkv, tick=lambda: advance(2))

            SC, D1, D2, TICK = 64 ** -0.5, 4, 6, 3
            heads = [("b", p, s_) for p in range(2) for s_ in range(2)] + [("a", p, s_) for p in range(4) for s_ in range(2)]
            QP, KP = [5, 9, 15], [7, 11, 13]
            tP_free, tT_free = [()] * 8, [()] * 6
            tmx, tO, hold = [(), ()], [], {}
            tga = []
            sets = []
            for i, (kind, p, s_) in enumerate(heads):
                if kind == "a":
                    sets.append((i, 0, 1, p, 4, s_ * 64, None))
                else:
                    sets += [(i, g, 3, QP[g] + p, KP[g] + p, 128 + 256 * g + 64 * (2 * p + s_), g) for g in range(3)]
            soft, pt_tok, bank_of = {}, {}, {}

            def attention():
                while pending:
                    yield
                t_rt = (t_free["RT"], t_free["ST"], t_free["BB"], t_tab)
                tP_free[:] = [t_rt] * 8
                tT_free[:] = [t_rt] * 6
                for j in range(len(sets) + D2):
                    if j < len(sets):
                        score(j)
                        yield
                    if 0 <= j - D1 < len(sets):
                        probs_T(j - D1)
                        yield
                    if j - D2 >= 0:
                        value(j - D2)
                        yield

            def spread(which, dg, after, ready):
                sec = (2, 5)[which]
                while (l, 1 + which) not in ada_tok:
                    yield
                td = [ts(dg[:, j, :], ident, ada[:, 8 * sec + j:8 * sec + j + 1], None, MUL, NOP,
                         ada_tok[l, 1 + which], after) for j in range(8)]
                yield
                for n in range(2):
                    b = take()
                    m = hold["dg", which] = mms([(PS[b][:, 128 * j:128 * j + 128], C["ones"], dg[:, 4 * n + j, :], True, True)
                                                 for j in range(4)], PF[b], td[4 * n:4 * n + 4])
                    e = act(GT[:, which, 512 * n:512 * n + 512], PS[b][:, :], ACT.Copy, m, ready)
                    give(b, e)
                    hold["gt", which, n] = e
                    yield

            def score(j):
                i, n, cnt, qp, kp, _, g = sets[j]
                kind, _, s_ = heads[i]
                rows = slice(64 * s_, 64 * s_ + 64)
                mx, sm = tiny(f"b_mx{i % 2}", 8), tiny(f"b_sm{i % 2}", 8)
                pb = PB[j % 8]
                b = bank_of[j] = take()
                m = mms([(PS[b][:, 256 * q:256 * q + 256], QK[rows, qp, 128 * q:128 * q + 128], QK[rows, kp, :], True, True)
                         for q in range(2)], PF[b], t_qk[qp], t_qk[kp])
                if kind == "a":
                    t = red(mx[:, 0:2], PS[b][:, :].rearrange("p (q k) -> p q k", q=2), MAX, m, tmx[i % 2])
                else:
                    for q in range(2):
                        t = V(lambda e, q=q: e.tensor_tensor_reduce(
                            pb[:, q, :], PS[b][:, 256 * q:256 * q + 256], MK[:, g, 256 * q:256 * q + 256],
                            1.0, -3e38, ADD, MAX, mx[:, 2 + 2 * n + q:3 + 2 * n + q]), m, tmx[i % 2], t_mask, tP_free[j % 8])
                    give(b, t)
                    if n < 2:
                        return
                    t = red(mx[:, 0:2], mx[:, 2:8].rearrange("p (g q) -> p q g", q=2), MAX, t)
                t = ts(mx[:, 0:2], mx[:, 0:2], -SC, None, MUL, NOP, t)
                te = []
                for k in range(cnt):
                    jj = j - cnt + 1 + k
                    for q in range(2):
                        o = PB[jj % 8][:, q, :]
                        src = PS[b][:, 256 * q:256 * q + 256] if kind == "a" else o
                        te.append(act(o, src, ACT.Exp, t, tP_free[jj % 8], scale=SC, bias=mx[:, q:q + 1],
                                      accum_out=sm[:, 2 + 2 * k + q:3 + 2 * k + q]))
                if kind == "a":
                    give(b, te[-1])
                    t = inv(sm[:, 0:2], sm[:, 2:4], te)
                else:
                    t = red(sm[:, 0:2], sm[:, 2:8].rearrange("p (g q) -> p q g", q=2), ADD, te)
                    t = inv(sm[:, 0:2], sm[:, 0:2], t)
                for k in range(cnt):
                    jj = j - cnt + 1 + k
                    soft[jj] = [ts(PB[jj % 8][:, q, :], PB[jj % 8][:, q, :], sm[:, q:q + 1], None, MUL, NOP, t)
                                for q in range(2)]
                tmx[i % 2] = soft[j][1]

            def probs_T(j):
                b = take()
                m = turns([(PS[b][:, 256 * k + 128 * q:256 * k + 128 * q + 128], PB[j % 8][:, q, 128 * k:128 * k + 128])
                           for q in range(2) for k in range(2)], PF[b], soft[j])
                tP_free[j % 8] = m
                pt_tok[j] = act(PTT[j % 6], PS[b][:, :].rearrange("p (k i) -> p k i", k=2), ACT.Copy, m, tT_free[j % 6])
                give(b, pt_tok[j])

            def value(j):
                i, n, cnt, _, _, vo, _ = sets[j]
                kind, p, s_ = heads[i]
                rows = slice(64 * s_, 64 * s_ + 64)
                if s_ == 0 and n == 0:
                    hold["b", i // 2] = take()
                b = hold["b", i // 2]
                m = mms([(PS[b][rows, 0:256], VB[:, k, vo:vo + 64], PTT[j % 6][:, k, :], n == 0 and k == 0,
                          n == cnt - 1 and k == 1) for k in range(2)],
                        PF[b] if s_ == 0 and n == 0 else (), pt_tok[j], t_v)
                tT_free[j % 6] = m
                if s_ == 1 and n == cnt - 1:
                    tile = p if kind == "a" else 4 + p
                    th = act(OH[:, tile, :], PS[b][:, 0:256], ACT.Copy, m)
                    tl = tt(OL[:, tile, :], PS[b][:, 0:256], OH[:, tile, :], SUB, th)
                    give(b, tl)
                    tO.append(tl)

            def sink_gate(n, p, m):
                e = act(GA[:, 2 * n:2 * n + 2, :], p.rearrange("p (k i) -> p k i", k=2), ACT.Tanh, m, t_tab, tuple(t_free["SQ"]), scale=0.5)
                tga.append(e)
                return (e,)

            side.append(attention())
            linear_a(16, 8, tT, sink_gate, tick=lambda: advance(4))

            while len(tO) < 2:
                advance()
            tu, tm = [], []

            def gated(n, p, m):
                g = GA[:, 2 * n:2 * n + 2, :]
                return stt(g, g, 1.0, p.rearrange("p (k i) -> p k i", k=2), ADD, MUL, m, tga)

            def sink_b(n, p, m):
                tu.append(gated(4 + n, p, m))
                return (tu[n],)

            linear_a(8, 2, [tuple(tO[:2])], sink_b, OH[:, 4:6, :], OL[:, 4:6, :], tick=lambda: advance(TICK))
            drain()
            t_att = (tO, tP_free, tT_free)

            def sink_a(n, p, m):
                g, a = GA[:, 8 + 2 * n:10 + 2 * n, :], GA[:, 2 * n:2 * n + 2, :]
                e0 = gated(n, p, m)
                e = tt(g, g, a, ADD, e0, tu[n])
                th = act(MH[:, 2 * n:2 * n + 2, :], g, ACT.Copy, e, scale=0.5)
                tm.append(stt(ML[:, 2 * n:2 * n + 2, :], g, 0.5, MH[:, 2 * n:2 * n + 2, :], MUL, SUB, th))
                return (e0,)

            side.append(spread(0, DG, (tT, t_att), t_att))
            advance()
            linear_a(8, 4, [tuple(tO[2:4]), tuple(tO[4:6])], sink_a, OH, OL, tick=advance)
            drain()
            if l == 0:
                ada_tok["acc", 1] = ada_tok["acc", 2] = tuple(tm)

            tx2, tsq2 = [], []

            def residual(which, n, t, p, deps):
                z = X[:, t, 512 * n:512 * n + 512]
                zt = ZT[2 * t + n]
                e0 = tt(zt, p, GT[:, which, 512 * n:512 * n + 512], MUL, deps)
                e1 = tt(z, z, zt, ADD, e0, tx)
                e2 = act(zt, z, ACT.Square, e1, accum_out=SSP[:, t, n:n + 1])
                return e0, e1, e2

            def sink_o(n, t, p, m):
                e0, e1, e2 = residual(0, n, t, p, (m, hold["gt", 0, n], t_att))
                tx2.append(e1)
                tsq2.append(e2)
                return (e0,)

            linear_b(2, 8, tm, sink_o, MH, ML, halved=True, staggered=True)

            tT, _ = rms_T(VE["g_mlp"][:, 8 * l:8 * l + 8], ada[:, 32:40], ada[:, 24:32], 2, tsq2,
                          (t_att, tO, hold["dg", 0]))
            DG2 = ar(4096, 8, 128)
            side.append(spread(1, DG2, tx2, t_att))

            pinned = [take() for _ in range(4)]
            tR, tD = {}, {}

            def ff_up(i):
                b = take()
                for w in range(2):
                    u, h, lw, tok = unit()
                    for g in range(4):
                        seq = []
                        for k in (2 * g, 2 * g + 1):
                            seq += three_w(PS[b][:, 256 * w:256 * w + 256], h[:, 128 * k:128 * k + 128],
                                           lw[:, 128 * k:128 * k + 128], TH[:, k, :], TL[:, k, :], k == 0, k == 7)
                        m = mms(seq, tok, tT[g], PF[b] if w == 0 and g == 0 else ())
                    used(u, m)
                r = RR[i % 2]
                t = act(r, PS[b][:, :], ACT.Relu, m, tR.get(i - 2, ()), tx2)
                give(b, t)
                t = tt(r, r, r, MUL, t)
                r2 = r.rearrange("p (w i) -> p w i", w=2)
                th = act(RH[i % 2], r2, ACT.Copy, t, tD.get(i - 2, ()))
                tR[i] = tt(RL[i % 2], r2, RH[i % 2], SUB, th)

            def down_product(i, w, t, n, h, lw):
                k = 2 * i + w
                return three(PS[pinned[2 * t + n]][:, :], RH[i % 2][:, w, 128 * t:128 * t + 128],
                             RL[i % 2][:, w, 128 * t:128 * t + 128], h[:, 512 * n:512 * n + 512],
                             lw[:, 512 * n:512 * n + 512], k == 0, k == 31)

            def ff_down(i):
                for w in range(2):
                    u, h, lw, tok = unit()
                    seq = []
                    for n in range(2):
                        for t in range(2):
                            seq += down_product(i, w, t, n, h, lw)
                    m = mms(seq, tok, tR[i], [PF[p] for p in pinned] if 2 * i + w == 0 else ())
                    used(u, m)
                tD[i] = m

            def ff_last():
                us = [unit(False) for w in range(2)]
                for t in range(2):
                    for n in range(2):
                        seq = []
                        for w in range(2):
                            seq += down_product(15, w, t, n, *us[w][1:3])
                        t_down[t, n] = mms(seq, us[0][3], us[1][3], tR[15])
                        emit_last(t, n)
                for w in range(2):
                    used(us[w][0], t_down[1, 1])

            for i in range(16):
                ff_up(i)
                if i:
                    advance()
                    ff_down(i - 1)
            t_down, tx3, tsq3 = {}, {}, []

            def emit_last(t, n):
                p = pinned[2 * t + n]
                e0, tx3[t, n], e2 = residual(1, n, t, PS[p][:, :], (t_down[t, n], hold["gt", 1, n], tsq2))
                give(p, e0)
                tsq3.append(e2)

            ff_last()
            tx3 = [[tx3[t, n] for n in range(2)] for t in range(2)]
            return tx3, (tx3, t_down[1, 1], tR[15]), tsq3

        SSP = tiny("b_ssp", 4, 2)
        def finish(tok):
            s = sem("s_out")
            for t in range(2):
                Y.bare(lambda e, t=t: e.dma_start(out[128 * t:128 * t + 128, :], X[:, t, :]).then_inc(s, 16), tok[t])
            Y.bare(lambda e: e.wait_ge(s, 32))

        def program():
            tz, tgb, tO = gla()
            tx, tf, extra = ln(0, 0, tz, LNG, tgb, None, ar(0, 2, 1024), tO, False, tO)
            tz, tgb, gb, zb, t_up = moe(0, tx, tf, tO, extra)
            tx, tT, rest = ln(0, 1, tz, gb, tgb, zb, ar(13312, 2, 1024), t_up, True, t_up)
            tz, tgb, tO = mlstm(tx, tT, rest)
            tx, tf, extra = ln(1, 0, tz, LNG, tgb, None, ar(0, 2, 1024), tO, False, tO)
            tz, tgb, gb, zb, t_up = moe(1, tx, tf, tO, extra)
            tx, _, extra = ln(1, 1, tz, gb, tgb, zb)
            tsq = [act(ar(0, 2, 1024)[:, t, 512 * n:512 * n + 512], X[:, t, 512 * n:512 * n + 512], ACT.Square, tx[t][n],
                       accum_out=SSP[:, t, n:n + 1]) for t in range(2) for n in range(2)]
            next(extra, None)
            prior = (tx, tsq)
            for l in range(2):
                tx, prior, tsq = block2(l, tx, prior, tsq, None if l else extra)
            return tx

        finish(program())
        block = ctx.enter_context(nc.Block())

        @block.sync
        def _(e):
            Y.emit(e)

        @block.scalar
        def _(e):
            S.emit(e)

        @block.vector
        def _(e):
            V.emit(e)

        @block.gpsimd
        def _(e):
            G.emit(e)

        @block.tensor
        def _(e):
            P.emit(e)
    return {"counts": {n: q.n for n, q in (("pe", P), ("act", S), ("dve", V), ("pool", G))}}


def _chunks(u):
    return np.ascontiguousarray(u.reshape(-1, 2, 128, 1024).transpose(0, 2, 1, 3)).reshape(-1, 2048)


def _stat(w):
    k, n = w.shape[0] // 128, w.shape[1] // 128
    u = w.reshape(k, 128, n, 128).transpose(2, 1, 0, 3)
    per = 8 // k
    u = u.reshape(n // per, per, 128, k, 128).transpose(0, 2, 1, 3, 4)
    return _chunks(u.reshape(-1, 128, 1024))


def _move(w):
    k, n = w.shape[0] // 256, w.shape[1] // 512
    return _chunks(w.reshape(k, 2, 128, n, 512).transpose(3, 0, 2, 1, 4).reshape(-1, 128, 1024))


def _halves(u):
    return np.ascontiguousarray(u.reshape(2, 2, -1, 2048).transpose(1, 0, 2, 3)).reshape(-1, 2048)


def _col(v):
    return np.ascontiguousarray(np.reshape(v, (-1, 128)).T)


def _table(parts):
    where, at = {}, 0
    for n, a in parts:
        where[n] = (at, a.shape[1])
        at += a.shape[1]
    return where, np.ascontiguousarray(np.concatenate([a for _, a in parts], axis=1))


def _constants():
    f = np.float32
    i = np.arange(128)
    causal = (i[:, None] <= i[None, :]).astype(f)
    ones = np.ones((128, 128), f)
    decay = (causal * (i[:, None] // 64 == i[None, :] // 64) / 16.0).astype(f)
    fold = (i[:, None] % 64 == np.arange(64)[None, :]).astype(f)
    return [("ident", np.eye(128, dtype=f)), ("tri3", np.concatenate([causal, ones, causal], 1)),
            ("before", (i[:, None] < i[None, :]).astype(f)), ("ones", ones), ("fold", fold),
            ("slots", np.broadcast_to(np.arange(1, 65, dtype=f), (128, 64))),
            ("bar", np.broadcast_to(f(-1e-30) * np.tri(4, k=-1, dtype=f).reshape(1, 16), (128, 16))),
            ("decay", decay)]


def layout(i):
    D = {}
    x = i["x"][0]
    D["x"] = np.ascontiguousarray(x)
    D["xT"] = np.ascontiguousarray(x.reshape(256, 8, 128).transpose(2, 1, 0).reshape(128, 2048))
    cst_at, D["cst"] = _table(_constants())
    gw = i["gla_w_in"][0]
    mw = i["mlstm_w_in"][0]
    heads = np.concatenate([np.arange(256) + 256 * h + 1024 * j for h in range(4) for j in range(2)])
    vecs = [("glr", gw[:, 3072:].reshape(8, 128, 16).transpose(1, 0, 2).reshape(128, 128)),
            ("gla_g", _col(i["gla_norm_g"][0])), ("mlstm_g", _col(i["mlstm_norm_g"][0])),
            ("conv_w", np.concatenate([_col(i["mlstm_conv_w"][0, j][heads]) for j in range(4)], 1)),
            ("conv_b", _col(i["mlstm_conv_b"][0][heads])),
            ("ln_g", _col(i["ln_g"])), ("ln_b", _col(i["ln_b"])),
            ("g_mix", _col(i["g_mix_2"])), ("g_mlp", _col(i["g_mlp_2"])), ("b_ada", _col(i["b_ada_2"])),
            ("c", _col(i["c_2"][0])),
            ("router", i["router_w"].reshape(8, 128, 16).transpose(1, 0, 2).reshape(128, 128)),
            ("mbias", np.concatenate([i["mlstm_b_gates"][0], np.zeros(120, np.float32)]).reshape(128, 1)),
            ("mgate", mw[:, 4096:].reshape(8, 128, 8).transpose(1, 0, 2).reshape(128, 64))]
    vec_at, D["vec"] = _table(vecs)
    D["wgu"] = np.concatenate([i["gla_w_gate_up"][0], i["gla_b_gate"]], 0)
    D["lnrow"] = np.concatenate([i["ln_g"].reshape(4, 1024), i["ln_b"].reshape(4, 1024)], 1)
    D["gla_qk"] = _stat(gw[:, 0:1024])
    D["gla_v"], D["gla_r"] = _move(gw[:, 1024:2048]), _move(gw[:, 2048:3072])
    D["gla_o"] = _halves(_move(i["gla_w_out"][0]))
    for n in range(2):
        up = [np.concatenate([_move(i["moe_w1"][n, e]), _move(i["moe_w3"][n, e])]) for e in range(16)]
        down = [_move(i["moe_w2"][n, e]) for e in range(16)]
        seq = [up[0]]
        for e in range(1, 16):
            seq += [up[e], down[e - 1]]
        D[f"moe{n}"] = np.concatenate(seq + [down[15]])
    D["ml_qk"] = _stat(mw[:, heads])
    D["ml_v"], D["ml_gate"] = _move(mw[:, 2048:3072]), _move(mw[:, 3072:4096])
    D["ml_o"] = _halves(_move(i["mlstm_w_out"][0]))
    ada = i["w_ada_2"]
    D["ada"] = np.ascontiguousarray(ada.reshape(2, 8, 128, 3, 2048).transpose(0, 3, 1, 2, 4)).reshape(-1, 2048)
    D["rope"], D["masks"] = _rotation(), _dilated()
    qa, ka, qb, kb = i["q_norm_a_2"], i["k_norm_a_2"], i["q_norm_b_2"], i["k_norm_b_2"]
    gains = []
    for l in range(2):
        row = []
        for n, g in enumerate([qa[l], ka[l], qb[l, 0], kb[l, 0], qb[l, 1], kb[l, 1], qb[l, 2], kb[l, 2]]):
            swap = g.reshape(2, 2, 16)[:, ::-1] if n < 2 else g.reshape(2, 32)[::-1]
            row += [g, swap.reshape(64)]
        gains.append(np.concatenate(row))
    D["gains"] = np.stack(gains)
    perm = np.concatenate([np.arange(64) + 64 * h for h in (0, 4, 1, 5, 2, 6, 3, 7)])
    for l in range(2):
        w = i["w_in_2"][l]
        q, k, v = w[:, 0:512][:, perm], w[:, 512:640], w[:, 640:768]
        g3 = [[w[:, 768 + 768 * g + 256 * j:1024 + 768 * g + 256 * j] for j in range(3)] for g in range(3)]
        cols = [q, k, g3[0][0], v, g3[0][1], g3[0][2], g3[1][0], g3[1][1], g3[2][1], g3[1][2], g3[2][0], g3[2][2]]
        D[f"b2_in{l}"] = _move(np.concatenate(cols, axis=1))
        D[f"b2_gate{l}"] = _stat(w[:, 3072:5120])
        D[f"b2_a{l}"] = _stat(i["w_branch_a_2"][l][perm])
        D[f"b2_b{l}"] = _stat(i["w_branch_b_2"][l])
        D[f"b2_o{l}"] = _halves(_move(i["w_out_2"][l]))
        f1 = _stat(i["w_ff1_2"][l]).reshape(16, 128, 2048)
        f2 = _chunks(i["w_ff2_2"][l].reshape(32, 128, 1024)).reshape(16, 128, 2048)
        seq = [f1[0]]
        for n in range(1, 16):
            seq += [f1[n], f2[n - 1]]
        D[f"b2_ff{l}"] = np.concatenate(seq + [f2[15]])
    order = [("gla_qk", []), ("gla_v", [2, 3]), ("gla_r", [0, 1, 1, 2, 2, 3]), ("gla_o", []), ("moe0", []),
             ("ml_v", [2, 3]), ("ml_qk", [1, 3, 5, 7]), ("ml_gate", [1, 3]), ("ml_o", []), ("moe1", [])]
    for l in range(2):
        order += [(f"b2_in{l}", [] if l else [2, 4]), (f"b2_gate{l}", [] if l else [3, 4, 5, 6]), (f"b2_b{l}", []),
                  (f"b2_a{l}", [] if l else [1]), (f"b2_o{l}", [] if l else [0]),
                  (f"b2_ff{l}", [] if l else [1 + n + 2 * (n // 8) for n in range(24)])]
    return D, cst_at, vec_at, order


def _rotation():
    f = np.float32

    def cs(pos, dim):
        inv = (f(10000.0) ** (-np.arange(0, dim, 2, dtype=f) / f(dim))).astype(f)
        ang = pos.astype(f)[:, None] * inv[None, :]
        return np.cos(ang).astype(f), np.sin(ang).astype(f)

    s = np.arange(256)
    (rc, rs), (cc, c_s), (sc, ss) = cs(s // 64, 32), cs(s % 64, 32), cs(s, 64)
    ax = np.stack([np.concatenate([rc, rc, cc, cc], 1), np.concatenate([-rs, rs, -c_s, c_s], 1)])
    seq = np.stack([np.concatenate([sc, sc], 1), np.concatenate([-ss, ss], 1)])
    t = np.stack([ax, seq]).reshape(2, 2, 2, 128, 64)
    return np.ascontiguousarray(t.transpose(3, 0, 1, 2, 4)).reshape(128, 512)


def _dilated():
    i = np.arange(256)
    d = i[None, :] - i[:, None]
    m = [np.abs(d) <= 64, d % 4 == 0, d % 16 == 0]
    m = np.stack([np.where(x, 0.0, -1e30).astype(np.float32) for x in m]).reshape(3, 2, 128, 256)
    return np.ascontiguousarray(m.transpose(2, 0, 1, 3)).reshape(128, 1536)


def whole(name, c):
    if name == "ml_qk":
        return 2
    return {94: 0}.get(c, (0, 0, 0, 0, 1, 0)[c % 6]) if name.startswith("moe") else 0


def build(nc, D, cst_at, vec_at, order, out):
    aps = {}
    for n, a in D.items():
        aps[n] = nc.dram_tensor(f"in_{n}", a.shape, mybir.dt.from_np(a.dtype), kind="ExternalInput").ap()
    chunks, stops, moe, spare, sent = [], {}, {}, {}, 0
    for n, extra in order:
        count = D[n].shape[0] // 128
        for c in range(count):
            for _ in range(extra.count(c)):
                at = 128 * sent
                chunks.append(("ada", aps["ada"][at:at + 128, :], sent // 24, sent // 8 % 3, sent % 8))
                sent += 1
            chunks.append(("w", aps[n][128 * c:128 * c + 128, :], whole(n, c)))
        if n.startswith("moe"):
            i, at = int(n[3]), len(chunks) - count
            moe[i] = chunks[at:]
            stops[len(chunks)] = i
            spare[i] = [(p, at + c, at + last) for p, c, last in
                        ((3, 3, 3), (1, 4, 95), (2, 5, 95), (4, 6, 95), (5, 7, 76), (0, 8, 95), (6, 11, 95))]
    small = {"cst": (cst_at, D["cst"].shape[1]), "vec": (vec_at, D["vec"].shape[1]), "chunks": chunks, "stops": stops, "moe": moe,
             "spare": spare}
    return two_block_kernel(nc, aps, out, small)


def kernel(**inputs):
    import concourse.bacc as _bacc
    from concourse.bass_utils import run_bass_kernel_spmd as _run

    nc = _bacc.Bacc("TRN2", target_bir_lowering=False, num_devices=1)
    ins = {k: np.asarray(v) for k, v in inputs.items()}
    D, cst_at, vec_at, order = layout(ins)
    out = nc.dram_tensor("out_dram", (256, 1024), mybir.dt.float32, kind="ExternalOutput").ap()
    build(nc, D, cst_at, vec_at, order, out)
    r = _run(nc, [{f"in_{n}": a for n, a in D.items()}], core_ids=[0])
    return r.results[0]["out_dram"].reshape(1, 256, 1024)
```
